# Optimizing a Trainium2 kernel written in Bass

```python
import math
import jax, jax.numpy as jnp
from jax import lax
import numpy as np

D_MODEL = 1024
BATCH = 1
SEQ = 512
DEPTH = 2

CHUNK = 64
EPS = 1e-6
N_A_LAYERS = DEPTH // 2
N_B_LAYERS = DEPTH - N_A_LAYERS

SSM_EXPAND = 2
D_INNER = SSM_EXPAND * D_MODEL
SSM_HEAD_DIM = 64
N_SSM_HEADS = D_INNER // SSM_HEAD_DIM
N_SSM_GROUPS = 8
HEADS_PER_GROUP = N_SSM_HEADS // N_SSM_GROUPS
D_STATE = 128
SSM_CONV = 4
D_CONV_CH = D_INNER + 2 * N_SSM_GROUPS * D_STATE
D_IN_PROJ = D_INNER + D_CONV_CH + N_SSM_HEADS

ATT_HEAD_DIM = 64
N_Q_HEADS = D_MODEL // ATT_HEAD_DIM
N_KV_HEADS = 4
Q_PER_KV = N_Q_HEADS // N_KV_HEADS
Q_DIM = N_Q_HEADS * ATT_HEAD_DIM
KV_DIM = N_KV_HEADS * ATT_HEAD_DIM
WINDOW = 128
WINDOW_CHUNKS = WINDOW // CHUNK

D_FF = 2816
FFN_CONV = 3

kernel_name = "yoco_mamba2_swa_sink_convffn"

def rmsnorm(x, w):
    xf = x.astype(jnp.float32)
    y = xf * lax.rsqrt(jnp.mean(xf * xf, axis=-1, keepdims=True) + EPS)
    return (y * w.astype(jnp.float32)).astype(x.dtype)

def causal_dwconv(u, w, b):
    k = w.shape[0]
    out = lax.conv_general_dilated(
        u, w[:, None, :].astype(u.dtype), window_strides=(1,), padding=[(k - 1, 0)],
        dimension_numbers=('NWC', 'WIO', 'NWC'), feature_group_count=u.shape[-1])
    return out + b.astype(u.dtype)

def ssd_scan(x, dt, a, bm, cm):
    b, L = x.shape[:2]
    nc = L // CHUNK
    G, J, P, N = N_SSM_GROUPS, HEADS_PER_GROUP, SSM_HEAD_DIM, D_STATE
    x = x.astype(jnp.float32).reshape(b, nc, CHUNK, G, J, P)
    dt = dt.reshape(b, nc, CHUNK, G, J)
    bm = bm.astype(jnp.float32).reshape(b, nc, CHUNK, G, N)
    cm = cm.astype(jnp.float32).reshape(b, nc, CHUNK, G, N)
    da_cs = jnp.cumsum(dt * a.reshape(G, J), axis=2)
    xdt = x * dt[..., None]
    seg = da_cs[:, :, :, None] - da_cs[:, :, None, :]
    tri = jnp.tril(jnp.ones((CHUNK, CHUNK), dtype=bool))[None, None, :, :, None, None]
    lmat = jnp.exp(jnp.where(tri, seg, -jnp.inf))
    cb = jnp.einsum('bclgn,bcsgn->bclsg', cm, bm)
    y_diag = jnp.einsum('bclsg,bclsgj,bcsgjp->bclgjp', cb, lmat, xdt)
    decay_to_end = jnp.exp(da_cs[:, :, -1:] - da_cs)
    states = jnp.einsum('bclgn,bclgj,bclgjp->bcgjpn', bm, decay_to_end, xdt)
    chunk_decay = jnp.exp(da_cs[:, :, -1])

    def step(h, inp):
        st, dec = inp
        return dec[..., None, None] * h + st, h

    h0 = jnp.zeros((b, G, J, P, N), jnp.float32)
    _, states_in = lax.scan(step, h0, (jnp.moveaxis(states, 1, 0), jnp.moveaxis(chunk_decay, 1, 0)))
    states_in = jnp.moveaxis(states_in, 0, 1)
    y_off = jnp.einsum('bclgn,bclgj,bcgjpn->bclgjp', cm, jnp.exp(da_cs), states_in)
    return (y_diag + y_off).reshape(b, L, N_SSM_HEADS, P)

def mamba2_mixer(h, in_proj, conv_w, conv_b, dt_bias, a_log, d_skip, gate_w, out_proj):
    b, L, _ = h.shape
    zxbcdt = h @ in_proj
    z, xbc, dt_raw = jnp.split(zxbcdt, [D_INNER, D_INNER + D_CONV_CH], axis=-1)
    xbc = jax.nn.silu(causal_dwconv(xbc, conv_w, conv_b))
    xs, bm, cm = jnp.split(xbc, [D_INNER, D_INNER + N_SSM_GROUPS * D_STATE], axis=-1)
    xs = xs.reshape(b, L, N_SSM_HEADS, SSM_HEAD_DIM)
    bm = bm.reshape(b, L, N_SSM_GROUPS, D_STATE)
    cm = cm.reshape(b, L, N_SSM_GROUPS, D_STATE)
    dt = jax.nn.softplus(dt_raw.astype(jnp.float32) + dt_bias.astype(jnp.float32))
    a = -jnp.exp(a_log.astype(jnp.float32))
    y = ssd_scan(xs, dt, a, bm, cm)
    y = y + xs.astype(jnp.float32) * d_skip.astype(jnp.float32)[:, None]
    yg = (y.reshape(b, L, D_INNER) * jax.nn.silu(z.astype(jnp.float32))).reshape(b, L, N_SSM_GROUPS, -1)
    yg = yg * lax.rsqrt(jnp.mean(yg * yg, axis=-1, keepdims=True) + EPS)
    y = yg.reshape(b, L, D_INNER) * gate_w.astype(jnp.float32)
    return y.astype(h.dtype) @ out_proj

def chunk_band(t):
    nc = t.shape[1]
    parts = []
    for s in range(WINDOW_CHUNKS - 1, 0, -1):
        parts.append(jnp.pad(t[:, :nc - s], ((0, 0), (s, 0), (0, 0), (0, 0), (0, 0))))
    parts.append(t)
    return jnp.concatenate(parts, axis=2)

def swa_sink_attention(h, w_q, b_q, sinks, w_o, b_o, k, v):
    b, L, _ = h.shape
    nc = L // CHUNK
    q = (h @ w_q + b_q).reshape(b, nc, CHUNK, N_KV_HEADS, Q_PER_KV, ATT_HEAD_DIM)
    kb = chunk_band(k.reshape(b, nc, CHUNK, N_KV_HEADS, ATT_HEAD_DIM))
    vb = chunk_band(v.reshape(b, nc, CHUNK, N_KV_HEADS, ATT_HEAD_DIM))
    s = jnp.einsum('bcqhgd,bckhd->bchgqk', q, kb).astype(jnp.float32) * (ATT_HEAD_DIM ** -0.5)
    key_chunk_off = (WINDOW_CHUNKS - 1) - jnp.arange(WINDOW_CHUNKS * CHUNK) // CHUNK
    valid = jnp.arange(nc)[:, None] >= key_chunk_off[None, :]
    s = jnp.where(valid[None, :, None, None, None, :], s, -jnp.inf)
    sink = jnp.broadcast_to(sinks.astype(jnp.float32).reshape(1, 1, N_KV_HEADS, Q_PER_KV, 1, 1),
                            s.shape[:-1] + (1,))
    p = jax.nn.softmax(jnp.concatenate([s, sink], axis=-1), axis=-1)[..., :-1]
    o = jnp.einsum('bchgqk,bckhd->bcqhgd', p.astype(vb.dtype), vb).reshape(b, L, Q_DIM)
    return o @ w_o + b_o

def conv_ffn(h, up, conv_w, conv_b, down):
    u = causal_dwconv(h @ up, conv_w, conv_b)
    gate, val = jnp.split(u, 2, axis=-1)
    return (jax.nn.silu(gate) * val) @ down

def setup_inputs(seed: int = 0) -> dict:
    key = jax.random.key(seed)
    ks = iter(jax.random.split(key, 40))

    def nrm(shape, scale):
        return jax.random.normal(next(ks), shape, jnp.float32) * scale

    def gain(shape):
        return 1.0 + nrm(shape, 0.05)

    x = nrm((BATCH, SEQ, D_MODEL), 1.0)
    a_norm_pre = gain((N_A_LAYERS, D_MODEL))
    a_in_proj = nrm((N_A_LAYERS, D_MODEL, D_IN_PROJ), D_MODEL ** -0.5)
    a_conv_w = nrm((N_A_LAYERS, SSM_CONV, D_CONV_CH), SSM_CONV ** -0.5)
    a_conv_b = nrm((N_A_LAYERS, D_CONV_CH), 0.02)
    dt0 = jnp.exp(jax.random.uniform(next(ks), (N_A_LAYERS, N_SSM_HEADS), jnp.float32,
                                     minval=math.log(1e-3), maxval=math.log(1e-1)))
    a_dt_bias = dt0 + jnp.log(-jnp.expm1(-dt0))
    a_a_log = jnp.log(jax.random.uniform(next(ks), (N_A_LAYERS, N_SSM_HEADS), jnp.float32,
                                         minval=1.0, maxval=16.0))
    a_d_skip = gain((N_A_LAYERS, N_SSM_HEADS))
    a_gate_norm = gain((N_A_LAYERS, D_INNER))
    a_out_proj = nrm((N_A_LAYERS, D_INNER, D_MODEL), D_INNER ** -0.5)
    a_norm_post = gain((N_A_LAYERS, D_MODEL))
    kv_norm = gain((D_MODEL,))
    w_kv = nrm((D_MODEL, 2 * KV_DIM), D_MODEL ** -0.5)
    b_kv = nrm((2 * KV_DIM,), 0.02)
    b_norm_pre = gain((N_B_LAYERS, D_MODEL))
    w_q = nrm((N_B_LAYERS, D_MODEL, Q_DIM), D_MODEL ** -0.5)
    b_q = nrm((N_B_LAYERS, Q_DIM), 0.02)
    sinks = nrm((N_B_LAYERS, N_Q_HEADS), 0.5)
    w_o = nrm((N_B_LAYERS, Q_DIM, D_MODEL), Q_DIM ** -0.5)
    b_o = nrm((N_B_LAYERS, D_MODEL), 0.02)
    b_norm_post = gain((N_B_LAYERS, D_MODEL))
    f_norm_pre = gain((DEPTH, D_MODEL))
    f_up = nrm((DEPTH, D_MODEL, 2 * D_FF), D_MODEL ** -0.5)
    f_conv_w = nrm((DEPTH, FFN_CONV, 2 * D_FF), FFN_CONV ** -0.5)
    f_conv_b = nrm((DEPTH, 2 * D_FF), 0.02)
    f_down = nrm((DEPTH, D_FF, D_MODEL), D_FF ** -0.5)
    f_norm_post = gain((DEPTH, D_MODEL))
    return {
        "x": x,
        "a_norm_pre": a_norm_pre, "a_in_proj": a_in_proj, "a_conv_w": a_conv_w, "a_conv_b": a_conv_b,
        "a_dt_bias": a_dt_bias, "a_a_log": a_a_log, "a_d_skip": a_d_skip, "a_gate_norm": a_gate_norm,
        "a_out_proj": a_out_proj, "a_norm_post": a_norm_post,
        "kv_norm": kv_norm, "w_kv": w_kv, "b_kv": b_kv,
        "b_norm_pre": b_norm_pre, "w_q": w_q, "b_q": b_q, "sinks": sinks, "w_o": w_o, "b_o": b_o,
        "b_norm_post": b_norm_post,
        "f_norm_pre": f_norm_pre, "f_up": f_up, "f_conv_w": f_conv_w, "f_conv_b": f_conv_b,
        "f_down": f_down, "f_norm_post": f_norm_post,
    }

def reference(x, a_norm_pre, a_in_proj, a_conv_w, a_conv_b, a_dt_bias, a_a_log, a_d_skip, a_gate_norm,
              a_out_proj, a_norm_post, kv_norm, w_kv, b_kv, b_norm_pre, w_q, b_q, sinks, w_o, b_o,
              b_norm_post, f_norm_pre, f_up, f_conv_w, f_conv_b, f_down, f_norm_post):
    b, L, _ = x.shape
    h = x
    k = v = None
    for i in range(DEPTH):
        if i < N_A_LAYERS:
            mix = mamba2_mixer(rmsnorm(h, a_norm_pre[i]), a_in_proj[i], a_conv_w[i], a_conv_b[i],
                               a_dt_bias[i], a_a_log[i], a_d_skip[i], a_gate_norm[i], a_out_proj[i])
            h = h + rmsnorm(mix, a_norm_post[i])
        else:
            j = i - N_A_LAYERS
            if j == 0:
                kv = rmsnorm(h, kv_norm) @ w_kv + b_kv
                k, v = jnp.split(kv, 2, axis=-1)
                k = k.reshape(b, L, N_KV_HEADS, ATT_HEAD_DIM)
                v = v.reshape(b, L, N_KV_HEADS, ATT_HEAD_DIM)
            mix = swa_sink_attention(rmsnorm(h, b_norm_pre[j]), w_q[j], b_q[j], sinks[j], w_o[j], b_o[j], k, v)
            h = h + rmsnorm(mix, b_norm_post[j])
        ffn = conv_ffn(rmsnorm(h, f_norm_pre[i]), f_up[i], f_conv_w[i], f_conv_b[i], f_down[i])
        h = h + rmsnorm(ffn, f_norm_post[i])
    return h


_drawn_inputs = setup_inputs


def setup_inputs(seed=0):
    import zlib

    import numpy as np

    out = dict(_drawn_inputs(seed))
    spreads = {}
    factors = {'b_norm_pre': 2.816, 'b_q': 7.056, 'sinks': 8.0}
    for name, (base, spread) in spreads.items():
        noise = np.random.default_rng([zlib.crc32(name.encode()), seed]).standard_normal(out[name].shape)
        drawn = base * np.exp(spread * noise) if base else spread * noise
        out[name] = __import__('jax').numpy.asarray(drawn.astype(out[name].dtype))
    for name, factor in factors.items():
        out[name] = (out[name] * factor).astype(out[name].dtype)
    return out
```

```python
from contextlib import ExitStack, contextmanager

import numpy as np
import concourse.bass as bass
from concourse import mybir
from concourse.alu_op_type import AluOpType as ALU

F32, F32R = mybir.dt.float32, mybir.dt.float32r
ACT = mybir.ActivationFunctionType
AX_X = mybir.AxisListType.X
ds = bass.ds

P = 128
DM, SEQ, EPS = 1024, 512, 1e-6
KT = DM // P
DI, DS, NG, NH = 2048, 128, 8, 32
HG = NH // NG
SC = 128
NC = SEQ // SC
GROUP_SLABS = 6
DFF = 2816
FT = DFF // P
CH = 64
NCH = SEQ // CH
RING = 3
N_IN = NG * GROUP_SLABS
OUT0 = N_IN
OUT_K = DI // P
UP = [OUT0 + OUT_K, 0]
DOWN = [UP[0] + 2 * FT, 0]
KV0 = DOWN[0] + FT
Q0 = KV0 + 4
O0 = Q0 + KT
UP[1] = O0 + KT
DOWN[1] = UP[1] + 2 * FT
N_SLABS = DOWN[1] + FT
_cols, _n = {}, 0
for _name, _count in (("a_pre", KT), ("a_conv", 4 * 32), ("a_convb", 32), ("a_gate", OUT_K), ("a_post", KT),
                      ("kvn", KT), ("b_kv", 4), ("b_pre", KT), ("b_q", KT), ("b_o", KT), ("b_post", KT),
                      ("f_pre", 2 * KT), ("f_conv", 2 * 3 * 2 * FT), ("f_convb", 2 * 2 * FT), ("f_post", 2 * KT)):
    _cols[_name] = _n
    _n += _count
COL, N_COLS = _cols, _n


class Core:
    pass


class Steps:

    def __init__(self, eng, sem):
        self.eng, self.sem, self.base, self.n = eng, sem, 0, 0

    def done(self, ins):
        ins.then_inc(self.sem, 1)
        self.n += 1

    def wait(self):
        self.eng.wait_ge(self.sem, self.base + self.n)

    def link(self, ins):
        self.done(ins)
        self.wait()


@contextmanager
def looped(eng, lo, hi, *tallies):
    before = [(s, s.base + s.n, per) for s, per in tallies]
    with eng.Fori(lo, hi) as i:
        for s, b, per in before:
            s.base, s.n = b + (i - lo) * per, 0
        yield i
        for s, b, per in before:
            assert s.n == per, (s.n, per)
    for s, b, per in before:
        s.base, s.n = b + (hi - lo) * per, 0


def bcast(ap, shape):
    return ap.to_broadcast(shape)


def sp_program(k, sp):
    sp.dma_start(k.par[:, :], k.d_par).then_inc(k.par_loaded, 16)
    for c in range(KT):
        sp.dma_start(k.h[:, c, :], k.d_x[:, c, :]).then_inc(k.x_loaded[c], 16)
    for s in range(RING):
        sp.dma_start(k.raw[s][:, :], k.d_slabs[s * P:(s + 1) * P, :]).then_inc(k.raw_loaded[s], 16)
        if s == 0:
            sp.dma_start(k.wdt[:, :], k.d_wdt).then_inc(k.small_loaded, 16)
            sp.dma_start(k.hpar[:, :], k.d_hpar).then_inc(k.small_loaded, 16)
            for half in range(2):
                rows = slice(64 * half, 64 * half + 64)
                sp.dma_start(k.dskip[rows, :], bcast(k.d_dskip[half:half + 1, :], [64, 16])).then_inc(k.small_loaded, 16)
                sp.dma_start(k.nsink[rows, :], bcast(k.d_sinks[half:half + 1, :], [64, 8])).then_inc(k.small_loaded, 16)
    with sp.Fori(1, N_SLABS // RING) as r:
        for s in range(RING):
            row = sp.snap(r * (RING * P) + s * P)
            sp.wait_ge(k.lo_done, r * RING + (s + 1 - RING))
            sp.dma_start(k.raw[s][:, :], k.d_slabs[ds(row, P), :]).then_inc(k.raw_loaded[s], 16)
    for c in range(KT):
        sp.wait_ge(k.h_done, 3 * KT + c + 1)
        sp.dma_start(k.d_out[:, c, :], k.h[:, c, :]).then_inc(k.stored, 16)
    sp.wait_ge(k.stored, 16 * KT)


def pool_program(k, pool):
    pool.memset(k.ones[:, :], 1.0).then_inc(k.ones_set, 1)
    pool.wait_ge(k.ones_set, 1)
    pool.affine_select(out=k.ident[:, :], in_=k.ones[:, :], compare_op=ALU.is_equal, fill=0.0,
                       base=0, pattern=[[1, P]], channel_multiplier=-1).then_inc(k.consts_ready, 1)
    pool.affine_select(out=k.tri[:, :], in_=k.ones[:, :], compare_op=ALU.is_ge, fill=0.0,
                       base=0, pattern=[[1, P]], channel_multiplier=-1).then_inc(k.consts_ready, 1)
    with pool.Fori(0, N_SLABS // RING) as r:
        for s in range(RING):
            pool.wait_ge(k.hi_done, r * RING + (s + 1))
            pool.tensor_tensor(k.wlo[s][:, :], k.raw[s][:, :], k.whi[s][:, :], ALU.subtract).then_inc(k.lo_done, 1)


def pe_program(k, pe):
    ps = k.ps

    def slab_a(n, bank, hi, lo, m0=True):
        s = n % RING if isinstance(n, int) else n[1]
        for c in range(KT):
            wh, wl = k.whi[s][:, c * P:(c + 1) * P], k.wlo[s][:, c * P:(c + 1) * P]
            pe.matmul(ps[:, bank, :], wh, hi[:, c, :], start=(c == 0), stop=False)
            pe.matmul(ps[:, bank, :], wh, lo[:, c, :], start=False, stop=False)
            last = pe.matmul(ps[:, bank, :], wl, hi[:, c, :], start=False, stop=(c == KT - 1))
        last.then_inc(k.slab_used, 1)

    def first_slabs_a(n, banks, hi, lo, parts_ready, base):
        for c in range(KT):
            pe.wait_ge(parts_ready, base + c + 1)
            for j, bank in enumerate(banks):
                s = (n + j) % RING
                if c == 0:
                    pe.wait_ge(k.lo_done, n + j + 1)
                wh, wl = k.whi[s][:, c * P:(c + 1) * P], k.wlo[s][:, c * P:(c + 1) * P]
                pe.matmul(ps[:, bank, :], wh, hi[:, c, :], start=(c == 0), stop=False)
                pe.matmul(ps[:, bank, :], wh, lo[:, c, :], start=False, stop=False)
                last = pe.matmul(ps[:, bank, :], wl, hi[:, c, :], start=False, stop=(c == KT - 1))
                if c == KT - 1:
                    last.then_inc(k.slab_used, 1)

    def three(m, s, hi_k, lo_k, start, stop):
        wh, wl = k.whi[s][:, m * P:(m + 1) * P], k.wlo[s][:, m * P:(m + 1) * P]
        pe.matmul(ps[:, m, :], wh, hi_k, start=start, stop=False)
        pe.matmul(ps[:, m, :], wh, lo_k, start=False, stop=False)
        return pe.matmul(ps[:, m, :], wl, hi_k, start=False, stop=stop)

    def slab_b(s, hi_k, lo_k, start=False):
        for m in range(KT):
            last = three(m, s, hi_k, lo_k, start, False)
        last.then_inc(k.slab_used, 1)

    def tail_b(slots, parts):
        for m in range(KT):
            for j, (s, (hi_k, lo_k)) in enumerate(zip(slots, parts)):
                last = three(m, s, hi_k, lo_k, False, j == 1)
                if m == KT - 1 and j == 0:
                    last.then_inc(k.slab_used, 1)
            last.then_inc(k.mix_ready if m < KT - 1 else k.slab_used, 1)

    def column_sums(norm):
        pe.wait_ge(k.sq_added, KT * (norm + 1))
        pe.matmul(ps[:, 6, :], k.ones[:, :], k.acc[:, :], start=True, stop=True).then_inc(k.sums_ready, 1)

    def ssd_1(g, p):
        pe.wait_ge(k.xbc_done, g * 4 + 4)
        if not isinstance(g, int) or g > 0:
            pe.wait_ge(k.gate_rstd_done, g)
            pe.wait_ge(k.y_done, g * 2)
        for c in range(NC):
            t = slice(c * SC, (c + 1) * SC)
            last = pe.matmul(ps[:, 3, t], k.bt[p][:, t], k.ct[p][:, t], start=True, stop=True)
        last.then_inc(k.cb_ready, 1)
        for c in range(NC):
            t = slice(c * SC, (c + 1) * SC)
            last = pe.transpose(ps[:, 7, t], k.bt[p][:, t], k.ident[:, :])
        last.then_inc(k.btok_ready, 1)
        for j in range(2):
            for c in range(NC):
                t = slice(c * SC, (c + 1) * SC)
                last = pe.transpose(ps[:, 5 + j, t], k.xt[p][:, j, t], k.ident[:, :])
            last.then_inc(k.xtok_ready, 1)

    def ssd_2(g, p):
        pe.wait_ge(k.btok_done, g + 1)
        pe.wait_ge(k.xtok_done, g * 4 + 4)
        pe.wait_ge(k.cbm_done, g + 1)
        for c in range(NC - 1):
            out = ps[:, 4, c * 256:(c + 1) * 256] if c < 2 else ps[:, 3, 0:256]
            last = pe.matmul(out, k.btok[:, c, :], k.xdd[:, c, :], start=True, stop=True)
        last.then_inc(k.state_ready, 1)

    def ssd_3(g, p):
        for hh in range(HG):
            if hh == 0:
                pe.wait_ge(k.m_done, g * 4 + 4)
            j, half = hh // 2, hh % 2
            for c in range(NC):
                t = slice(c * SC, (c + 1) * SC)
                last = pe.matmul(ps[64 * half:64 * half + 64, 5 + j, t], k.xdt[:, c, hh * 64:hh * 64 + 64],
                                 k.csb[:, hh, t], start=True, stop=True)
        last.then_inc(k.ydiag_ready, 1)

    def ssd_4(g, p):
        pe.wait_ge(k.state_done, g + 1)
        for j, bank in enumerate((7, 4)):
            for c in range(1, NC):
                t = slice(c * SC, (c + 1) * SC)
                last = pe.matmul(ps[:, bank, t], k.hst[:, c - 1, j * P:(j + 1) * P], k.ct[p][:, t],
                                 start=True, stop=True)
        last.then_inc(k.yoff_ready, 1)

    def ssd_5(g):
        pe.wait_ge(k.gate_acc_done, g + 1)
        pe.matmul(ps[:, 3, :], k.ones[:, :], k.gacc[:, :], start=True, stop=True).then_inc(k.gate_sums_ready, 1)

    def in_proj_group(G, p, first_done=False):
        g, q = G - 1, 1 - p
        has_ssd = not (isinstance(G, int) and G == 0)
        for j in range(GROUP_SLABS):
            n = G * GROUP_SLABS + j
            if not (first_done and j < RING):
                pe.wait_ge(k.lo_done, n + 1)
                if j == 0:
                    pe.wait_ge(k.conv_done, G * 4)
                elif j < 3:
                    pe.wait_ge(k.z_done, G * 2 + (j - 2))
                else:
                    pe.wait_ge(k.conv_done, G * 4 + (j - 2))
                slab_a((n, j % RING), j % RING, k.hs_hi, k.hs_lo)
            if has_ssd:
                if j == 0 and not (isinstance(G, int) and G == 1):
                    ssd_5(g - 1)
                if j == 1:
                    ssd_1(g, q)
                if j == 2:
                    ssd_2(g, q)
                if j == 3:
                    ssd_3(g, q)
                if j == 4:
                    ssd_4(g, q)

    pe.wait_ge(k.ones_set, 1)
    pe.wait_ge(k.consts_ready, 2)
    column_sums(0)
    first_slabs_a(0, (0, 1, 2), k.hs_hi, k.hs_lo, k.lo_part_done, 0)
    pe.wait_ge(k.small_loaded, 16 * 6)
    for c in range(KT):
        last = pe.matmul(ps[0:NH, 3, :], k.wdt[:, c * NH:(c + 1) * NH], k.hn[:, c, :], start=(c == 0), stop=(c == KT - 1))
    last.then_inc(k.dt_ready, 1)
    in_proj_group(0, 0, first_done=True)
    pe.wait_ge(k.dtw_done, 1)
    for c in range(NC):
        for i, src in enumerate((k.dt_, k.ncs, k.dtw)):
            last = pe.transpose(ps[:, 4, c * 96 + i * NH:c * 96 + (i + 1) * NH], src[:, c * SC:(c + 1) * SC], k.ident[0:NH, 0:NH])
    last.then_inc(k.tok_ready, 1)
    pe.wait_ge(k.tok_done, 1)
    in_proj_group(1, 1)
    with pe.Fori(1, NG // 2) as i:
        in_proj_group(i * 2, 0)
        in_proj_group(i * 2 + 1, 1)
    g, q = NG - 1, (NG - 1) % 2
    ssd_5(g - 1)
    ssd_1(g, q)
    ssd_2(g, q)
    ssd_3(g, q)
    ssd_4(g, q)
    ssd_5(g)

    pe.wait_ge(k.gate_rstd_done, NG)
    pe.wait_ge(k.y_done, 2 * NG)
    pe.wait_ge(k.z_done, 2 * NG)
    pe.wait_ge(k.conv_done, 4 * NG)

    def out_slab(kk, s, start=False):
        pe.wait_ge(k.lo_done, OUT0 + kk + 1)
        pe.wait_ge(k.yn_done, kk + 1)
        slab_b(s, k.yn_hi[s][:, :], k.yn_lo[s][:, :], start)

    out_slab(0, OUT0 % RING, True)
    out_slab(1, (OUT0 + 1) % RING)
    with pe.Fori(0, 4) as i:
        for j in range(3):
            out_slab(i * 3 + (2 + j), (OUT0 + 2 + j) % RING)
    pe.wait_ge(k.lo_done, OUT0 + OUT_K)
    pe.wait_ge(k.yn_done, OUT_K)
    sl = [(OUT0 + OUT_K - 2 + j) % RING for j in range(2)]
    tail_b(sl, [(k.yn_hi[s][:, :], k.yn_lo[s][:, :]) for s in sl])

    def boundary(t, hi, lo, n):
        pe.wait_ge(k.mix_read, KT * (t + 1))
        column_sums(1 + 2 * t)
        if n is None:
            return
        first_slabs_a(n, [(n + j) % 6 for j in range(RING)], hi, lo, k.lo_part_done, k.lo_base[t])
        pe.wait_ge(k.rstd_done, 2 + 2 * t)
        column_sums(2 + 2 * t)

    def ffn(l):
        act_hi, act_lo = k.f_hi, k.f_lo
        u0 = UP[l]

        def up_slab(i):
            dyn = not isinstance(i, tuple)
            place, stat = (i, i) if dyn else i
            pe.wait_ge(k.lo_done, place + (u0 + 1))
            pe.wait_ge(k.u_done, place + (l * 2 * FT - 5))
            slab_a((0, (u0 + stat) % RING), (u0 + stat) % 6, k.hs_hi, k.hs_lo)

        for i in range(RING, 8):
            pe.wait_ge(k.lo_done, u0 + i + 1)
            if l * 2 * FT + i - 5 > 0 and i >= 6:
                pe.wait_ge(k.u_done, l * 2 * FT + i - 5)
            slab_a((0, (u0 + i) % RING), (u0 + i) % 6, k.hs_hi, k.hs_lo)
        with pe.Fori(0, 6) as r:
            for j in range(6):
                up_slab((r * 6 + (8 + j), 8 + j))
        d0 = DOWN[l]
        pe.wait_ge(k.u_done, (l + 1) * 2 * FT)
        pe.wait_ge(k.rstd_done, 3 + 4 * l)

        def down_slab(kk, stat, start=False):
            pe.wait_ge(k.lo_done, kk + (d0 + 1))
            pe.wait_ge(k.f_done, kk + (l * FT + 1))
            hi_k = act_hi[:, kk, :]
            lo_k = act_lo[:, kk, :]
            slab_b((d0 + stat) % RING, hi_k, lo_k, start)

        down_slab(0, 0, True)
        down_slab(1, 1)
        with pe.Fori(0, 6) as r:
            for j in range(3):
                down_slab(r * 3 + (2 + j), 2 + j)
        pe.wait_ge(k.lo_done, d0 + FT)
        pe.wait_ge(k.f_done, (l + 1) * FT)
        tail_b([(d0 + FT - 2 + j) % RING for j in range(2)],
               [(act_hi[:, FT - 2 + j, :], act_lo[:, FT - 2 + j, :]) for j in range(2)])

    boundary(0, k.hs_hi, k.hs_lo, UP[0])
    ffn(0)
    boundary(1, k.hk_hi, k.hk_lo, KV0)

    pe.wait_ge(k.lo_done, KV0 + 4)
    slab_a(KV0 + 3, (KV0 + 3) % 6, k.hk_hi, k.hk_lo)
    for i in range(KT):
        n = Q0 + i
        pe.wait_ge(k.lo_done, n + 1)
        if i == 0:
            pe.wait_ge(k.lo_part_done, k.lo_q_base + KT)
        if n - KV0 >= 6:
            pe.wait_ge(k.qkv_read, n - KV0 - 5)
        slab_a(n, n % 6, k.hs_hi, k.hs_lo)
        if i >= 2 and i < 6:
            b = i - 2
            if b == 0:
                pe.wait_ge(k.kqv_done, 4)
            else:
                pe.wait_ge(k.vtok_done, b)
            for w in range(2):
                c = 2 * b + w
                for kt in range(2):
                    last = pe.transpose(ps[:, 7, (w * 2 + kt) * P:(w * 2 + kt + 1) * P],
                                        k.vp[:, kt, c * CH:c * CH + P], k.ident[:, :])
            last.then_inc(k.vtok_ready, 1)
    pe.wait_ge(k.kqv_done, 12)
    pe.wait_ge(k.qkv_read, 12)

    def scores(a):
        kt, c = a // NCH, a % NCH
        if a >= 2:
            pe.wait_ge(k.exp_done, a - 1)
        for u in range(4):
            r = slice(64 * (u // 2), 64 * (u // 2) + 64)
            last = pe.matmul(ps[:, 2 * (a % 2) + u // 2, (u % 2) * P:(u % 2 + 1) * P], k.qt[r, kt, c, (u % 2) * P:(u % 2 + 1) * P],
                             k.kp[r, kt, c * CH:c * CH + P], start=True, stop=True)
        last.then_inc(k.scores_ready, 1)

    scores(0)
    scores(1)
    for a in range(2 * NCH):
        kt, c = a // NCH, a % NCH
        pe.wait_ge(k.probs_done, a + 1)
        if a >= 2:
            pe.wait_ge(k.pt_done, a - 1)
        for u in range(4):
            last = pe.transpose(ps[:, 4 + a % 2, u * P:(u + 1) * P], k.pr[a % 2][:, u, :], k.ident[:, :])
        last.then_inc(k.pt_ready, 1)
        if a + 2 < 2 * NCH:
            scores(a + 2)
        pe.wait_ge(k.pt_done, a + 1)
        if a == 0:
            pe.wait_ge(k.vtok_done, 4)
        if a >= 2:
            pe.wait_ge(k.o_done, a - 1)
        for half in range(2):
            last = pe.matmul(ps[64 * half:64 * half + 64, 6 + a % 2, 0:256],
                             k.vtok[:, c, kt, 64 * half:64 * half + 64],
                             k.pts[a % 2][:, 2 * half * P:(2 * half + 2) * P], start=True, stop=True)
        last.then_inc(k.o_ready, 1)
    pe.wait_ge(k.o_done, 2 * NCH)
    for kk in range(KT - 2):
        pe.wait_ge(k.lo_done, O0 + kk + 1)
        slab_b((O0 + kk) % RING, k.o_hi[:, kk, :], k.o_lo[:, kk, :], kk == 0)
    pe.wait_ge(k.lo_done, O0 + KT)
    tail_b([(O0 + KT - 2 + j) % RING for j in range(2)],
           [(k.o_hi[:, KT - 2 + j, :], k.o_lo[:, KT - 2 + j, :]) for j in range(2)])
    boundary(2, k.hs_hi, k.hs_lo, UP[1])
    ffn(1)
    boundary(3, None, None, None)


def act_program(k, act):
    ps, par = k.ps, k.par

    def col(name, i):
        if isinstance(i, int):
            return par[:, COL[name] + i:COL[name] + i + 1]
        return par[:, ds(i + COL[name], 1)]

    def hi(n, s):
        if not isinstance(n, int) or n >= RING:
            act.wait_ge(k.slab_used, n - (RING - 1))
        lap = (n // RING + 1) if isinstance(n, int) else None
        act.wait_ge(k.raw_loaded[s], 16 * lap)
        act.activation(k.whi[s][:, :], k.raw[s][:, :], ACT.Copy).then_inc(k.hi_done, 1)

    def hi_loop(n, s, lap):
        act.wait_ge(k.slab_used, n - (RING - 1))
        act.wait_ge(k.raw_loaded[s], lap * 16)
        act.activation(k.whi[s][:, :], k.raw[s][:, :], ACT.Copy).then_inc(k.hi_done, 1)

    squares = [0]

    def square(src, bias=None):
        q = squares[0]
        if q >= 2:
            act.wait_ge(k.sq_added, q - 1)
        kw = {} if bias is None else {"bias": bias}
        act.activation(k.sq[q % 2][:, :], src, ACT.Square, **kw).then_inc(k.sq_done, 1)
        squares[0] += 1

    lns = Steps(act, k.ln_done)

    def rstd(norm, out):
        act.wait_ge(k.sums_ready, norm + 1)
        if norm:
            act.wait_ge(k.rstd_done, norm)
        lns.link(act.activation(k.lnv[:, :], ps[:, 6, :], ACT.Ln, bias=k.eps[:, :], scale=1.0 / DM))
        act.activation(out, k.lnv[:, :], ACT.Exp, scale=-0.5).then_inc(k.rstd_done, 1)

    act.wait_ge(k.eps_set, 1)
    for c in range(KT):
        act.wait_ge(k.x_loaded[c], 16)
        square(k.h[:, c, :])
    for s in range(RING):
        hi(s, s)
    rstd(0, k.rpre[:, :])
    for c in range(KT):
        act.wait_ge(k.hn_done, c + 1)
        act.activation(k.hs_hi[:, c, :], k.hn[:, c, :], ACT.Copy).then_inc(k.hi_part_done, 1)

    own = Steps(act, k.act_own)

    def dt_steps():
        act.wait_ge(k.small_loaded, 16 * 6)
        act.wait_ge(k.dt_ready, 1)
        own.link(act.activation(k.dtx[:, :], ps[0:NH, 3, :], ACT.Identity, bias=k.hpar[:, 0:1]))
        own.link(act.activation(k.dta[:, :], k.dtx[:, :], ACT.Abs))
        act.activation(k.dte[:, :], k.dta[:, :], ACT.Exp, scale=-1.0).then_inc(k.dt_exp, 1)
        act.activation(k.aneg[:, :], k.hpar[:, 1:2], ACT.Exp).then_inc(k.dt_exp, 1)
        act.wait_ge(k.dt_u, 1)
        own.link(act.activation(k.dtl[:, :], k.dtu[:, :], ACT.Ln))
        act.activation(k.dtr[:, :], k.dtl[:, :], ACT.Exp, scale=-1.0).then_inc(k.dt_exp, 1)
        act.wait_ge(k.cs_done, 1)
        for c in range(NC):
            t = slice(c * SC, (c + 1) * SC)
            act.activation(k.dtw[:, t], k.cs[:, t], ACT.Exp, scale=-1.0, bias=k.cs[:, (c + 1) * SC - 1:(c + 1) * SC]).then_inc(k.dt_exp, 1)
        act.dma_start(k.d_cs, k.cs[:, :]).then_inc(k.cs_stored, 16)
        act.wait_ge(k.cs_stored, 16)
        load_cs(0)

    def load_cs(g):
        rows = k.d_cs[ds(g * HG, HG), :] if not isinstance(g, int) else k.d_cs[g * HG:(g + 1) * HG, :]
        act.dma_start(k.csb[:, :, :], bcast(rows.rearrange("(o h) t -> o h t", o=1), [P, HG, SEQ])).then_inc(k.cs_loaded, 16)

    def in_group(G, p):
        static = isinstance(G, int)
        g, q = G - 1, 1 - p
        ssd = not (static and G == 0)
        base = G * GROUP_SLABS

        def step(j):
            s = j % RING
            if static:
                hi(base + j + RING, s)
            else:
                hi_loop(base + (j + RING), s, G * 2 + (j // 3 + 2))

        def tap0(i):
            tile = (G + 16, G + 24, G * 2, G * 2 + 1)[i]
            act.wait_ge(k.xbc_done, G * 4 + (i - 1))
            act.activation(k.cacc[i % 2][:, :], ps[:, i % RING, :], ACT.Identity, bias=col("a_convb", tile),
                           scale=col("a_conv", 3 * 32 + tile)).then_inc(k.tap0_done, 1)

        def conv_silu(i):
            dst = (k.bt[p][:, :], k.ct[p][:, :], k.xt[p][:, 0, :], k.xt[p][:, 1, :])[i]
            act.wait_ge(k.conv_done, G * 4 + (i + 1))
            if i == 0 and (not static or G >= 2):
                act.wait_ge(k.y_done, G * 2 - 2)
            act.activation(dst, k.cacc[i % 2][:, :], ACT.Silu).then_inc(k.xbc_done, 1)

        step(0)
        tap0(0)
        if ssd:
            exps(g, q)
            if not (static and g == 0):
                gate_rstd(g - 1)
        conv_silu(0)
        step(1)
        tap0(1)
        if ssd:
            b_tokens(g)
        conv_silu(1)
        step(2)
        tap0(2)
        conv_silu(2)
        step(3)
        tap0(3)
        conv_silu(3)
        step(4)
        act.activation(k.sz[p][:, 0, :], ps[:, 1, :], ACT.Silu).then_inc(k.z_done, 1)
        if ssd:
            act.wait_ge(k.ydiag_ready, g + 1)
            load_cs(g + 1)
        step(5)
        act.activation(k.sz[p][:, 1, :], ps[:, 2, :], ACT.Silu).then_inc(k.z_done, 1)
        if ssd:
            y_squares(g)

    def exps(g, q):
        act.wait_ge(k.cs_loaded, g * 16 + 16)
        if not isinstance(g, int) or g >= 1:
            act.wait_ge(k.y_done, g * 2)
        for half in range(2):
            r = slice(64 * half, 64 * half + 64)
            src = k.csb[r, :, :].rearrange("p (j e) t -> p e j t", e=2)[:, half, :, SC:SEQ]
            act.activation(k.e2[r, :, :], src, ACT.Exp).then_inc(k.e_done, 1)
        act.activation(k.dec[:, :, :], k.csb[:, :, :].rearrange("p h (c t) -> p h c t", t=SC)[:, :, :, SC - 1],
                       ACT.Exp).then_inc(k.e_done, 1)
        for hh in range(HG):
            act.wait_ge(k.seg_done, g * HG + (hh + 1))
            act.activation(k.csb[:, hh, :], k.csb[:, hh, :], ACT.Exp).then_inc(k.l_done, 1)

    def b_tokens(g):
        act.wait_ge(k.btok_ready, g + 1)
        if not isinstance(g, int) or g >= 1:
            act.wait_ge(k.state_ready, g)
        act.activation(k.btok[:, :, :], ps[:, 7, :].rearrange("p (c n) -> p c n", c=NC), ACT.Copy).then_inc(k.btok_done, 1)

    def gate_rstd(g):
        act.wait_ge(k.gate_sums_ready, g + 1)
        if not isinstance(g, int) or g >= 1:
            act.wait_ge(k.yn_scaled, g * 2)
        act.activation(k.grstd[:, :], ps[:, 3, :], ACT.Ln, bias=k.eps[:, :], scale=1.0 / (DI // NG)).then_inc(k.gln_done, 1)
        act.wait_ge(k.gln_done, g + 1)
        act.activation(k.grstd[:, :], k.grstd[:, :], ACT.Exp, scale=-0.5).then_inc(k.gate_rstd_done, 1)

    def y_squares(g):
        for j in range(2):
            act.wait_ge(k.y_done, g * 2 + (j + 1))
            if j == 0 and (not isinstance(g, int) or g >= 1):
                act.wait_ge(k.gate_acc_done, g)
            act.activation(k.gsq[j][:, :], k.yg[:, g * 2 + j, :], ACT.Square).then_inc(k.gsq_done, 1)

    act.wait_ge(k.eps_set, 1)
    hi(RING, 0)
    act.activation(k.cacc[0][:, :], ps[:, 0, :], ACT.Identity, bias=col("a_convb", 16), scale=col("a_conv", 96 + 16)).then_inc(k.tap0_done, 1)
    hi(RING + 1, 1)
    act.activation(k.cacc[1][:, :], ps[:, 1, :], ACT.Identity, bias=col("a_convb", 24), scale=col("a_conv", 96 + 24)).then_inc(k.tap0_done, 1)
    hi(RING + 2, 2)
    act.wait_ge(k.conv_done, 1)
    act.activation(k.bt[0][:, :], k.cacc[0][:, :], ACT.Silu).then_inc(k.xbc_done, 1)
    act.wait_ge(k.conv_done, 2)
    act.activation(k.ct[0][:, :], k.cacc[1][:, :], ACT.Silu).then_inc(k.xbc_done, 1)
    act.wait_ge(k.xbc_done, 1)
    act.activation(k.cacc[0][:, :], ps[:, 2, :], ACT.Identity, bias=col("a_convb", 0), scale=col("a_conv", 96)).then_inc(k.tap0_done, 1)
    hi(RING + 3, 0)
    act.wait_ge(k.xbc_done, 2)
    act.activation(k.cacc[1][:, :], ps[:, 0, :], ACT.Identity, bias=col("a_convb", 1), scale=col("a_conv", 97)).then_inc(k.tap0_done, 1)
    for i in range(2):
        act.wait_ge(k.conv_done, 3 + i)
        act.activation(k.xt[0][:, i, :], k.cacc[i][:, :], ACT.Silu).then_inc(k.xbc_done, 1)
    hi(RING + 4, 1)
    act.activation(k.sz[0][:, 0, :], ps[:, 1, :], ACT.Silu).then_inc(k.z_done, 1)
    dt_steps()
    hi(RING + 5, 2)
    act.activation(k.sz[0][:, 1, :], ps[:, 2, :], ACT.Silu).then_inc(k.z_done, 1)
    in_group(1, 1)
    with act.Fori(1, NG // 2) as i:
        in_group(i * 2, 0)
        in_group(i * 2 + 1, 1)
    g, q = NG - 1, (NG - 1) % 2
    exps(g, q)
    gate_rstd(g - 1)
    b_tokens(g)
    def yn_hi(kk, s):
        if isinstance(kk, int):
            act.wait_ge(k.yn_scaled, kk + 1)
        if not isinstance(kk, int) or kk >= RING:
            act.wait_ge(k.slab_used, kk + (OUT0 - RING + 1))
        act.activation(k.yn_hi[s][:, :], k.yg[:, kk, :], ACT.Copy).then_inc(k.yn_hi_done, 1)

    y_squares(g)
    gate_rstd(g)
    for kk in range(3):
        yn_hi(kk, (OUT0 + kk) % RING)
    act.wait_ge(k.yn_scaled, OUT_K)
    for kk in range(2):
        hi(OUT0 + kk + RING, (OUT0 + kk) % RING)
        yn_hi(kk + RING, (OUT0 + kk) % RING)
    with act.Fori(0, 3) as i:
        for j in range(3):
            s = (OUT0 + 2 + j) % RING
            hi_loop(i * 3 + (OUT0 + 2 + j + RING), s, i + ((OUT0 + 2 + j + RING) // RING + 1))
            yn_hi(i * 3 + (2 + j + RING), s)
    for kk in range(11, 14):
        s = (OUT0 + kk) % RING
        hi(OUT0 + kk + RING, s)
        if kk + RING < OUT_K:
            yn_hi(kk + RING, s)

    def boundary(t, w_post, off, nxt, bias=False):
        for m in range(KT):
            if m < KT - 1:
                act.wait_ge(k.mix_ready, (KT - 1) * t + m + 1)
            else:
                act.wait_ge(k.slab_used, (UP[0], KV0, UP[1], N_SLABS)[t])
            b = col("b_o", m) if bias else None
            square(ps[:, m, :], b)
            kw = {"bias": k.bo_post[:, m:m + 1]} if bias else {}
            act.activation(k.mix[:, m, :], ps[:, m, :], ACT.Identity if bias else ACT.Copy,
                           scale=col(w_post, off + m), **kw).then_inc(k.mix_read, 1)
        if nxt:
            hi(nxt + 1, (nxt + 1) % RING)
        rstd(1 + 2 * t, k.rpost[:, :])
        if nxt:
            hi(nxt + 2, (nxt + 2) % RING)

    def next_parts(t, name, off, dst, with_squares=True):
        for c in range(KT):
            act.wait_ge(k.h_done, KT * t + c + 1)
            act.activation(dst[:, c, :], k.h[:, c, :], ACT.Copy, scale=col(name, off + c)).then_inc(k.hi_part_done, 1)
            if with_squares:
                square(k.h[:, c, :])

    def ffn(l):
        u0, d0, i0 = UP[l], DOWN[l], l * FT
        def pair(p, par2, stat, lap0):
            for v in range(2):
                s = (u0 + 2 * stat + v) % RING
                if lap0 is None:
                    hi(u0 + 2 * p + v + RING, s)
                else:
                    hi_loop(p * 2 + (u0 + v + RING), s, lap0(v))
                act.wait_ge(k.u_done, p * 2 + (2 * i0 + v + 1))
                tile = p + (v * FT)
                if v == 0 and not (isinstance(p, int) and i0 + p < 2):
                    act.wait_ge(k.f_prod_done, p + (i0 - 1))
                act.activation(k.cv[par2][v][:, :], k.u[par2][v][:, :], ACT.Identity,
                               bias=col("f_convb", tile + l * 2 * FT),
                               scale=col("f_conv", tile + (l * 3 + 2) * 2 * FT)).then_inc(k.ftap0_done, 1)
            act.wait_ge(k.fconv_done, p * 2 + (2 * i0 + 1))
            act.activation(k.cv[par2][0][:, :], k.cv[par2][0][:, :], ACT.Silu).then_inc(k.fsilu_done, 1)
            act.wait_ge(k.f_prod_done, p + (i0 + 1))
            act.activation(k.f_hi[:, p, :], k.u[par2][0][:, :], ACT.Copy).then_inc(k.f_hi_done, 1)

        for p in range(4):
            pair(p, p % 2, p, None)
        with act.Fori(0, 3) as r:
            for j in range(6):
                p = r * 6 + (4 + j)
                lap0 = lambda v, j=j: r * 4 + ((u0 + 2 * (4 + j) + v + RING) // RING + 1)
                pair(p, j % 2, 4 + j, lap0)
        for kk in range(2):
            hi(d0 + kk + RING, (d0 + kk) % RING)
        with act.Fori(0, 5) as r:
            for j in range(3):
                n = d0 + 2 + j + RING
                hi_loop(r * 3 + n, n % RING, r + (n // RING + 1))
        for n in range(d0 + 17 + RING, min(d0 + 20 + RING, N_SLABS)):
            hi(n, n % RING)

    boundary(0, "a_post", 0, UP[0])
    next_parts(0, "f_pre", 0, k.hs_hi)
    rstd(2, k.rpre[:, :])
    ffn(0)
    boundary(1, "f_post", 0, KV0)
    next_parts(1, "kvn", 0, k.hk_hi)
    rstd(4, k.rpre[:, :])
    for c in range(KT):
        act.activation(k.hs_hi[:, c, :], k.h[:, c, :], ACT.Copy, scale=col("b_pre", c)).then_inc(k.hi_part_done, 1)
    for i in range(12):
        n = KV0 + i
        hi(n + RING, n % RING)
        act.wait_ge(k.qkv_read, i + 1)
        src = k.qs[i % 2][:, :]
        if i < 4:
            dst = (k.kp if i < 2 else k.vp)[:, i % 2, CH:CH + SEQ]
            b = col("b_kv", i)
        else:
            dst = k.qt[:, (i - 4) // 4, :, ((i - 4) % 4) * CH:((i - 4) % 4 + 1) * CH]
            src = src.rearrange("p (c t) -> p c t", t=CH)
            b = col("b_q", i - 4)
        act.activation(dst, src, ACT.Identity, bias=b).then_inc(k.kqv_done, 1)
        if 6 <= i < 10:
            b = i - 6
            act.wait_ge(k.vtok_ready, b + 1)
            act.activation(k.vtok[:, 2 * b:2 * b + 2, :, :],
                           ps[:, 7, :].rearrange("p (w t d) -> p w t d", w=2, t=2), ACT.Copy).then_inc(k.vtok_done, 1)
    for a in range(2 * NCH + 1):
        if a < 2 * NCH:
            c = a % NCH
            lo_key = CH if c == 0 else 0
            act.wait_ge(k.nmax_done, a + 1)
            if a >= 2:
                act.wait_ge(k.pt_ready, a - 1)
            for u in range(4):
                act.activation(k.pr[a % 2][:, u, lo_key:P], ps[:, 2 * (a % 2) + u // 2, (u % 2) * P + lo_key:(u % 2 + 1) * P], ACT.Exp,
                               bias=k.nmax[a % 2][:, u:u + 1], scale=CH ** -0.5, accum_out=k.psum_[a % 2][:, u:u + 1])
            act.activation(k.esink[a % 2][:, :], k.dsink[a % 2][:, :], ACT.Exp).then_inc(k.exp_done, 1)
        if a >= 1:
            b = a - 1
            kt, c = b // NCH, b % NCH
            act.wait_ge(k.pt_ready, b + 1)
            if b >= 2:
                act.wait_ge(k.o_ready, b - 1)
            act.activation(k.pts[b % 2][:, :], ps[:, 4 + b % 2, :], ACT.Copy).then_inc(k.pt_done, 1)
            act.wait_ge(k.o_ready, b + 1)
            act.activation(k.o_hi[:, kt * 4:kt * 4 + 4, c * CH:(c + 1) * CH],
                           ps[:, 6 + b % 2, 0:256].rearrange("p (t q) -> p t q", t=4), ACT.Copy).then_inc(k.o_hi_done, 1)
    for kk in range(KT - 2):
        hi(O0 + kk + RING, (O0 + kk) % RING)
    act.wait_ge(k.misc, 1)
    boundary(2, "b_post", 0, UP[1], bias=True)
    next_parts(2, "f_pre", KT, k.hs_hi)
    rstd(6, k.rpre[:, :])
    ffn(1)
    boundary(3, "f_post", KT, None)


def dve_program(k, dve):
    ps, par = k.ps, k.par
    own = Steps(dve, k.dve_own)

    def col(name, i):
        if isinstance(i, int):
            return par[:, COL[name] + i:COL[name] + i + 1]
        return par[:, ds(i + COL[name], 1)]

    adds = [0]

    def add_square(m, norm):
        q = adds[0]
        dve.wait_ge(k.sq_done, q + 1)
        if m == 0:
            if norm:
                dve.wait_ge(k.sums_ready, norm)
            if q:
                dve.wait_ge(k.sq_added, q)
            dve.tensor_copy(k.acc[:, :], k.sq[q % 2][:, :]).then_inc(k.sq_added, 1)
        else:
            dve.wait_ge(k.sq_added, q)
            dve.tensor_tensor(k.acc[:, :], k.acc[:, :], k.sq[q % 2][:, :], ALU.add).then_inc(k.sq_added, 1)
        adds[0] += 1

    dve.memset(k.eps[:, :], EPS).then_inc(k.eps_set, 1)
    for c in range(KT):
        add_square(c, 0)
    dve.wait_ge(k.par_loaded, 16)
    dve.wait_ge(k.rstd_done, 1)
    for c in range(KT + 1):
        if c < KT:
            dve.scalar_tensor_tensor(out=k.hn[:, c, :], in0=k.h[:, c, :], scalar=col("a_pre", c), in1=k.rpre[:, :],
                                     op0=ALU.mult, op1=ALU.mult).then_inc(k.hn_done, 1)
        if c:
            dve.wait_ge(k.hi_part_done, c)
            dve.tensor_tensor(k.hs_lo[:, c - 1, :], k.hn[:, c - 1, :], k.hs_hi[:, c - 1, :], ALU.subtract).then_inc(k.lo_part_done, 1)

    def conv(G, i):
        tile = (G + 16, G + 24, G * 2, G * 2 + 1)[i]
        acc = k.cacc[i % 2]
        dve.wait_ge(k.tap0_done, G * 4 + (i + 1))
        for s in (1, 2, 3):
            ins = dve.scalar_tensor_tensor(out=acc[:, s:SEQ], in0=ps[:, i % RING, 0:SEQ - s],
                                           scalar=col("a_conv", (3 - s) * 32 + tile), in1=acc[:, s:SEQ],
                                           op0=ALU.mult, op1=ALU.add)
            if s < 3:
                own.link(ins)
            else:
                ins.then_inc(k.conv_done, 1)

    def dt_steps():
        dve.wait_ge(k.dt_exp, 1)
        dve.tensor_scalar(k.dtu[:, :], k.dte[:, :], 1.0, None, ALU.add).then_inc(k.dt_u, 1)
        dve.wait_ge(k.dt_u, 1)
        own.link(dve.tensor_scalar(k.dta[:, :], k.dtu[:, :], -1.0, None, ALU.add))
        own.link(dve.tensor_tensor(k.dte[:, :], k.dte[:, :], k.dta[:, :], ALU.subtract))
        dve.wait_ge(k.dt_exp, 3)
        own.link(dve.tensor_tensor(k.dte[:, :], k.dte[:, :], k.dtr[:, :], ALU.mult))
        own.link(dve.tensor_tensor(k.dte[:, :], k.dte[:, :], k.dtl[:, :], ALU.add))
        own.link(dve.scalar_tensor_tensor(out=k.dt_[:, :], in0=k.dtx[:, :], scalar=0.0, in1=k.dte[:, :], op0=ALU.max, op1=ALU.add))
        own.link(dve.tensor_scalar(k.dta[:, :], k.dt_[:, :], k.aneg[:, :], -1.0, ALU.mult, ALU.mult))
        for c in range(NC):
            t = slice(c * SC, (c + 1) * SC)
            own.done(dve.tensor_tensor_scan(out=k.cs[:, t], data0=k.ones[0:NH, :], data1=k.dta[:, t], initial=0.0,
                                            op0=ALU.mult, op1=ALU.add))
        own.wait()
        dve.tensor_scalar(k.ncs[:, :], k.cs[:, :], -1.0, None, ALU.mult).then_inc(k.cs_done, 1)
        dve.wait_ge(k.dt_exp, 7)
        dve.wait_ge(k.cs_done, 1)
        dve.tensor_tensor(k.dtw[:, :], k.dtw[:, :], k.dt_[:, :], ALU.mult).then_inc(k.dtw_done, 1)
        dve.wait_ge(k.tok_ready, 1)
        dve.tensor_copy(k.tok[:, :], ps[:, 4, 0:NC * 96]).then_inc(k.tok_done, 1)
        dve.wait_ge(k.tok_done, 1)
        dve.wait_ge(k.small_loaded, 16 * 6)
        dve.wait_ge(k.cs_stored, 16)

    tokv = k.tok[:, :].rearrange("p (c i h) -> p c i h", c=NC, i=3)

    def group_columns(g):
        if not isinstance(g, int) or g >= 1:
            dve.wait_ge(k.l_done, g * 4)
            dve.wait_ge(k.xtok_done, g * 4)
        src = tokv[:, :, :, ds(g * HG, HG)] if not isinstance(g, int) else tokv[:, :, :, g * HG:(g + 1) * HG]
        dve.tensor_scalar(k.tokg[:, :, :, :], src, 1.0, None, ALU.mult).then_inc(k.tokg_done, 1)
        dve.wait_ge(k.tokg_done, g + 1)

    def segments(g):
        dve.wait_ge(k.cs_loaded, g * 16 + 16)
        dve.wait_ge(k.e_done, g * 3 + 3)
        for hh in range(HG):
            for c in range(NC):
                t = slice(c * SC, (c + 1) * SC)
                last = dve.tensor_scalar(k.csb[:, hh, t], k.csb[:, hh, t], k.tokg[:, c, 1, hh:hh + 1], 0.0, ALU.add, ALU.min)
            last.then_inc(k.seg_done, 1)

    def ssd_1(g):
        dve.wait_ge(k.cb_ready, g + 1)
        if not isinstance(g, int) or g >= 1:
            dve.wait_ge(k.m_done, g * 4)
        dve.tensor_tensor(k.cbm[:, :].rearrange("p (c l) -> p c l", c=NC), ps[:, 3, :].rearrange("p (c l) -> p c l", c=NC),
                          bcast(k.tri[:, :].rearrange("p (o l) -> p o l", o=1), [P, NC, SC]), ALU.mult).then_inc(k.cbm_done, 1)
        if not isinstance(g, int) or g >= 1:
            dve.wait_ge(k.ydiag_ready, g)
        for j in range(2):
            dve.wait_ge(k.xtok_ready, g * 2 + (j + 1))
            for dst, i in ((k.xdt, 0), (k.xdd, 2)):
                w = k.tokg[:, :, i, 2 * j:2 * j + 2].rearrange("p c (h o) -> p c h o", o=1)
                dve.tensor_tensor(dst[:, :, j * P:(j + 1) * P].rearrange("p c (h d) -> p c h d", h=2),
                                  ps[:, 5 + j, :].rearrange("p (c h d) -> p c h d", c=NC, h=2),
                                  bcast(w, [P, NC, 2, 64]), ALU.mult).then_inc(k.xtok_done, 1)

    def ssd_2(g):
        dve.wait_ge(k.cbm_done, g + 1)
        for hh in range(HG):
            dve.wait_ge(k.l_done, g * 4 + (hh + 1))
            dve.tensor_tensor(k.csb[:, hh, :], k.csb[:, hh, :], k.cbm[:, :], ALU.mult).then_inc(k.m_done, 1)

    def ssd_3(g):
        dve.wait_ge(k.state_ready, g + 1)
        dve.wait_ge(k.e_done, g * 3 + 3)
        if not isinstance(g, int) or g >= 1:
            dve.wait_ge(k.yoff_ready, g)
        own.link(dve.tensor_scalar(k.hst[:, 0, :], ps[:, 4, 0:256], 1.0, None, ALU.mult))
        for c in (1, 2):
            w = bcast(k.dec[:, :, c:c + 1], [P, HG, 64])
            own.link(dve.tensor_tensor(k.htmp[:, :].rearrange("p (h d) -> p h d", h=HG),
                                       k.hst[:, c - 1, :].rearrange("p (h d) -> p h d", h=HG), w, ALU.mult))
            src = ps[:, 4, 256:512] if c == 1 else ps[:, 3, 0:256]
            ins = dve.tensor_tensor(k.hst[:, c, :], k.htmp[:, :], src, ALU.add)
            if c == 1:
                own.link(ins)
            else:
                ins.then_inc(k.state_done, 1)

    def ssd_4(g, q):
        dve.wait_ge(k.ydiag_ready, g + 1)
        if not isinstance(g, int) or g >= 1:
            dve.wait_ge(k.y_done, g * 2)
        for j in range(2):
            tile = g * 2 + j
            dcol = k.dskip[:, tile:tile + 1] if isinstance(g, int) else k.dskip[:, ds(tile, 1)]
            own.link(dve.scalar_tensor_tensor(out=k.yt[j][:, :], in0=k.xt[q][:, j, :], scalar=dcol, in1=ps[:, 5 + j, :],
                                              op0=ALU.mult, op1=ALU.add))
            if j == 0:
                dve.wait_ge(k.yoff_ready, g + 1)
            own.link(dve.tensor_tensor(k.yo[:, :], ps[:, (7, 4)[j], SC:SEQ], k.e2[:, j, :], ALU.mult))
            own.link(dve.tensor_tensor(k.yt[j][:, SC:SEQ], k.yt[j][:, SC:SEQ], k.yo[:, :], ALU.add))
            if j == 0:
                dve.wait_ge(k.z_done, g * 2 + 2)
            dve.tensor_tensor(k.yg[:, tile, :], k.yt[j][:, :], k.sz[q][:, j, :], ALU.mult).then_inc(k.y_done, 1)

    def ssd_5(g):
        dve.wait_ge(k.gsq_done, g * 2 + 2)
        if not isinstance(g, int) or g >= 1:
            dve.wait_ge(k.gate_sums_ready, g)
        dve.tensor_tensor(k.gacc[:, :], k.gsq[0][:, :], k.gsq[1][:, :], ALU.add).then_inc(k.gate_acc_done, 1)

    def norm_y(g):
        dve.wait_ge(k.gate_rstd_done, g + 1)
        for j in range(2):
            tile = g * 2 + j
            dve.scalar_tensor_tensor(out=k.yg[:, tile, :], in0=k.yg[:, tile, :], scalar=col("a_gate", tile),
                                     in1=k.grstd[:, :], op0=ALU.mult, op1=ALU.mult).then_inc(k.yn_scaled, 1)

    def in_group(G, p):
        g, q = G - 1, 1 - p
        group_columns(g)
        segments(g)
        if not (isinstance(G, int) and G == 1):
            ssd_5(g - 1)
        conv(G, 0)
        conv(G, 1)
        ssd_1(g)
        if not (isinstance(G, int) and G == 1):
            norm_y(g - 1)
        conv(G, 2)
        ssd_2(g)
        ssd_3(g)
        conv(G, 3)
        ssd_4(g, q)

    for i in range(4):
        conv(0, i)
    dt_steps()
    in_group(1, 1)
    with looped(dve, 1, NG // 2, (own, 2 * (4 * 2 + 4 + 6))) as i:
        in_group(i * 2, 0)
        in_group(i * 2 + 1, 1)
    g, q = NG - 1, (NG - 1) % 2
    group_columns(g)
    segments(g)
    ssd_5(g - 1)
    ssd_1(g)
    norm_y(g - 1)
    ssd_2(g)
    ssd_3(g)
    ssd_4(g, q)
    ssd_5(g)
    norm_y(g)
    for kk in range(OUT_K):
        b = (OUT0 + kk) % RING
        dve.wait_ge(k.yn_hi_done, kk + 1)
        dve.wait_ge(k.yn_scaled, OUT_K)
        dve.tensor_tensor(k.yn_lo[b][:, :], k.yg[:, kk, :], k.yn_hi[b][:, :], ALU.subtract).then_inc(k.yn_done, 1)

    def post(t):
        for m in range(KT):
            add_square(m, 1 + 2 * t)
        dve.wait_ge(k.rstd_done, 2 + 2 * t)

    def update(t, c):
        if c == 0:
            dve.wait_ge(k.mix_read, KT * (t + 1))
        own.link(dve.tensor_tensor(k.mix[:, c, :], k.mix[:, c, :], k.rpost[:, :], ALU.mult))
        dve.tensor_tensor(k.h[:, c, :], k.h[:, c, :], k.mix[:, c, :], ALU.add).then_inc(k.h_done, 1)

    def low(t, c, name, off, hi, lo, base):
        dve.wait_ge(k.h_done, KT * t + c + 1)
        dve.wait_ge(k.hi_part_done, base + c + 1)
        dve.scalar_tensor_tensor(out=lo[:, c, :], in0=k.h[:, c, :], scalar=col(name, off + c), in1=hi[:, c, :],
                                 op0=ALU.mult, op1=ALU.subtract).then_inc(k.lo_part_done, 1)

    def boundary(t, name, off, hi, lo):
        post(t)
        if name is None:
            for c in range(KT):
                update(t, c)
            return
        update(t, 0)
        for c in range(KT):
            if c + 1 < KT:
                update(t, c + 1)
            low(t, c, name, off, hi, lo, k.lo_base[t])
            add_square(c, 2 + 2 * t)

    def ffn(l):
        u0, d0, i0 = UP[l], DOWN[l], l * FT
        dve.wait_ge(k.rstd_done, k.pre_count[l])

        def pair(p, par2, stat):
            for v in range(2):
                u, cv = k.u[par2][v], k.cv[par2][v]
                dve.wait_ge(k.slab_used, p * 2 + (u0 + v + 1))
                if not (isinstance(p, int) and i0 + p < 2) and v == 0:
                    dve.wait_ge(k.f_done, p + (i0 - 1))
                dve.tensor_tensor(u[:, :], ps[:, (u0 + 2 * stat + v) % 6, :], k.rpre[:, :], ALU.mult).then_inc(k.u_done, 1)
                dve.wait_ge(k.ftap0_done, p * 2 + (2 * i0 + v + 1))
                for s in (1, 2):
                    w = col("f_conv", p + (v * FT + (l * 3 + 2 - s) * 2 * FT))
                    ins = dve.scalar_tensor_tensor(out=cv[:, s:SEQ], in0=u[:, 0:SEQ - s], scalar=w, in1=cv[:, s:SEQ],
                                                   op0=ALU.mult, op1=ALU.add)
                    if s == 1:
                        own.link(ins)
                    else:
                        ins.then_inc(k.fconv_done, 1)
            dve.wait_ge(k.fconv_done, p * 2 + (2 * i0 + 2))
            dve.wait_ge(k.fsilu_done, p + (i0 + 1))
            dve.tensor_tensor(k.u[par2][0][:, :], k.cv[par2][0][:, :], k.cv[par2][1][:, :], ALU.mult).then_inc(k.f_prod_done, 1)
            dve.wait_ge(k.f_prod_done, p + (i0 + 1))
            dve.wait_ge(k.f_hi_done, p + (i0 + 1))
            dve.tensor_tensor(k.f_lo[:, p, :], k.u[par2][0][:, :], k.f_hi[:, p, :], ALU.subtract).then_inc(k.f_done, 1)

        for p in range(4):
            pair(p, p % 2, p)
        with looped(dve, 0, 3, (own, 12)) as r:
            for j in range(6):
                pair(r * 6 + (4 + j), j % 2, 4 + j)

    boundary(0, "f_pre", 0, k.hs_hi, k.hs_lo)
    ffn(0)
    dve.tensor_tensor(k.bo_post[:, :], par[:, COL["b_o"]:COL["b_o"] + KT], par[:, COL["b_post"]:COL["b_post"] + KT], ALU.mult).then_inc(k.misc, 1)
    dve.wait_ge(k.small_loaded, 16 * 6)
    dve.tensor_scalar(k.nsink[:, :], k.nsink[:, :], -1.0, None, ALU.mult).then_inc(k.misc, 1)
    boundary(1, "kvn", 0, k.hk_hi, k.hk_lo)
    for c in range(KT):
        low(1, c, "b_pre", 0, k.hs_hi, k.hs_lo, k.lo_q_base)
    dve.memset(k.kp[:, :, 0:CH], 0.0).then_inc(k.pads_set, 1)
    dve.memset(k.vp[:, :, 0:CH], 0.0).then_inc(k.pads_set, 1)
    dve.memset(k.pr[0][:, :, 0:CH], 0.0).then_inc(k.pads_set, 1)
    dve.wait_ge(k.rstd_done, 5)
    for i in range(12):
        n = KV0 + i
        dve.wait_ge(k.slab_used, n + 1)
        if i >= 2:
            dve.wait_ge(k.kqv_done, i - 1)
        dve.tensor_tensor(k.qs[i % 2][:, :], ps[:, n % 6, :], k.rpre[:, :], ALU.mult).then_inc(k.qkv_read, 1)

    dve.wait_ge(k.misc, 2)

    def row_max(a):
        kt, c = a // NCH, a % NCH
        lo_key = CH if c == 0 else 0
        b = a % 2
        dve.wait_ge(k.scores_ready, a + 1)
        if a >= 2:
            dve.wait_ge(k.exp_done, a - 1)
        src = ps[:, 2 * b:2 * b + 2, 0:2 * P].rearrange("p g (u t) -> p g u t", u=2)[:, :, :, lo_key:P]
        own.link(dve.tensor_reduce(out=k.rmax[b][:, :].rearrange("p (g u) -> p g u", g=2), in_=src,
                                   axis=AX_X, op=ALU.max))
        sink = k.nsink[:, kt * 4:kt * 4 + 4]
        own.link(dve.scalar_tensor_tensor(out=k.nmax[b][:, :], in0=k.rmax[b][:, :], scalar=-(CH ** -0.5), in1=sink,
                                          op0=ALU.mult, op1=ALU.min))
        dve.tensor_tensor(k.dsink[b][:, :], k.nmax[b][:, :], sink, ALU.subtract).then_inc(k.nmax_done, 1)

    def low_o(a):
        kt, c = a // NCH, a % NCH
        dve.wait_ge(k.o_hi_done, a + 1)
        dst = slice(c * CH, (c + 1) * CH)
        dve.tensor_tensor(k.o_lo[:, kt * 4:kt * 4 + 4, dst], ps[:, 6 + a % 2, 0:256].rearrange("p (t q) -> p t q", t=4),
                          k.o_hi[:, kt * 4:kt * 4 + 4, dst], ALU.subtract).then_inc(k.o_done, 1)

    row_max(0)
    for a in range(2 * NCH):
        if a + 1 < 2 * NCH:
            row_max(a + 1)
        b = a % 2
        dve.wait_ge(k.exp_done, a + 1)
        own.link(dve.tensor_tensor(k.den[:, :], k.psum_[b][:, :], k.esink[b][:, :], ALU.add))
        if a:
            dve.wait_ge(k.probs_done, a)
        own.link(dve.reciprocal(k.rden[:, :], k.den[:, :]))
        w = bcast(k.rden[:, :].rearrange("p (u o) -> p u o", o=1), [P, 4, P])
        if a % NCH == 0:
            if a:
                dve.wait_ge(k.pt_ready, a - 1)
                dve.memset(k.pr[b][:, :, 0:CH], 0.0).then_inc(k.pads_set, 1)
            dve.wait_ge(k.pads_set, 3 + a // NCH)
        dve.tensor_tensor(k.pr[b][:, :, :], k.pr[b][:, :, :], w, ALU.mult).then_inc(k.probs_done, 1)
        if a >= 1:
            low_o(a - 1)
    low_o(2 * NCH - 1)
    boundary(2, "f_pre", KT, k.hs_hi, k.hs_lo)
    ffn(1)
    boundary(3, None, 0, None, None)


def trunk(nc, d_x, d_slabs, d_wdt, d_par, d_hpar, d_dskip, d_sinks, d_out):
    k = Core()
    k.d_x, k.d_slabs, k.d_wdt, k.d_par, k.d_hpar, k.d_dskip, k.d_sinks, k.d_out = (
        d_x, d_slabs, d_wdt, d_par, d_hpar, d_dskip, d_sinks, d_out)
    k.d_cs = nc.dram_tensor("cs_scratch", (NH, SEQ), F32, kind="Internal").ap()
    with ExitStack() as ctx:
        def sb(stack, name, shape, dt=F32):
            return stack.enter_context(nc.sbuf_tensor(name, shape, dt))

        keep = ctx
        k.h = sb(keep, "h", [P, KT, SEQ])
        k.hs_hi, k.hs_lo = (sb(keep, f"hs_{x}", [P, KT, SEQ], F32R) for x in ("hi", "lo"))
        k.raw = [sb(keep, f"raw{s}", [P, DM]) for s in range(RING)]
        k.whi = [sb(keep, f"whi{s}", [P, DM], F32R) for s in range(RING)]
        k.wlo = [sb(keep, f"wlo{s}", [P, DM], F32R) for s in range(RING)]
        k.par = sb(keep, "par", [P, N_COLS])
        k.hpar = sb(keep, "hpar", [NH, 2])
        k.dskip = sb(keep, "dskip", [P, OUT_K])
        k.nsink = sb(keep, "nsink", [P, 8])
        k.ones, k.ident, k.tri = (sb(keep, x, [P, P]) for x in ("ones", "ident", "tri"))
        k.eps = sb(keep, "eps", [P, 1])
        k.bo_post = sb(keep, "bo_post", [P, KT])
        k.rpre, k.rpost, k.acc, k.lnv = (sb(keep, x, [P, SEQ]) for x in ("rpre", "rpost", "acc", "lnv"))
        k.sq = [sb(keep, f"sq{i}", [P, SEQ]) for i in range(2)]

        with ExitStack() as st:
            k.yg = sb(st, "yg", [P, OUT_K, SEQ])
            k.hn = k.yg
            with ExitStack() as s2:
                k.xt = [sb(s2, f"xt{i}", [P, 2, SEQ]) for i in range(2)]
                k.bt = [sb(s2, f"bt{i}", [P, SEQ]) for i in range(2)]
                k.ct = [sb(s2, f"ct{i}", [P, SEQ]) for i in range(2)]
                k.sz = [sb(s2, f"sz{i}", [P, 2, SEQ]) for i in range(2)]
                k.cacc = [sb(s2, f"cacc{i}", [P, SEQ]) for i in range(2)]
                k.csb = sb(s2, "csb", [P, HG, SEQ])
                k.btok = sb(s2, "btok", [P, NC, P])
                k.xdt, k.xdd = (sb(s2, x, [P, NC, 256]) for x in ("xdt", "xdd"))
                k.cbm = sb(s2, "cbm", [P, SEQ])
                k.hst = sb(s2, "hst", [P, 3, 256])
                k.htmp = sb(s2, "htmp", [P, 256])
                k.dec = sb(s2, "dec", [P, HG, NC])
                k.e2 = sb(s2, "e2", [P, 2, SEQ - SC])
                k.tok = sb(s2, "tok", [P, NC * 96])
                k.tokg = sb(s2, "tokg", [P, NC, 3, HG])
                k.wdt = sb(s2, "wdt", [P, KT * NH])
                k.yt = [sb(s2, f"yt{i}", [P, SEQ]) for i in range(2)]
                k.yo = sb(s2, "yo", [P, SEQ - SC])
                k.grstd = sb(s2, "grstd", [P, SEQ])
            k.dtx, k.dta = k.yt[0][0:NH, :], k.yt[1][0:NH, :]
            with ExitStack() as s3:
                k.yn_hi = [sb(s3, f"yn_hi{i}", [P, SEQ], F32R) for i in range(RING)]
                k.yn_lo = [sb(s3, f"yn_lo{i}", [P, SEQ], F32R) for i in range(RING)]
        k.dte, k.dtu = k.rpost[0:NH, :], k.acc[0:NH, :]
        k.dtl, k.dtr = k.lnv[0:NH, :], k.sq[0][0:NH, :]
        k.dt_, k.ncs = k.xdt[0:NH, 0:2, :].rearrange("p c t -> p (c t)"), k.xdt[0:NH, 2:4, :].rearrange("p c t -> p (c t)")
        k.dtw, k.cs = k.xdd[0:NH, 0:2, :].rearrange("p c t -> p (c t)"), k.xdd[0:NH, 2:4, :].rearrange("p c t -> p (c t)")
        k.gsq = k.sq
        k.gacc = k.acc
        k.aneg = k.dec[0:NH, 0, 0:1]

        with ExitStack() as st:
            k.f_hi, k.f_lo = (sb(st, f"f_{x}", [P, FT, SEQ], F32R) for x in ("hi", "lo"))
            k.mix = sb(st, "mix", [P, KT, SEQ])
            k.u = [[k.mix[:, 4 * b + v, :] for v in range(2)] for b in range(2)]
            k.cv = [[k.mix[:, 4 * b + 2 + v, :] for v in range(2)] for b in range(2)]
        with ExitStack() as st:
            k.hk_hi, k.hk_lo = (sb(st, f"hk_{x}", [P, KT, SEQ], F32R) for x in ("hi", "lo"))
            k.o_hi, k.o_lo = k.hk_hi, k.hk_lo
            k.qt = sb(st, "qt", [P, 2, NCH, 4 * CH])
            k.kp, k.vp = (sb(st, x, [P, 2, CH + SEQ]) for x in ("kp", "vp"))
            k.vtok = sb(st, "vtok", [P, NCH, 2, P])
            k.pr = [sb(st, f"pr{i}", [P, 4, P]) for i in range(2)]
            k.pts = [sb(st, f"pts{i}", [P, 4 * P]) for i in range(2)]
            k.qs = [sb(st, f"qs{i}", [P, SEQ]) for i in range(2)]
            k.rmax, k.nmax, k.dsink, k.esink, k.psum_ = (
                [sb(st, f"{name}{i}", [P, 4]) for i in range(2)] for name in ("rmax", "nmax", "dsink", "esink", "psum"))
            k.den, k.rden = (sb(st, x, [P, 4]) for x in ("den", "rden"))

        k.ps = ctx.enter_context(nc.psum_tensor("ps", [P, 8, SEQ], F32))

        def sems(*names):
            return [ctx.enter_context(nc.semaphore(name)) for name in names]

        k.par_loaded, k.small_loaded, k.stored, k.ones_set, k.consts_ready, k.eps_set, k.pads_set, k.misc = sems(
            "par_loaded", "small_loaded", "stored", "ones_set", "consts_ready", "eps_set", "pads_set", "misc")
        k.hi_done, k.lo_done, k.slab_used = sems(
            "hi_done", "lo_done", "slab_used")
        k.sq_done, k.sq_added, k.sums_ready, k.ln_done, k.rstd_done, k.hn_done, k.hi_part_done, k.lo_part_done = sems(
            "sq_done", "sq_added", "sums_ready", "ln_done", "rstd_done", "hn_done", "hi_part_done", "lo_part_done")
        k.mix_ready, k.mix_read, k.h_done = sems(
            "mix_ready", "mix_read", "h_done")
        k.dt_ready, k.dt_exp, k.dt_u, k.cs_done, k.dtw_done, k.tok_ready, k.tok_done, k.cs_stored, k.cs_loaded = sems(
            "dt_ready", "dt_exp", "dt_u", "cs_done", "dtw_done", "tok_ready", "tok_done", "cs_stored", "cs_loaded")
        k.tap0_done, k.conv_done, k.xbc_done, k.z_done, k.tokg_done, k.e_done, k.seg_done, k.l_done, k.cb_ready, k.cbm_done = sems(
            "tap0_done", "conv_done", "xbc_done", "z_done", "tokg_done", "e_done", "seg_done", "l_done", "cb_ready", "cbm_done")
        k.btok_ready, k.btok_done, k.xtok_ready, k.xtok_done, k.m_done, k.state_ready, k.state_done, k.ydiag_ready = sems(
            "btok_ready", "btok_done", "xtok_ready", "xtok_done", "m_done", "state_ready", "state_done", "ydiag_ready")
        k.yoff_ready, k.y_done, k.gsq_done, k.gate_acc_done, k.gate_sums_ready, k.gln_done, k.gate_rstd_done = sems(
            "yoff_ready", "y_done", "gsq_done", "gate_acc_done", "gate_sums_ready", "gln_done", "gate_rstd_done")
        k.yn_scaled, k.yn_hi_done, k.yn_done = sems(
            "yn_scaled", "yn_hi_done", "yn_done")
        k.u_done, k.ftap0_done, k.fconv_done, k.fsilu_done, k.f_prod_done, k.f_hi_done, k.f_done = sems(
            "u_done", "ftap0_done", "fconv_done", "fsilu_done", "f_prod_done", "f_hi_done", "f_done")
        k.qkv_read, k.kqv_done, k.vtok_ready, k.vtok_done, k.scores_ready, k.nmax_done, k.exp_done, k.probs_done = sems(
            "qkv_read", "kqv_done", "vtok_ready", "vtok_done", "scores_ready", "nmax_done", "exp_done", "probs_done")
        k.pt_ready, k.pt_done, k.o_ready, k.o_hi_done, k.o_done = sems(
            "pt_ready", "pt_done", "o_ready", "o_hi_done", "o_done")
        k.act_own, k.dve_own = sems(
            "act_own", "dve_own")
        k.raw_loaded = [ctx.enter_context(nc.semaphore(f"raw_loaded{s}")) for s in range(RING)]
        k.x_loaded = [ctx.enter_context(nc.semaphore(f"x_loaded{c}")) for c in range(KT)]
        k.lo_base = {0: KT, 1: 2 * KT, 2: 4 * KT}
        k.lo_q_base = 3 * KT
        k.pre_count = [3, 7]

        block = ctx.enter_context(nc.Block())

        @block.sync
        def _(sp):
            sp_program(k, sp)

        @block.gpsimd
        def _(pool):
            pool_program(k, pool)

        @block.tensor
        def _(pe):
            pe_program(k, pe)

        @block.scalar
        def _(act):
            act_program(k, act)

        @block.vector
        def _(dve):
            dve_program(k, dve)


def kernel(**inputs):
    import concourse.bacc as bacc
    from concourse.bass_utils import run_bass_kernel_spmd

    a = {n: np.asarray(v) for n, v in inputs.items()}

    def tiles(v):
        return v.reshape(-1, P).T

    def slabs_a(w):
        return w.reshape(KT, P, -1, P).transpose(2, 1, 0, 3).reshape(-1, P, DM)

    w_in = a["a_in_proj"][0]
    w_in_tiles = slabs_a(w_in[:, :NG * GROUP_SLABS * P])
    xbc = DI // P
    order = [t for g in range(NG)
             for t in (xbc + 16 + g, xbc + 24 + g, xbc + 2 * g, xbc + 2 * g + 1, 2 * g, 2 * g + 1)]
    def by_kv(v, axis):
        v = np.moveaxis(v, axis, 0)
        v = v.reshape(2, 2, 4, 64, *v.shape[1:]).swapaxes(1, 2).reshape(v.shape)
        return np.moveaxis(v, 0, axis)

    slabs = np.concatenate([
        w_in_tiles[order], a["a_out_proj"][0].reshape(-1, P, DM),
        slabs_a(a["f_up"][0]).reshape(2, FT, P, DM).swapaxes(0, 1).reshape(-1, P, DM), a["f_down"][0].reshape(-1, P, DM),
        slabs_a(a["w_kv"]), slabs_a(by_kv(a["w_q"][0], 1)), by_kv(a["w_o"][0], 0).reshape(-1, P, DM),
        slabs_a(a["f_up"][1]).reshape(2, FT, P, DM).swapaxes(0, 1).reshape(-1, P, DM), a["f_down"][1].reshape(-1, P, DM),
    ])
    params = {
        "a_pre": a["a_norm_pre"], "a_conv": a["a_conv_w"], "a_convb": a["a_conv_b"], "a_gate": a["a_gate_norm"],
        "a_post": a["a_norm_post"], "kvn": a["kv_norm"], "b_kv": a["b_kv"], "b_pre": a["b_norm_pre"],
        "b_q": by_kv(a["b_q"][0], 0), "b_o": a["b_o"], "b_post": a["b_norm_post"], "f_pre": a["f_norm_pre"],
        "f_conv": a["f_conv_w"], "f_convb": a["f_conv_b"], "f_post": a["f_norm_post"],
    }
    arrays = {
        "x": a["x"][0].T.reshape(KT, P, SEQ).transpose(1, 0, 2),
        "slabs": slabs.reshape(N_SLABS * P, DM),
        "wdt": w_in[:, NG * GROUP_SLABS * P:].reshape(KT, P, NH).transpose(1, 0, 2).reshape(P, KT * NH),
        "par": np.concatenate([tiles(params[n]) for n in COL], axis=1),
        "hpar": np.stack([a["a_dt_bias"][0], a["a_a_log"][0]], axis=1),
        "dskip": a["a_d_skip"][0].reshape(OUT_K, 2).T,
        "sinks": a["sinks"][0].reshape(8, 2).T,
    }
    arrays = {n: np.ascontiguousarray(v) for n, v in arrays.items()}
    nc = bacc.Bacc("TRN2", target_bir_lowering=False, num_devices=1)
    args = [nc.dram_tensor(f"in_{n}", v.shape, F32, kind="ExternalInput").ap() for n, v in arrays.items()]
    out = nc.dram_tensor("out", (P, KT, SEQ), F32, kind="ExternalOutput").ap()
    trunk(nc, *args, out)
    r = run_bass_kernel_spmd(nc, [{f"in_{n}": v for n, v in arrays.items()}], core_ids=[0])
    got = np.asarray(r.results[0]["out"])
    return got.transpose(1, 0, 2).reshape(DM, SEQ).T[None].copy()
```

```python
from contextlib import ExitStack, contextmanager

import numpy as np
import concourse.bass as bass
from concourse import mybir
from concourse.alu_op_type import AluOpType as ALU

F32, F32R = mybir.dt.float32, mybir.dt.float32r
ACT = mybir.ActivationFunctionType
AX_X = mybir.AxisListType.X
ds = bass.ds

P = 128
DM, SEQ, EPS = 1024, 512, 1e-6
KT = DM // P
DI, DS, NG, NH = 2048, 128, 8, 32
HG = NH // NG
SC = 128
NC = SEQ // SC
GROUP_SLABS = 6
DFF = 2816
FT = DFF // P
CH = 64
NCH = SEQ // CH
RING = 4
CONV_BANK = (2, 0, 1, 2)
N_IN = NG * GROUP_SLABS
OUT0 = N_IN
OUT_K = DI // P
UP = [OUT0 + OUT_K, 0]
DOWN = [UP[0] + 2 * FT, 0]
KV0 = DOWN[0] + FT
Q0 = KV0 + 4
O0 = Q0 + KT
UP[1] = O0 + KT
DOWN[1] = UP[1] + 2 * FT
N_SLABS = DOWN[1] + FT
_cols, _n = {}, 0
for _name, _count in (("a_pre", KT), ("a_conv", 4 * 32), ("a_convb", 32), ("a_gate", OUT_K), ("a_post", KT),
                      ("kvn", KT), ("b_kv", 4), ("b_pre", KT), ("b_q", KT), ("b_o", KT), ("b_post", KT),
                      ("f_pre", 2 * KT), ("f_conv", 2 * 3 * 2 * FT), ("f_convb", 2 * 2 * FT), ("f_post", 2 * KT)):
    _cols[_name] = _n
    _n += _count
COL, N_COLS = _cols, _n


class Core:
    pass


class Steps:

    def __init__(self, eng, sem):
        self.eng, self.sem, self.base, self.n = eng, sem, 0, 0

    def done(self, ins):
        ins.then_inc(self.sem, 1)
        self.n += 1

    def wait(self):
        self.eng.wait_ge(self.sem, self.base + self.n)

    def link(self, ins):
        self.done(ins)
        self.wait()


@contextmanager
def looped(eng, lo, hi, *tallies):
    before = [(s, s.base + s.n, per) for s, per in tallies]
    with eng.Fori(lo, hi) as i:
        for s, b, per in before:
            s.base, s.n = b + (i - lo) * per, 0
        yield i
        for s, b, per in before:
            assert s.n == per, (s.n, per)
    for s, b, per in before:
        s.base, s.n = b + (hi - lo) * per, 0


def bcast(ap, shape):
    return ap.to_broadcast(shape)


def sp_program(k, sp):
    sp.dma_start(k.par[:, :], k.d_par).then_inc(k.par_loaded, 16)
    for c in range(KT):
        sp.dma_start(k.h[:, c, :], k.d_x[:, c, :]).then_inc(k.x_loaded[c], 16)
    for s in range(RING):
        sp.dma_start(k.raw[s][:, :], k.d_slabs[s * P:(s + 1) * P, :]).then_inc(k.raw_loaded[s], 16)
        if s == 0:
            sp.dma_start(k.wdt[:, :], k.d_wdt).then_inc(k.small_loaded, 16)
            sp.dma_start(k.hpar[:, :], k.d_hpar).then_inc(k.small_loaded, 16)
            for half in range(2):
                rows = slice(64 * half, 64 * half + 64)
                sp.dma_start(k.dskip[rows, :], bcast(k.d_dskip[half:half + 1, :], [64, 16])).then_inc(k.small_loaded, 16)
                sp.dma_start(k.nsink[rows, :], bcast(k.d_sinks[half:half + 1, :], [64, 8])).then_inc(k.small_loaded, 16)
    with sp.Fori(1, N_SLABS // RING) as r:
        for s in range(RING):
            row = sp.snap(r * (RING * P) + s * P)
            sp.wait_ge(k.lo_done, r * RING + (s + 1 - RING))
            sp.dma_start(k.raw[s][:, :], k.d_slabs[ds(row, P), :]).then_inc(k.raw_loaded[s], 16)
    for c in range(KT):
        sp.wait_ge(k.h_done, 3 * KT + c + 1)
        sp.dma_start(k.d_out[:, c, :], k.h[:, c, :]).then_inc(k.stored, 16)
    sp.wait_ge(k.stored, 16 * KT)


def pool_program(k, pool):
    pool.memset(k.ones[:, :], 1.0).then_inc(k.ones_set, 1)
    pool.wait_ge(k.ones_set, 1)
    pool.affine_select(out=k.ident[:, :], in_=k.ones[:, :], compare_op=ALU.is_equal, fill=0.0,
                       base=0, pattern=[[1, P]], channel_multiplier=-1).then_inc(k.consts_ready, 1)
    pool.affine_select(out=k.tri[:, :], in_=k.ones[:, :], compare_op=ALU.is_ge, fill=0.0,
                       base=0, pattern=[[1, P]], channel_multiplier=-1).then_inc(k.consts_ready, 1)

    def lows(first, end):
        def low(n, s):
            pool.wait_ge(k.hi_done, n + 1)
            pool.tensor_tensor(k.wlo[s][:, :], k.raw[s][:, :], k.whi[s][:, :], ALU.subtract).then_inc(k.lo_done, 1)

        turns = (end - first) // RING
        with pool.Fori(0, turns) as r:
            for j in range(RING):
                low(r * RING + (first + j), (first + j) % RING)
        for n in range(first + turns * RING, end):
            low(n, n % RING)

    def squares(norm):
        for m in range(KT):
            add_square(k, pool, m, norm)

    lows(0, UP[0] + RING)
    squares(2)
    lows(UP[0] + RING, KV0 + RING)
    squares(4)
    lows(KV0 + RING, UP[1] + RING)
    squares(6)
    lows(UP[1] + RING, N_SLABS)


def add_square(k, eng, m, norm):
    q = norm * KT + m
    eng.wait_ge(k.sq_done, q + 1)
    if q:
        eng.wait_ge(k.sq_added, q)
    if m == 0:
        if norm:
            eng.wait_ge(k.sums_ready, norm)
        eng.tensor_copy(k.acc[:, :], k.sq[q % 2][:, :]).then_inc(k.sq_added, 1)
    else:
        eng.tensor_tensor(k.acc[:, :], k.acc[:, :], k.sq[q % 2][:, :], ALU.add).then_inc(k.sq_added, 1)


def pe_program(k, pe):
    ps = k.ps

    def slab_a(n, bank, hi, lo, m0=True):
        s = n % RING if isinstance(n, int) else n[1]
        for c in range(KT):
            wh, wl = k.whi[s][:, c * P:(c + 1) * P], k.wlo[s][:, c * P:(c + 1) * P]
            pe.matmul(ps[:, bank, :], wh, hi[:, c, :], start=(c == 0), stop=False)
            pe.matmul(ps[:, bank, :], wh, lo[:, c, :], start=False, stop=False)
            last = pe.matmul(ps[:, bank, :], wl, hi[:, c, :], start=False, stop=(c == KT - 1))
        last.then_inc(k.slab_used, 1)

    def first_slabs_a(n, banks, hi, lo, parts_ready, base):
        for c in range(KT):
            pe.wait_ge(parts_ready, base + c + 1)
            for j, bank in enumerate(banks):
                s = (n + j) % RING
                if c == 0:
                    pe.wait_ge(k.lo_done, n + j + 1)
                wh, wl = k.whi[s][:, c * P:(c + 1) * P], k.wlo[s][:, c * P:(c + 1) * P]
                pe.matmul(ps[:, bank, :], wh, hi[:, c, :], start=(c == 0), stop=False)
                pe.matmul(ps[:, bank, :], wh, lo[:, c, :], start=False, stop=False)
                last = pe.matmul(ps[:, bank, :], wl, hi[:, c, :], start=False, stop=(c == KT - 1))
                if c == KT - 1:
                    last.then_inc(k.slab_used, 1)

    def three(m, s, hi_k, lo_k, start, stop):
        wh, wl = k.whi[s][:, m * P:(m + 1) * P], k.wlo[s][:, m * P:(m + 1) * P]
        pe.matmul(ps[:, m, :], wh, hi_k, start=start, stop=False)
        pe.matmul(ps[:, m, :], wh, lo_k, start=False, stop=False)
        return pe.matmul(ps[:, m, :], wl, hi_k, start=False, stop=stop)

    def slab_b(s, hi_k, lo_k, start=False, order=range(KT), bank_0=None):
        for m in order:
            if m == 0 and bank_0 is not None:
                pe.wait_ge(*bank_0)
            last = three(m, s, hi_k, lo_k, start, False)
        last.then_inc(k.slab_used, 1)

    def tail_b(slots, parts):
        for m in range(KT):
            for j, (s, (hi_k, lo_k)) in enumerate(zip(slots, parts)):
                last = three(m, s, hi_k, lo_k, False, j == 1)
                if m == KT - 1 and j == 0:
                    last.then_inc(k.slab_used, 1)
            last.then_inc(k.mix_ready if m < KT - 1 else k.slab_used, 1)

    def column_sums(norm):
        pe.wait_ge(k.sq_added, KT * (norm + 1))
        pe.matmul(ps[:, 6, :], k.ones[:, :], k.acc[:, :], start=True, stop=True).then_inc(k.sums_ready, 1)

    def ssd_1(g, p):
        pe.wait_ge(k.xbc_done, g * 4 + 4)
        if not isinstance(g, int) or g > 0:
            pe.wait_ge(k.gate_rstd_done, g)
            pe.wait_ge(k.y_done, g * 2)
        for c in range(NC):
            t = slice(c * SC, (c + 1) * SC)
            last = pe.matmul(ps[:, 3, t], k.bt[p][:, t], k.ct[p][:, t], start=True, stop=True)
        last.then_inc(k.cb_ready, 1)
        for c in range(NC):
            t = slice(c * SC, (c + 1) * SC)
            last = pe.transpose(ps[:, 7, t], k.bt[p][:, t], k.ident[:, :])
        last.then_inc(k.btok_ready, 1)
        for j in range(2):
            for c in range(NC):
                t = slice(c * SC, (c + 1) * SC)
                last = pe.transpose(ps[:, 5 + j, t], k.xt[p][:, j, t], k.ident[:, :])
            last.then_inc(k.xtok_ready, 1)

    def ssd_2(g, p):
        pe.wait_ge(k.btok_done, g + 1)
        pe.wait_ge(k.xtok_done, g * 4 + 4)
        pe.wait_ge(k.cbm_done, g + 1)
        for c in range(NC - 1):
            out = ps[:, 4, c * 256:(c + 1) * 256] if c < 2 else ps[:, 3, 0:256]
            last = pe.matmul(out, k.btok[:, c, :], k.xdd[:, c, :], start=True, stop=True)
        last.then_inc(k.state_ready, 1)

    def ssd_3(g, p):
        for hh in range(HG):
            if hh == 0:
                pe.wait_ge(k.m_done, g * 4 + 4)
            j, half = hh // 2, hh % 2
            for c in range(NC):
                t = slice(c * SC, (c + 1) * SC)
                last = pe.matmul(ps[64 * half:64 * half + 64, 5 + j, t], k.xdt[:, c, hh * 64:hh * 64 + 64],
                                 k.csb[:, hh, t], start=True, stop=True)
        last.then_inc(k.ydiag_ready, 1)

    def ssd_4(g, p):
        pe.wait_ge(k.state_done, g + 1)
        for j, bank in enumerate((7, 4)):
            for c in range(1, NC):
                t = slice(c * SC, (c + 1) * SC)
                last = pe.matmul(ps[:, bank, t], k.hst[:, c - 1, j * P:(j + 1) * P], k.ct[p][:, t],
                                 start=True, stop=True)
        last.then_inc(k.yoff_ready, 1)

    def ssd_5(g):
        pe.wait_ge(k.gate_acc_done, g + 1)
        pe.matmul(ps[:, 3, :], k.ones[:, :], k.gacc[:, :], start=True, stop=True).then_inc(k.gate_sums_ready, 1)

    def in_proj_group(G, p):
        g, q = G - 1, 1 - p
        base = G * GROUP_SLABS - 2
        for j in range(GROUP_SLABS if not (isinstance(G, int) and G == NG) else 2):
            pe.wait_ge(k.lo_done, base + (j + 1))
            if j < 3:
                pe.wait_ge(k.conv_done, G * 4 + (j - 2))
            elif j < 5:
                pe.wait_ge(k.z_done, G * 2 + (j - 4))
            else:
                pe.wait_ge(k.conv_done, G * 4 + 1)
            slab_a((0, (p * GROUP_SLABS - 2 + j) % RING), j % 3, k.hs_hi, k.hs_lo)
            if j == 0 and not (isinstance(G, int) and G == 1):
                ssd_5(g - 1)
            if j == 1:
                if isinstance(G, int) and G == 1:
                    token_columns()
                ssd_1(g, q)
            if j == 2:
                ssd_2(g, q)
            if j == 3:
                ssd_3(g, q)
            if j == 4:
                ssd_4(g, q)

    def token_columns():
        pe.wait_ge(k.dtw_done, 1)
        for c in range(NC):
            for i, src in enumerate((k.dt_, k.ncs, k.dtw)):
                last = pe.transpose(ps[:, 4, c * 96 + i * NH:c * 96 + (i + 1) * NH], src[:, c * SC:(c + 1) * SC], k.ident[0:NH, 0:NH])
        last.then_inc(k.tok_ready, 1)

    pe.wait_ge(k.ones_set, 1)
    pe.wait_ge(k.consts_ready, 2)
    column_sums(0)
    first_slabs_a(0, (2, 0, 1), k.hs_hi, k.hs_lo, k.lo_part_done, 0)
    pe.wait_ge(k.small_loaded, 16 * 6)
    for c in range(KT):
        last = pe.matmul(ps[0:NH, 3, :], k.wdt[:, c * NH:(c + 1) * NH], k.hn[:, c, :], start=(c == 0), stop=(c == KT - 1))
    last.then_inc(k.dt_ready, 1)
    pe.wait_ge(k.lo_done, 4)
    pe.wait_ge(k.conv_done, 1)
    slab_a((0, 3), 2, k.hs_hi, k.hs_lo)
    in_proj_group(1, 1)
    with pe.Fori(1, NG // 2) as i:
        in_proj_group(i * 2, 0)
        in_proj_group(i * 2 + 1, 1)
    in_proj_group(NG, 0)
    ssd_2(NG - 1, 1)
    ssd_3(NG - 1, 1)
    ssd_4(NG - 1, 1)
    ssd_5(NG - 1)

    pe.wait_ge(k.gate_rstd_done, NG)
    pe.wait_ge(k.y_done, 2 * NG)
    pe.wait_ge(k.z_done, 2 * NG)
    pe.wait_ge(k.conv_done, 4 * NG)

    def out_slab(kk, s, start=False):
        pe.wait_ge(k.lo_done, OUT0 + kk + 1)
        pe.wait_ge(k.yn_done, kk + 1)
        slab_b(s, k.yn_hi[s][:, :], k.yn_lo[s][:, :], start)

    out_slab(0, OUT0 % RING, True)
    out_slab(1, (OUT0 + 1) % RING)
    with pe.Fori(0, 3) as i:
        for j in range(RING):
            out_slab(i * RING + (2 + j), (OUT0 + 2 + j) % RING)
    pe.wait_ge(k.lo_done, OUT0 + OUT_K)
    pe.wait_ge(k.yn_done, OUT_K)
    sl = [(OUT0 + OUT_K - 2 + j) % RING for j in range(2)]
    tail_b(sl, [(k.yn_hi[s][:, :], k.yn_lo[s][:, :]) for s in sl])

    def boundary(t, hi, lo, n):
        pe.wait_ge(k.mix_read, KT * (t + 1))
        column_sums(1 + 2 * t)
        if n is None:
            return
        first_slabs_a(n, [(n + j) % 4 for j in range(3)], hi, lo, k.lo_part_done, k.lo_base[t])
        pe.wait_ge(k.rstd_done, 2 + 2 * t)
        column_sums(2 + 2 * t)

    def ffn(l):
        u0, d0 = UP[l], DOWN[l]
        pe.wait_ge(k.lo_done, u0 + 4)
        slab_a((0, (u0 + 3) % RING), (u0 + 3) % 4, k.hs_hi, k.hs_lo)
        with pe.Fori(1, FT // 2) as r:
            for j in range(4):
                pe.wait_ge(k.lo_done, r * 4 + (u0 + j + 1))
                pe.wait_ge(k.u_done, r * 4 + (l * 2 * FT + j - 3))
                slab_a((0, (u0 + j) % RING), (u0 + j) % 4, k.hs_hi, k.hs_lo)
        pe.wait_ge(k.rstd_done, 3 + 4 * l)

        def down_slab(kk, j, start=False):
            s = (d0 + j) % RING
            pe.wait_ge(k.lo_done, kk + (d0 + 1))
            pe.wait_ge(k.f_lo_done, kk + (l * FT + 1))
            if start:
                slab_b(s, k.f_hi[s][:, :], k.f_lo[s][:, :], start, (4, 5, 6, 7, 0, 1, 2, 3), (k.u_done, (l + 1) * 2 * FT))
            else:
                slab_b(s, k.f_hi[s][:, :], k.f_lo[s][:, :])

        for kk in range(RING):
            down_slab(kk, kk, kk == 0)
        with pe.Fori(1, 5) as r:
            for j in range(RING):
                down_slab(r * RING + j, j)
        pe.wait_ge(k.lo_done, d0 + FT)
        pe.wait_ge(k.f_lo_done, (l + 1) * FT)
        sl = [(d0 + FT - 2 + j) % RING for j in range(2)]
        tail_b(sl, [(k.f_hi[s][:, :], k.f_lo[s][:, :]) for s in sl])

    boundary(0, k.hs_hi, k.hs_lo, UP[0])
    ffn(0)
    boundary(1, k.hk_hi, k.hk_lo, KV0)

    pe.wait_ge(k.lo_done, KV0 + 4)
    slab_a(KV0 + 3, (KV0 + 3) % 4, k.hk_hi, k.hk_lo)

    def scores(a):
        kt, c = a // NCH, a % NCH
        if a >= 2:
            pe.wait_ge(k.exp_done, a - 1)
        for u in range(4):
            r = slice(64 * (u // 2), 64 * (u // 2) + 64)
            last = pe.matmul(ps[:, 2 + 2 * (a % 2) + u // 2, (u % 2) * P:(u % 2 + 1) * P],
                             k.qt[r, kt, c, (u % 2) * P:(u % 2 + 1) * P],
                             k.kp[r, kt, c * CH:c * CH + P], start=True, stop=True)
        last.then_inc(k.scores_ready, 1)

    def probs_t(a):
        pe.wait_ge(k.probs_done, a + 1)
        if a >= 1:
            pe.wait_ge(k.pt_done, a)
        for u in range(4):
            last = pe.transpose(ps[:, 6, u * P:(u + 1) * P], k.pr[a % 2][:, u, :], k.ident[:, :])
        last.then_inc(k.pt_ready, 1)

    def mix_values(a):
        kt, c = a // NCH, a % NCH
        pe.wait_ge(k.pt_done, a + 1)
        if a >= 1:
            pe.wait_ge(k.o_done, a)
        for half in range(2):
            last = pe.matmul(ps[64 * half:64 * half + 64, 7, 0:256],
                             k.vtok[:, c, kt, 64 * half:64 * half + 64],
                             k.pts[a % 2][:, 2 * half * P:(2 * half + 2) * P], start=True, stop=True)
        last.then_inc(k.o_ready, 1)

    def q_slab_half(n, bank, c0):
        s = n % RING
        for c in range(c0, c0 + KT // 2):
            wh, wl = k.whi[s][:, c * P:(c + 1) * P], k.wlo[s][:, c * P:(c + 1) * P]
            pe.matmul(ps[:, bank, :], wh, k.hs_hi[:, c, :], start=(c == 0), stop=False)
            pe.matmul(ps[:, bank, :], wh, k.hs_lo[:, c, :], start=False, stop=False)
            last = pe.matmul(ps[:, bank, :], wl, k.hs_hi[:, c, :], start=False, stop=(c == KT - 1))
        if c0:
            last.then_inc(k.slab_used, 1)

    def attend(h):
        if h == 0:
            pe.wait_ge(k.kqv_done, 8)
            pe.wait_ge(k.qkv_read, 8)
        if h == NCH:
            pe.wait_ge(k.kqv_done, 12)
        if h < 2 * NCH:
            scores(h)
        if 0 <= h - 2 < 2 * NCH:
            probs_t(h - 2)
        if h == 3:
            pe.wait_ge(k.vtok_done, 4)
        if 0 <= h - 3 < 2 * NCH:
            mix_values(h - 3)

    for i in range(KT):
        n = Q0 + i
        pe.wait_ge(k.lo_done, n + 1)
        if i == 0:
            pe.wait_ge(k.lo_part_done, k.lo_q_base + KT)
        pe.wait_ge(k.qkv_read, n - KV0 - (1 if i >= 2 else 3))
        q_slab_half(n, k.q_bank[i], 0)
        if i >= 4:
            attend(2 * (i - 4))
        q_slab_half(n, k.q_bank[i], KT // 2)
        if i >= 4:
            attend(2 * (i - 4) + 1)
        if i < 4:
            b = i
            if b == 0:
                pe.wait_ge(k.kqv_done, 4)
            else:
                pe.wait_ge(k.vtok_done, b)
            for w in range(2):
                c = 2 * b + w
                for kt in range(2):
                    last = pe.transpose(ps[:, 7, (w * 2 + kt) * P:(w * 2 + kt + 1) * P],
                                        k.vp[:, kt, c * CH:c * CH + P], k.ident[:, :])
            last.then_inc(k.vtok_ready, 1)
    for h in range(NCH, 2 * NCH + 3):
        attend(h)
    pe.wait_ge(k.o_done, 2 * NCH)
    for kk in range(KT - 2):
        pe.wait_ge(k.lo_done, O0 + kk + 1)
        slab_b((O0 + kk) % RING, k.o_hi[:, kk, :], k.o_lo[:, kk, :], kk == 0)
    pe.wait_ge(k.lo_done, O0 + KT)
    tail_b([(O0 + KT - 2 + j) % RING for j in range(2)],
           [(k.o_hi[:, KT - 2 + j, :], k.o_lo[:, KT - 2 + j, :]) for j in range(2)])
    boundary(2, k.hs_hi, k.hs_lo, UP[1])
    ffn(1)
    boundary(3, None, None, None)


def act_program(k, act):
    ps, par = k.ps, k.par

    def col(name, i):
        if isinstance(i, int):
            return par[:, COL[name] + i:COL[name] + i + 1]
        return par[:, ds(i + COL[name], 1)]

    def hi(n, s):
        if n >= N_SLABS:
            return
        if n >= RING:
            act.wait_ge(k.slab_used, n - (RING - 1))
        act.wait_ge(k.raw_loaded[s], 16 * (n // RING + 1))
        act.activation(k.whi[s][:, :], k.raw[s][:, :], ACT.Copy).then_inc(k.hi_done, 1)

    def hi_loop(n, s, lap):
        act.wait_ge(k.slab_used, n - (RING - 1))
        act.wait_ge(k.raw_loaded[s], lap * 16)
        act.activation(k.whi[s][:, :], k.raw[s][:, :], ACT.Copy).then_inc(k.hi_done, 1)

    squares = [0]

    def square(src, bias=None):
        q = squares[0]
        if q >= 2:
            act.wait_ge(k.sq_added, q - 1)
        kw = {} if bias is None else {"bias": bias}
        act.activation(k.sq[q % 2][:, :], src, ACT.Square, **kw).then_inc(k.sq_done, 1)
        squares[0] += 1

    lns = Steps(act, k.ln_done)

    def rstd(norm, out):
        act.wait_ge(k.sums_ready, norm + 1)
        if norm:
            act.wait_ge(k.rstd_done, norm)
        lns.link(act.activation(out, ps[:, 6, :], ACT.Ln, bias=k.eps[:, :], scale=1.0 / DM))
        act.activation(out, out, ACT.Exp, scale=-0.5).then_inc(k.rstd_done, 1)

    act.preload_act_table_set("natural_log_exp_and_others")
    act.wait_ge(k.eps_set, 1)
    for c in range(KT):
        act.wait_ge(k.x_loaded[c], 16)
        square(k.h[:, c, :])
    for s in range(RING):
        hi(s, s)
    rstd(0, k.rpre[:, :])
    for c in range(KT):
        act.wait_ge(k.hn_done, c + 1)
        act.activation(k.hs_hi[:, c, :], k.hn[:, c, :], ACT.Copy).then_inc(k.hi_part_done, 1)

    own = Steps(act, k.act_own)

    def dt_steps():
        act.preload_act_table_set("natural_log_exp_and_others")
        act.wait_ge(k.small_loaded, 16 * 6)
        act.wait_ge(k.dt_ready, 1)
        own.link(act.activation(k.dtx[:, :], ps[0:NH, 3, :], ACT.Identity, bias=k.hpar[:, 0:1]))
        own.link(act.activation(k.dta[:, :], k.dtx[:, :], ACT.Abs))
        act.activation(k.dte[:, :], k.dta[:, :], ACT.Exp, scale=-1.0).then_inc(k.dt_exp, 1)
        act.activation(k.aneg[:, :], k.hpar[:, 1:2], ACT.Exp).then_inc(k.dt_exp, 1)
        act.wait_ge(k.dt_u, 1)
        own.link(act.activation(k.dtl[:, :], k.dtu[:, :], ACT.Ln))
        act.activation(k.dtr[:, :], k.dtl[:, :], ACT.Exp, scale=-1.0).then_inc(k.dt_exp, 1)
        hi(3 + RING, 3)
        tap0(0, 3)
        act.wait_ge(k.cs_done, 1)
        for c in range(NC):
            t = slice(c * SC, (c + 1) * SC)
            act.activation(k.dtw[:, t], k.cs[:, t], ACT.Exp, scale=-1.0, bias=k.cs[:, (c + 1) * SC - 1:(c + 1) * SC]).then_inc(k.dt_exp, 1)
        act.dma_start(k.d_cs, k.cs[:, :]).then_inc(k.cs_stored, 16)
        act.wait_ge(k.cs_stored, 16)
        load_cs(0)

    def load_cs(g):
        rows = k.d_cs[ds(g * HG, HG), :] if not isinstance(g, int) else k.d_cs[g * HG:(g + 1) * HG, :]
        act.dma_start(k.csb[:, :, :], bcast(rows.rearrange("(o h) t -> o h t", o=1), [P, HG, SEQ])).then_inc(k.cs_loaded, 16)

    def tap0(G, i):
        tile = (G + 16, G + 24, G * 2, G * 2 + 1)[i]
        if not (isinstance(G, int) and G == 0 and i < 2):
            act.wait_ge(k.xbc_done, G * 4 + (i - 1))
        act.activation(k.cacc[i % 2][:, :], ps[:, CONV_BANK[i], :], ACT.Identity, bias=col("a_convb", tile),
                       scale=col("a_conv", 3 * 32 + tile)).then_inc(k.tap0_done, 1)

    def conv_silu(G, p, i):
        dst = (k.bt[p][:, :], k.ct[p][:, :], k.xt[p][:, 0, :], k.xt[p][:, 1, :])[i]
        act.wait_ge(k.conv_done, G * 4 + (i + 1))
        if i == 0 and (not isinstance(G, int) or G >= 2):
            act.wait_ge(k.y_done, G * 2 - 2)
        act.activation(dst, k.cacc[i % 2][:, :], ACT.Silu).then_inc(k.xbc_done, 1)

    def in_group(G, p, i=None):
        static = isinstance(G, int)
        g = G - 1
        end = static and G == NG

        def step(j):
            s = (p * GROUP_SLABS - 2 + j) % RING
            if static:
                hi(G * GROUP_SLABS - 2 + j + RING, s)
            else:
                hi_loop(G * GROUP_SLABS + (j + RING - 2), s, i * 3 + ((p * GROUP_SLABS - 2 + j + RING) // RING + 1))

        act.preload_act_table_set("natural_log_exp_and_others")
        step(0)
        if not (static and g == 0):
            gate_rstd(g - 1)
        exps(g)
        step(1)
        b_tokens(g)
        for j in range(2):
            if j == 0 and not (static and g == 0):
                act.wait_ge(k.y_done, g * 2)
            act.activation(k.sz[:, j, :], ps[:, j, :], ACT.Silu).then_inc(k.z_done, 1)
        if not end:
            step(2)
            tap0(G, 0)
            step(3)
            tap0(G, 1)
            conv_silu(G, p, 0)
            conv_silu(G, p, 1)
            act.wait_ge(k.ydiag_ready, g + 1)
            load_cs(g + 1)
            step(4)
            tap0(G, 2)
            y_squares(g)
            conv_silu(G, p, 2)
            step(5)
            tap0(G, 3)
            conv_silu(G, p, 3)

    def exps(g):
        act.wait_ge(k.cs_loaded, g * 16 + 16)
        if not isinstance(g, int) or g >= 1:
            act.wait_ge(k.y_done, g * 2)
        for half in range(2):
            r = slice(64 * half, 64 * half + 64)
            src = k.csb[r, :, :].rearrange("p (j e) t -> p e j t", e=2)[:, half, :, SC:SEQ]
            act.activation(k.e2[r, :, :], src, ACT.Exp).then_inc(k.e_done, 1)
        act.activation(k.dec[:, :, :], k.csb[:, :, :].rearrange("p h (c t) -> p h c t", t=SC)[:, :, :, SC - 1],
                       ACT.Exp).then_inc(k.e_done, 1)
        for hh in range(HG):
            act.wait_ge(k.seg_done, g * HG + (hh + 1))
            act.activation(k.csb[:, hh, :], k.csb[:, hh, :], ACT.Exp).then_inc(k.l_done, 1)

    def b_tokens(g):
        act.wait_ge(k.btok_ready, g + 1)
        if not isinstance(g, int) or g >= 1:
            act.wait_ge(k.state_ready, g)
        act.activation(k.btok[:, :, :], ps[:, 7, :].rearrange("p (c n) -> p c n", c=NC), ACT.Copy).then_inc(k.btok_done, 1)

    def gate_rstd(g):
        act.wait_ge(k.gate_sums_ready, g + 1)
        if not isinstance(g, int) or g >= 1:
            act.wait_ge(k.yn_scaled, g * 2)
        act.activation(k.grstd[:, :], ps[:, 3, :], ACT.Ln, bias=k.eps[:, :], scale=1.0 / (DI // NG)).then_inc(k.gln_done, 1)
        act.wait_ge(k.gln_done, g + 1)
        act.activation(k.grstd[:, :], k.grstd[:, :], ACT.Exp, scale=-0.5).then_inc(k.gate_rstd_done, 1)

    def y_squares(g):
        for j in range(2):
            act.wait_ge(k.y_done, g * 2 + (j + 1))
            if j == 0 and (not isinstance(g, int) or g >= 1):
                act.wait_ge(k.gate_acc_done, g)
            act.activation(k.gsq[j][:, :], k.yg[:, g * 2 + j, :], ACT.Square).then_inc(k.gsq_done, 1)

    hi(0 + RING, 0)
    tap0(0, 0)
    hi(1 + RING, 1)
    tap0(0, 1)
    hi(2 + RING, 2)
    conv_silu(0, 0, 0)
    tap0(0, 2)
    conv_silu(0, 0, 1)
    conv_silu(0, 0, 2)
    dt_steps()
    conv_silu(0, 0, 3)
    in_group(1, 1)
    with act.Fori(1, NG // 2) as i:
        in_group(i * 2, 0, i)
        in_group(i * 2 + 1, 1, i)
    in_group(NG, 0)
    act.preload_act_table_set("natural_log_exp_and_others")

    def yn_hi(kk):
        act.wait_ge(k.yn_scaled, kk + 1)
        if kk >= RING:
            act.wait_ge(k.slab_used, kk + (OUT0 - RING + 1))
        act.activation(k.yn_hi[kk % RING][:, :], k.yg[:, kk, :], ACT.Copy).then_inc(k.yn_hi_done, 1)

    y_squares(NG - 1)
    yn_hi(0)
    yn_hi(1)
    gate_rstd(NG - 1)
    yn_hi(2)
    yn_hi(3)
    for kk in range(2):
        hi(OUT0 + kk + RING, (OUT0 + kk) % RING)
        yn_hi(kk + RING)
    with act.Fori(0, 2) as i:
        for j in range(RING):
            s = (OUT0 + 2 + j) % RING
            hi_loop(i * RING + (OUT0 + 2 + j + RING), s, i + ((OUT0 + 2 + j + RING) // RING + 1))
            act.activation(k.yn_hi[s][:, :], k.yg[:, i * RING + (2 + j + RING), :], ACT.Copy).then_inc(k.yn_hi_done, 1)
    for kk in range(10, 14):
        hi(OUT0 + kk + RING, (OUT0 + kk) % RING)
        if kk + RING < OUT_K:
            yn_hi(kk + RING)

    def boundary(t, w_post, off, nxt, bias=False):
        for m in range(KT):
            if m < KT - 1:
                act.wait_ge(k.mix_ready, (KT - 1) * t + m + 1)
            else:
                act.wait_ge(k.slab_used, (UP[0], KV0, UP[1], N_SLABS)[t])
            b = col("b_o", m) if bias else None
            square(ps[:, m, :], b)
            kw = {"bias": k.bo_post[:, m:m + 1]} if bias else {}
            act.activation(k.mix[:, m, :], ps[:, m, :], ACT.Identity if bias else ACT.Copy,
                           scale=col(w_post, off + m), **kw).then_inc(k.mix_read, 1)
        if nxt:
            hi(nxt + 2, (nxt + 2) % RING)
        rstd(1 + 2 * t, k.rpost[:, :])
        if nxt:
            hi(nxt + 3, (nxt + 3) % RING)

    def next_parts(t, name, off, dst, nxt):
        for c in range(KT):
            act.wait_ge(k.h_done, KT * t + c + 1)
            act.activation(dst[:, c, :], k.h[:, c, :], ACT.Copy, scale=col(name, off + c)).then_inc(k.hi_part_done, 1)
            square(k.h[:, c, :])
            if t == 1:
                act.activation(k.hs_hi[:, c, :], k.h[:, c, :], ACT.Copy, scale=col("b_pre", c)).then_inc(k.hi_part_done, 1)
        hi(nxt + RING, nxt % RING)
        rstd(2 + 2 * t, k.rpre[:, :])

    def ffn(l):
        u0, d0, i0 = UP[l], DOWN[l], l * FT
        def pair(p, q, r=None):
            for v in range(2):
                s = (u0 + 2 * q + v) % RING
                if r is not None:
                    hi_loop(p * 2 + (u0 + v + RING), s, r + ((u0 + 2 * q + v + RING) // RING + 1))
                elif p or v:
                    hi(u0 + 2 * p + v + RING, s)
                act.wait_ge(k.u_done, p * 2 + (2 * i0 + v + 1))
                tile = p + (v * FT)
                if v == 0 and not (isinstance(p, int) and i0 + p < 2):
                    act.wait_ge(k.f_prod_done, p + (i0 - 1))
                act.activation(k.cv[q][v][:, :], k.u[q][v][:, :], ACT.Identity,
                               bias=col("f_convb", tile + l * 2 * FT),
                               scale=col("f_conv", tile + (l * 3 + 2) * 2 * FT)).then_inc(k.ftap0_done, 1)
            act.wait_ge(k.fconv_done, p * 2 + (2 * i0 + 1))
            act.activation(k.cv[q][0][:, :], k.cv[q][0][:, :], ACT.Silu).then_inc(k.fsilu_done, 1)

        def f_part(kk):
            act.wait_ge(k.f_prod_done, i0 + kk + 1)
            if kk >= RING:
                act.wait_ge(k.slab_used, d0 + kk - RING + 1)
            act.activation(k.f_hi[(d0 + kk) % RING][:, :], k.f[:, kk, :], ACT.Copy).then_inc(k.f_hi_done, 1)

        pair(0, 0)
        pair(1, 1)
        f_part(0)
        f_part(1)
        with act.Fori(1, FT // 2) as r:
            pair(r * 2, 0, r)
            pair(r * 2 + 1, 1, r)
        act.preload_act_table_set("natural_log_exp_and_others")
        f_part(2)
        f_part(3)
        for kk in range(RING):
            hi(d0 + kk + RING, (d0 + kk) % RING)
            f_part(kk + RING)
        with act.Fori(1, 4) as r:
            for j in range(RING):
                s = (d0 + j) % RING
                hi_loop(r * RING + (d0 + j + RING), s, r + ((d0 + j + RING) // RING + 1))
                act.activation(k.f_hi[s][:, :], k.f[:, r * RING + (j + RING), :], ACT.Copy).then_inc(k.f_hi_done, 1)
        for kk in range(FT - 6, FT - 2):
            hi(d0 + kk + RING, (d0 + kk) % RING)
            if kk + RING < FT:
                f_part(kk + RING)

    boundary(0, "a_post", 0, UP[0])
    next_parts(0, "f_pre", 0, k.hs_hi, UP[0])
    ffn(0)
    boundary(1, "f_post", 0, KV0)
    next_parts(1, "kvn", 0, k.hk_hi, KV0)
    def kqv(i):
        if i:
            hi(KV0 + i + RING, (KV0 + i) % RING)
        act.wait_ge(k.qkv_read, i + 1)
        src = k.qs[i % 2][:, :]
        if i < 4:
            dst = (k.kp if i < 2 else k.vp)[:, i % 2, CH:CH + SEQ]
            b = col("b_kv", i)
        else:
            dst = k.qt[:, (i - 4) // 4, :, ((i - 4) % 4) * CH:((i - 4) % 4 + 1) * CH]
            src = src.rearrange("p (c t) -> p c t", t=CH)
            b = col("b_q", i - 4)
        act.activation(dst, src, ACT.Identity, bias=b).then_inc(k.kqv_done, 1)

    def values_tokens(b):
        act.wait_ge(k.vtok_ready, b + 1)
        act.activation(k.vtok[:, 2 * b:2 * b + 2, :, :],
                       ps[:, 7, :].rearrange("p (w t d) -> p w t d", w=2, t=2), ACT.Copy).then_inc(k.vtok_done, 1)

    def attend(h):
        if h < 2 * NCH:
            b, lo_key = h % 2, CH if h % NCH == 0 else 0
            act.wait_ge(k.nmax_done, h + 1)
            if h >= 2:
                act.wait_ge(k.pt_ready, h - 1)
            for u in range(4):
                act.activation(k.pr[b][:, u, lo_key:P],
                               ps[:, 2 + 2 * b + u // 2, (u % 2) * P + lo_key:(u % 2 + 1) * P], ACT.Exp,
                               bias=k.nmax[b][:, u:u + 1], scale=CH ** -0.5, accum_out=k.psum_[b][:, u:u + 1])
            act.activation(k.esink[b][:, :], k.dsink[b][:, :], ACT.Exp).then_inc(k.exp_done, 1)
        a = h - 2
        if 0 <= a < 2 * NCH:
            act.wait_ge(k.pt_ready, a + 1)
            if a >= 2:
                act.wait_ge(k.o_ready, a - 1)
            act.activation(k.pts[a % 2][:, :], ps[:, 6, :], ACT.Copy).then_inc(k.pt_done, 1)
        a = h - 3
        if 0 <= a < 2 * NCH:
            kt, c = a // NCH, a % NCH
            act.wait_ge(k.o_ready, a + 1)
            act.activation(k.o_hi[:, kt * 4:kt * 4 + 4, c * CH:(c + 1) * CH],
                           ps[:, 7, 0:256].rearrange("p (t q) -> p t q", t=4), ACT.Copy).then_inc(k.o_hi_done, 1)

    for i in range(8):
        kqv(i)
        if i >= 4:
            values_tokens(i - 4)
    for i in range(8, 12):
        attend(2 * (i - 8))
        kqv(i)
        attend(2 * (i - 8) + 1)
    for h in range(NCH, 2 * NCH + 3):
        attend(h)
    for kk in range(KT - 2):
        hi(O0 + kk + RING, (O0 + kk) % RING)
    act.wait_ge(k.misc, 1)
    boundary(2, "b_post", 0, UP[1], bias=True)
    next_parts(2, "f_pre", KT, k.hs_hi, UP[1])
    ffn(1)
    boundary(3, "f_post", KT, None)


def dve_program(k, dve):
    ps, par = k.ps, k.par
    own = Steps(dve, k.dve_own)

    def col(name, i):
        if isinstance(i, int):
            return par[:, COL[name] + i:COL[name] + i + 1]
        return par[:, ds(i + COL[name], 1)]

    dve.memset(k.eps[:, :], EPS).then_inc(k.eps_set, 1)
    for c in range(KT):
        add_square(k, dve, c, 0)
    dve.wait_ge(k.par_loaded, 16)
    dve.wait_ge(k.rstd_done, 1)
    for c in range(KT + 1):
        if c < KT:
            dve.scalar_tensor_tensor(out=k.hn[:, c, :], in0=k.h[:, c, :], scalar=col("a_pre", c), in1=k.rpre[:, :],
                                     op0=ALU.mult, op1=ALU.mult).then_inc(k.hn_done, 1)
        if c:
            dve.wait_ge(k.hi_part_done, c)
            dve.tensor_tensor(k.hs_lo[:, c - 1, :], k.hn[:, c - 1, :], k.hs_hi[:, c - 1, :], ALU.subtract).then_inc(k.lo_part_done, 1)

    def conv(G, i):
        tile = (G + 16, G + 24, G * 2, G * 2 + 1)[i]
        acc = k.cacc[i % 2]
        dve.wait_ge(k.tap0_done, G * 4 + (i + 1))
        for s in (1, 2, 3):
            ins = dve.scalar_tensor_tensor(out=acc[:, s:SEQ], in0=ps[:, CONV_BANK[i], 0:SEQ - s],
                                           scalar=col("a_conv", (3 - s) * 32 + tile), in1=acc[:, s:SEQ],
                                           op0=ALU.mult, op1=ALU.add)
            if s < 3:
                own.link(ins)
            else:
                ins.then_inc(k.conv_done, 1)

    def dt_steps():
        dve.wait_ge(k.dt_exp, 1)
        dve.tensor_scalar(k.dtu[:, :], k.dte[:, :], 1.0, None, ALU.add).then_inc(k.dt_u, 1)
        dve.wait_ge(k.dt_u, 1)
        own.link(dve.tensor_scalar(k.dta[:, :], k.dtu[:, :], -1.0, None, ALU.add))
        own.link(dve.tensor_tensor(k.dte[:, :], k.dte[:, :], k.dta[:, :], ALU.subtract))
        dve.wait_ge(k.dt_exp, 3)
        own.link(dve.tensor_tensor(k.dte[:, :], k.dte[:, :], k.dtr[:, :], ALU.mult))
        own.link(dve.tensor_tensor(k.dte[:, :], k.dte[:, :], k.dtl[:, :], ALU.add))
        own.link(dve.scalar_tensor_tensor(out=k.dt_[:, :], in0=k.dtx[:, :], scalar=0.0, in1=k.dte[:, :], op0=ALU.max, op1=ALU.add))
        own.link(dve.tensor_scalar(k.dta[:, :], k.dt_[:, :], k.aneg[:, :], -1.0, ALU.mult, ALU.mult))
        for c in range(NC):
            t = slice(c * SC, (c + 1) * SC)
            own.done(dve.tensor_tensor_scan(out=k.cs[:, t], data0=k.ones[0:NH, :], data1=k.dta[:, t], initial=0.0,
                                            op0=ALU.mult, op1=ALU.add))
        own.wait()
        dve.tensor_scalar(k.ncs[:, :], k.cs[:, :], -1.0, None, ALU.mult).then_inc(k.cs_done, 1)
        conv(0, 3)
        dve.wait_ge(k.dt_exp, 7)
        dve.wait_ge(k.cs_done, 1)
        dve.tensor_tensor(k.dtw[:, :], k.dtw[:, :], k.dt_[:, :], ALU.mult).then_inc(k.dtw_done, 1)
        dve.wait_ge(k.tok_ready, 1)
        dve.tensor_copy(k.tok[:, :], ps[:, 4, 0:NC * 96]).then_inc(k.tok_done, 1)
        dve.wait_ge(k.tok_done, 1)
        dve.wait_ge(k.small_loaded, 16 * 6)
        dve.wait_ge(k.cs_stored, 16)

    tokv = k.tok[:, :].rearrange("p (c i h) -> p c i h", c=NC, i=3)

    def group_columns(g):
        if not isinstance(g, int) or g >= 1:
            dve.wait_ge(k.l_done, g * 4)
            dve.wait_ge(k.xtok_done, g * 4)
        src = tokv[:, :, :, ds(g * HG, HG)] if not isinstance(g, int) else tokv[:, :, :, g * HG:(g + 1) * HG]
        dve.tensor_scalar(k.tokg[:, :, :, :], src, 1.0, None, ALU.mult).then_inc(k.tokg_done, 1)
        dve.wait_ge(k.tokg_done, g + 1)

    def segments(g):
        dve.wait_ge(k.cs_loaded, g * 16 + 16)
        dve.wait_ge(k.e_done, g * 3 + 3)
        for hh in range(HG):
            for c in range(NC):
                t = slice(c * SC, (c + 1) * SC)
                last = dve.tensor_scalar(k.csb[:, hh, t], k.csb[:, hh, t], k.tokg[:, c, 1, hh:hh + 1], 0.0, ALU.add, ALU.min)
            last.then_inc(k.seg_done, 1)

    def ssd_1(g):
        dve.wait_ge(k.cb_ready, g + 1)
        if not isinstance(g, int) or g >= 1:
            dve.wait_ge(k.m_done, g * 4)
        dve.tensor_tensor(k.cbm[:, :].rearrange("p (c l) -> p c l", c=NC), ps[:, 3, :].rearrange("p (c l) -> p c l", c=NC),
                          bcast(k.tri[:, :].rearrange("p (o l) -> p o l", o=1), [P, NC, SC]), ALU.mult).then_inc(k.cbm_done, 1)
        if not isinstance(g, int) or g >= 1:
            dve.wait_ge(k.ydiag_ready, g)
        for j in range(2):
            dve.wait_ge(k.xtok_ready, g * 2 + (j + 1))
            for dst, i in ((k.xdt, 0), (k.xdd, 2)):
                w = k.tokg[:, :, i, 2 * j:2 * j + 2].rearrange("p c (h o) -> p c h o", o=1)
                dve.tensor_tensor(dst[:, :, j * P:(j + 1) * P].rearrange("p c (h d) -> p c h d", h=2),
                                  ps[:, 5 + j, :].rearrange("p (c h d) -> p c h d", c=NC, h=2),
                                  bcast(w, [P, NC, 2, 64]), ALU.mult).then_inc(k.xtok_done, 1)

    def ssd_2(g):
        dve.wait_ge(k.cbm_done, g + 1)
        for hh in range(HG):
            dve.wait_ge(k.l_done, g * 4 + (hh + 1))
            dve.tensor_tensor(k.csb[:, hh, :], k.csb[:, hh, :], k.cbm[:, :], ALU.mult).then_inc(k.m_done, 1)

    def ssd_3(g):
        dve.wait_ge(k.state_ready, g + 1)
        dve.wait_ge(k.e_done, g * 3 + 3)
        if not isinstance(g, int) or g >= 1:
            dve.wait_ge(k.yoff_ready, g)
        own.link(dve.tensor_scalar(k.hst[:, 0, :], ps[:, 4, 0:256], 1.0, None, ALU.mult))
        for c in (1, 2):
            w = bcast(k.dec[:, :, c:c + 1], [P, HG, 64])
            own.link(dve.tensor_tensor(k.htmp[:, :].rearrange("p (h d) -> p h d", h=HG),
                                       k.hst[:, c - 1, :].rearrange("p (h d) -> p h d", h=HG), w, ALU.mult))
            src = ps[:, 4, 256:512] if c == 1 else ps[:, 3, 0:256]
            ins = dve.tensor_tensor(k.hst[:, c, :], k.htmp[:, :], src, ALU.add)
            if c == 1:
                own.link(ins)
            else:
                ins.then_inc(k.state_done, 1)

    def ssd_4(g, q):
        dve.wait_ge(k.ydiag_ready, g + 1)
        if not isinstance(g, int) or g >= 1:
            dve.wait_ge(k.y_done, g * 2)
        for j in range(2):
            tile = g * 2 + j
            dcol = k.dskip[:, tile:tile + 1] if isinstance(g, int) else k.dskip[:, ds(tile, 1)]
            own.link(dve.scalar_tensor_tensor(out=k.yt[j][:, :], in0=k.xt[q][:, j, :], scalar=dcol, in1=ps[:, 5 + j, :],
                                              op0=ALU.mult, op1=ALU.add))
            if j == 0:
                dve.wait_ge(k.yoff_ready, g + 1)
            own.link(dve.tensor_tensor(k.yo[:, :], ps[:, (7, 4)[j], SC:SEQ], k.e2[:, j, :], ALU.mult))
            own.link(dve.tensor_tensor(k.yt[j][:, SC:SEQ], k.yt[j][:, SC:SEQ], k.yo[:, :], ALU.add))
            if j == 0:
                dve.wait_ge(k.z_done, g * 2 + 2)
            dve.tensor_tensor(k.yg[:, tile, :], k.yt[j][:, :], k.sz[:, j, :], ALU.mult).then_inc(k.y_done, 1)

    def ssd_5(g):
        dve.wait_ge(k.gsq_done, g * 2 + 2)
        if not isinstance(g, int) or g >= 1:
            dve.wait_ge(k.gate_sums_ready, g)
        dve.tensor_tensor(k.gacc[:, :], k.gsq[0][:, :], k.gsq[1][:, :], ALU.add).then_inc(k.gate_acc_done, 1)

    def norm_y(g):
        dve.wait_ge(k.gate_rstd_done, g + 1)
        for j in range(2):
            tile = g * 2 + j
            dve.scalar_tensor_tensor(out=k.yg[:, tile, :], in0=k.yg[:, tile, :], scalar=col("a_gate", tile),
                                     in1=k.grstd[:, :], op0=ALU.mult, op1=ALU.mult).then_inc(k.yn_scaled, 1)

    def in_group(G, p):
        g, q = G - 1, 1 - p
        end = isinstance(G, int) and G == NG
        group_columns(g)
        segments(g)
        if not (isinstance(G, int) and G == 1):
            norm_y(g - 1)
        ssd_1(g)
        ssd_2(g)
        if not end:
            conv(G, 0)
        ssd_3(g)
        if not end:
            conv(G, 1)
        ssd_4(g, q)
        if not end:
            conv(G, 2)
        ssd_5(g)
        if not end:
            conv(G, 3)

    for i in range(3):
        conv(0, i)
    dt_steps()
    in_group(1, 1)
    with looped(dve, 1, NG // 2, (own, 2 * (4 * 2 + 4 + 6))) as i:
        in_group(i * 2, 0)
        in_group(i * 2 + 1, 1)
    in_group(NG, 0)

    def yn_lo(kk):
        s = (OUT0 + kk) % RING
        dve.wait_ge(k.yn_hi_done, kk + 1)
        dve.wait_ge(k.yn_scaled, kk + 1)
        dve.tensor_tensor(k.yn_lo[s][:, :], k.yg[:, kk, :], k.yn_hi[s][:, :], ALU.subtract).then_inc(k.yn_done, 1)

    yn_lo(0)
    yn_lo(1)
    norm_y(NG - 1)
    for kk in range(2, OUT_K):
        yn_lo(kk)

    def post(t):
        for m in range(KT):
            add_square(k, dve, m, 1 + 2 * t)
        dve.wait_ge(k.rstd_done, 2 + 2 * t)

    def update(t, c):
        if c == 0:
            dve.wait_ge(k.mix_read, KT * (t + 1))
        own.link(dve.tensor_tensor(k.mix[:, c, :], k.mix[:, c, :], k.rpost[:, :], ALU.mult))
        dve.tensor_tensor(k.h[:, c, :], k.h[:, c, :], k.mix[:, c, :], ALU.add).then_inc(k.h_done, 1)

    def low(t, c, name, off, hi, lo, part):
        dve.wait_ge(k.h_done, KT * t + c + 1)
        dve.wait_ge(k.hi_part_done, part)
        dve.scalar_tensor_tensor(out=lo[:, c, :], in0=k.h[:, c, :], scalar=col(name, off + c), in1=hi[:, c, :],
                                 op0=ALU.mult, op1=ALU.subtract).then_inc(k.lo_part_done, 1)

    def boundary(t, name, off, hi, lo):
        post(t)
        if name is None:
            for c in range(KT):
                update(t, c)
            return
        update(t, 0)
        for c in range(KT):
            if c + 1 < KT:
                update(t, c + 1)
            low(t, c, name, off, hi, lo, k.lo_base[t] + (2 * c + 1 if t == 1 else c + 1))

    def ffn(l):
        u0, d0, i0 = UP[l], DOWN[l], l * FT
        dve.wait_ge(k.rstd_done, k.pre_count[l])

        def pair(p, q):
            for v in range(2):
                u, cv = k.u[q][v], k.cv[q][v]
                dve.wait_ge(k.slab_used, p * 2 + (u0 + v + 1))
                if not (isinstance(p, int) and i0 + p < 2) and v == 0:
                    dve.wait_ge(k.f_prod_done, p + (i0 - 1))
                dve.tensor_tensor(u[:, :], ps[:, (u0 + 2 * q + v) % 4, :], k.rpre[:, :], ALU.mult).then_inc(k.u_done, 1)
                dve.wait_ge(k.u_done, p * 2 + (2 * i0 + v + 1))
                dve.wait_ge(k.ftap0_done, p * 2 + (2 * i0 + v + 1))
                for s in (1, 2):
                    w = col("f_conv", p + (v * FT + (l * 3 + 2 - s) * 2 * FT))
                    ins = dve.scalar_tensor_tensor(out=cv[:, s:SEQ], in0=u[:, 0:SEQ - s], scalar=w, in1=cv[:, s:SEQ],
                                                   op0=ALU.mult, op1=ALU.add)
                    if s == 1:
                        own.link(ins)
                    else:
                        ins.then_inc(k.fconv_done, 1)
            dve.wait_ge(k.fconv_done, p * 2 + (2 * i0 + 2))
            dve.wait_ge(k.fsilu_done, p + (i0 + 1))
            dve.tensor_tensor(k.f[:, p, :], k.cv[q][0][:, :], k.cv[q][1][:, :], ALU.mult).then_inc(k.f_prod_done, 1)

        def f_part(kk, j):
            s = (d0 + j) % RING
            dve.wait_ge(k.f_hi_done, kk + (i0 + 1))
            dve.tensor_tensor(k.f_lo[s][:, :], k.f[:, kk, :], k.f_hi[s][:, :], ALU.subtract).then_inc(k.f_lo_done, 1)

        pair(0, 0)
        pair(1, 1)
        f_part(0, 0)
        f_part(1, 1)
        with looped(dve, 1, FT // 2, (own, 4)) as r:
            pair(r * 2, 0)
            pair(r * 2 + 1, 1)
        f_part(2, 2)
        f_part(3, 3)
        with dve.Fori(1, 5) as r:
            for j in range(RING):
                f_part(r * RING + j, j)
        for kk in (FT - 2, FT - 1):
            f_part(kk, kk)

    boundary(0, "f_pre", 0, k.hs_hi, k.hs_lo)
    ffn(0)
    dve.tensor_tensor(k.bo_post[:, :], par[:, COL["b_o"]:COL["b_o"] + KT], par[:, COL["b_post"]:COL["b_post"] + KT], ALU.mult).then_inc(k.misc, 1)
    dve.wait_ge(k.small_loaded, 16 * 6)
    dve.tensor_scalar(k.nsink[:, :], k.nsink[:, :], -1.0, None, ALU.mult).then_inc(k.misc, 1)
    boundary(1, "kvn", 0, k.hk_hi, k.hk_lo)
    for c in range(KT):
        low(1, c, "b_pre", 0, k.hs_hi, k.hs_lo, k.lo_base[1] + 2 * c + 2)
    dve.memset(k.kp[:, :, 0:CH], 0.0).then_inc(k.pads_set, 1)
    dve.memset(k.vp[:, :, 0:CH], 0.0).then_inc(k.pads_set, 1)
    dve.memset(k.pr[0][:, :, 0:CH], 0.0).then_inc(k.pads_set, 1)
    dve.wait_ge(k.rstd_done, 5)

    def scaled(i):
        bank = (KV0 + i) % 4 if i < 4 else k.q_bank[i - 4]
        dve.wait_ge(k.slab_used, KV0 + i + 1)
        if i >= 2:
            dve.wait_ge(k.kqv_done, i - 1)
        dve.tensor_tensor(k.qs[i % 2][:, :], ps[:, bank, :], k.rpre[:, :], ALU.mult).then_inc(k.qkv_read, 1)

    def row_max(a):
        kt, c = a // NCH, a % NCH
        lo_key = CH if c == 0 else 0
        b = a % 2
        dve.wait_ge(k.scores_ready, a + 1)
        if a >= 2:
            dve.wait_ge(k.exp_done, a - 1)
        src = ps[:, 2 + 2 * b:4 + 2 * b, 0:2 * P].rearrange("p g (u t) -> p g u t", u=2)[:, :, :, lo_key:P]
        own.link(dve.tensor_reduce(out=k.rmax[b][:, :].rearrange("p (g u) -> p g u", g=2), in_=src,
                                   axis=AX_X, op=ALU.max))
        sink = k.nsink[:, kt * 4:kt * 4 + 4]
        own.link(dve.scalar_tensor_tensor(out=k.nmax[b][:, :], in0=k.rmax[b][:, :], scalar=-(CH ** -0.5), in1=sink,
                                          op0=ALU.mult, op1=ALU.min))
        dve.tensor_tensor(k.dsink[b][:, :], k.nmax[b][:, :], sink, ALU.subtract).then_inc(k.nmax_done, 1)

    def low_o(a):
        kt, c = a // NCH, a % NCH
        dve.wait_ge(k.o_hi_done, a + 1)
        dst = slice(c * CH, (c + 1) * CH)
        dve.tensor_tensor(k.o_lo[:, kt * 4:kt * 4 + 4, dst], ps[:, 7, 0:256].rearrange("p (t q) -> p t q", t=4),
                          k.o_hi[:, kt * 4:kt * 4 + 4, dst], ALU.subtract).then_inc(k.o_done, 1)

    def normalise(a):
        b = a % 2
        dve.wait_ge(k.exp_done, a + 1)
        own.link(dve.tensor_tensor(k.den[:, :], k.psum_[b][:, :], k.esink[b][:, :], ALU.add))
        if a:
            dve.wait_ge(k.probs_done, a)
        own.link(dve.reciprocal(k.rden[:, :], k.den[:, :]))
        w = bcast(k.rden[:, :].rearrange("p (u o) -> p u o", o=1), [P, 4, P])
        if a % NCH == 0:
            if a:
                dve.wait_ge(k.pt_ready, a - 1)
                dve.memset(k.pr[b][:, :, 0:CH], 0.0).then_inc(k.pads_set, 1)
            dve.wait_ge(k.pads_set, 3 + a // NCH)
        dve.tensor_tensor(k.pr[b][:, :, :], k.pr[b][:, :, :], w, ALU.mult).then_inc(k.probs_done, 1)

    def attend(h):
        if h < 2 * NCH:
            row_max(h)
        if 0 <= h - 1 < 2 * NCH:
            normalise(h - 1)
        if 0 <= h - 3 < 2 * NCH:
            low_o(h - 3)

    for i in range(8):
        scaled(i)
    dve.wait_ge(k.misc, 2)
    for i in range(8, 12):
        attend(2 * (i - 8))
        scaled(i)
        attend(2 * (i - 8) + 1)
    for h in range(NCH, 2 * NCH + 3):
        attend(h)
    boundary(2, "f_pre", KT, k.hs_hi, k.hs_lo)
    ffn(1)
    boundary(3, None, 0, None, None)


def trunk(nc, d_x, d_slabs, d_wdt, d_par, d_hpar, d_dskip, d_sinks, d_out):
    k = Core()
    k.d_x, k.d_slabs, k.d_wdt, k.d_par, k.d_hpar, k.d_dskip, k.d_sinks, k.d_out = (
        d_x, d_slabs, d_wdt, d_par, d_hpar, d_dskip, d_sinks, d_out)
    k.d_cs = nc.dram_tensor("cs_scratch", (NH, SEQ), F32, kind="Internal").ap()
    with ExitStack() as ctx:
        def sb(stack, name, shape, dt=F32):
            return stack.enter_context(nc.sbuf_tensor(name, shape, dt))

        keep = ctx
        k.h = sb(keep, "h", [P, KT, SEQ])
        k.hs_hi, k.hs_lo = (sb(keep, f"hs_{x}", [P, KT, SEQ], F32R) for x in ("hi", "lo"))
        k.raw = [sb(keep, f"raw{s}", [P, DM]) for s in range(RING)]
        k.whi = [sb(keep, f"whi{s}", [P, DM], F32R) for s in range(RING)]
        k.wlo = [sb(keep, f"wlo{s}", [P, DM], F32R) for s in range(RING)]
        k.par = sb(keep, "par", [P, N_COLS])
        k.hpar = sb(keep, "hpar", [NH, 2])
        k.dskip = sb(keep, "dskip", [P, OUT_K])
        k.nsink = sb(keep, "nsink", [P, 8])
        k.ones, k.ident, k.tri = (sb(keep, x, [P, P]) for x in ("ones", "ident", "tri"))
        k.eps = sb(keep, "eps", [P, 1])
        k.bo_post = sb(keep, "bo_post", [P, KT])
        k.rpre, k.rpost, k.acc = (sb(keep, x, [P, SEQ]) for x in ("rpre", "rpost", "acc"))
        k.sq = [sb(keep, f"sq{i}", [P, SEQ]) for i in range(2)]

        with ExitStack() as st:
            k.yg = sb(st, "yg", [P, OUT_K, SEQ])
            k.hn = k.yg
            with ExitStack() as s2:
                k.xt = [sb(s2, f"xt{i}", [P, 2, SEQ]) for i in range(2)]
                k.bt = [sb(s2, f"bt{i}", [P, SEQ]) for i in range(2)]
                k.ct = [sb(s2, f"ct{i}", [P, SEQ]) for i in range(2)]
                k.sz = sb(s2, "sz", [P, 2, SEQ])
                k.cacc = [sb(s2, f"cacc{i}", [P, SEQ]) for i in range(2)]
                k.csb = sb(s2, "csb", [P, HG, SEQ])
                k.btok = sb(s2, "btok", [P, NC, P])
                k.xdt, k.xdd = (sb(s2, x, [P, NC, 256]) for x in ("xdt", "xdd"))
                k.cbm = sb(s2, "cbm", [P, SEQ])
                k.hst = sb(s2, "hst", [P, 3, 256])
                k.htmp = sb(s2, "htmp", [P, 256])
                k.dec = sb(s2, "dec", [P, HG, NC])
                k.e2 = sb(s2, "e2", [P, 2, SEQ - SC])
                k.tok = sb(s2, "tok", [P, NC * 96])
                k.tokg = sb(s2, "tokg", [P, NC, 3, HG])
                k.wdt = sb(s2, "wdt", [P, KT * NH])
                k.yt = [sb(s2, f"yt{i}", [P, SEQ]) for i in range(2)]
                k.yo = sb(s2, "yo", [P, SEQ - SC])
                k.grstd = sb(s2, "grstd", [P, SEQ])
            k.dtx, k.dta = k.yt[0][0:NH, :], k.yt[1][0:NH, :]
            with ExitStack() as s3:
                k.yn_hi = [sb(s3, f"yn_hi{i}", [P, SEQ], F32R) for i in range(RING)]
                k.yn_lo = [sb(s3, f"yn_lo{i}", [P, SEQ], F32R) for i in range(RING)]
        k.dte, k.dtu = k.rpost[0:NH, :], k.acc[0:NH, :]
        k.dtl, k.dtr = k.grstd[0:NH, :], k.sq[0][0:NH, :]
        k.dt_, k.ncs = k.xdt[0:NH, 0:2, :].rearrange("p c t -> p (c t)"), k.xdt[0:NH, 2:4, :].rearrange("p c t -> p (c t)")
        k.dtw, k.cs = k.xdd[0:NH, 0:2, :].rearrange("p c t -> p (c t)"), k.xdd[0:NH, 2:4, :].rearrange("p c t -> p (c t)")
        k.gsq = k.sq
        k.gacc = k.acc
        k.aneg = k.dec[0:NH, 0, 0:1]

        with ExitStack() as st:
            k.f = sb(st, "f", [P, FT, SEQ])
            k.f_hi = [sb(st, f"f_hi{i}", [P, SEQ], F32R) for i in range(RING)]
            k.f_lo = [sb(st, f"f_lo{i}", [P, SEQ], F32R) for i in range(RING)]
        with ExitStack() as st:
            k.hk_hi, k.hk_lo = (sb(st, f"hk_{x}", [P, KT, SEQ], F32R) for x in ("hi", "lo"))
            k.o_hi, k.o_lo = k.hk_hi, k.hk_lo
            k.qt = sb(st, "qt", [P, 2, NCH, 4 * CH])
            k.kp, k.vp = (sb(st, x, [P, 2, CH + SEQ]) for x in ("kp", "vp"))
            k.vtok = sb(st, "vtok", [P, NCH, 2, P])
            k.pr = [sb(st, f"pr{i}", [P, 4, P]) for i in range(2)]
            k.pts = [sb(st, f"pts{i}", [P, 4 * P]) for i in range(2)]
            k.qs = [sb(st, f"qs{i}", [P, SEQ]) for i in range(2)]
            k.rmax, k.nmax, k.dsink, k.esink, k.psum_ = (
                [sb(st, f"{name}{i}", [P, 4]) for i in range(2)] for name in ("rmax", "nmax", "dsink", "esink", "psum"))
            k.den, k.rden = (sb(st, x, [P, 4]) for x in ("den", "rden"))
            k.mix = sb(st, "mix", [P, KT, SEQ])
            k.u = [[k.mix[:, 4 * b + v, :] for v in range(2)] for b in range(2)]
            k.cv = [[k.mix[:, 4 * b + 2 + v, :] for v in range(2)] for b in range(2)]

        k.ps = ctx.enter_context(nc.psum_tensor("ps", [P, 8, SEQ], F32))

        def sems(*names):
            return [ctx.enter_context(nc.semaphore(name)) for name in names]

        k.par_loaded, k.small_loaded, k.stored, k.ones_set, k.consts_ready, k.eps_set, k.pads_set, k.misc = sems(
            "par_loaded", "small_loaded", "stored", "ones_set", "consts_ready", "eps_set", "pads_set", "misc")
        k.hi_done, k.lo_done, k.slab_used = sems(
            "hi_done", "lo_done", "slab_used")
        k.sq_done, k.sq_added, k.sums_ready, k.ln_done, k.rstd_done, k.hn_done, k.hi_part_done, k.lo_part_done = sems(
            "sq_done", "sq_added", "sums_ready", "ln_done", "rstd_done", "hn_done", "hi_part_done", "lo_part_done")
        k.mix_ready, k.mix_read, k.h_done = sems(
            "mix_ready", "mix_read", "h_done")
        k.dt_ready, k.dt_exp, k.dt_u, k.cs_done, k.dtw_done, k.tok_ready, k.tok_done, k.cs_stored, k.cs_loaded = sems(
            "dt_ready", "dt_exp", "dt_u", "cs_done", "dtw_done", "tok_ready", "tok_done", "cs_stored", "cs_loaded")
        k.tap0_done, k.conv_done, k.xbc_done, k.z_done, k.tokg_done, k.e_done, k.seg_done, k.l_done, k.cb_ready, k.cbm_done = sems(
            "tap0_done", "conv_done", "xbc_done", "z_done", "tokg_done", "e_done", "seg_done", "l_done", "cb_ready", "cbm_done")
        k.btok_ready, k.btok_done, k.xtok_ready, k.xtok_done, k.m_done, k.state_ready, k.state_done, k.ydiag_ready = sems(
            "btok_ready", "btok_done", "xtok_ready", "xtok_done", "m_done", "state_ready", "state_done", "ydiag_ready")
        k.yoff_ready, k.y_done, k.gsq_done, k.gate_acc_done, k.gate_sums_ready, k.gln_done, k.gate_rstd_done = sems(
            "yoff_ready", "y_done", "gsq_done", "gate_acc_done", "gate_sums_ready", "gln_done", "gate_rstd_done")
        k.yn_scaled, k.yn_hi_done, k.yn_done = sems(
            "yn_scaled", "yn_hi_done", "yn_done")
        k.u_done, k.ftap0_done, k.fconv_done, k.fsilu_done, k.f_prod_done, k.f_hi_done, k.f_lo_done = sems(
            "u_done", "ftap0_done", "fconv_done", "fsilu_done", "f_prod_done", "f_hi_done", "f_lo_done")
        k.qkv_read, k.kqv_done, k.vtok_ready, k.vtok_done, k.scores_ready, k.nmax_done, k.exp_done, k.probs_done = sems(
            "qkv_read", "kqv_done", "vtok_ready", "vtok_done", "scores_ready", "nmax_done", "exp_done", "probs_done")
        k.pt_ready, k.pt_done, k.o_ready, k.o_hi_done, k.o_done = sems(
            "pt_ready", "pt_done", "o_ready", "o_hi_done", "o_done")
        k.act_own, k.dve_own = sems(
            "act_own", "dve_own")
        k.raw_loaded = [ctx.enter_context(nc.semaphore(f"raw_loaded{s}")) for s in range(RING)]
        k.x_loaded = [ctx.enter_context(nc.semaphore(f"x_loaded{c}")) for c in range(KT)]
        k.lo_base = {0: KT, 1: 2 * KT, 2: 4 * KT}
        k.lo_q_base = 3 * KT
        k.pre_count = [3, 7]
        k.q_bank = [2, 3, 0, 1, 0, 1, 0, 1]

        block = ctx.enter_context(nc.Block())

        @block.sync
        def _(sp):
            sp_program(k, sp)

        @block.gpsimd
        def _(pool):
            pool_program(k, pool)

        @block.tensor
        def _(pe):
            pe_program(k, pe)

        @block.scalar
        def _(act):
            act_program(k, act)

        @block.vector
        def _(dve):
            dve_program(k, dve)


def kernel(**inputs):
    import concourse.bacc as bacc
    from concourse.bass_utils import run_bass_kernel_spmd

    a = {n: np.asarray(v) for n, v in inputs.items()}

    def tiles(v):
        return v.reshape(-1, P).T

    def slabs_a(w):
        return w.reshape(KT, P, -1, P).transpose(2, 1, 0, 3).reshape(-1, P, DM)

    w_in = a["a_in_proj"][0]
    w_in_tiles = slabs_a(w_in[:, :NG * GROUP_SLABS * P])
    xbc = DI // P
    tiles_of = [(xbc + 16 + g, xbc + 24 + g, xbc + 2 * g, xbc + 2 * g + 1, 2 * g, 2 * g + 1) for g in range(NG)]
    order = [t for group in tiles_of for t in group]
    def by_kv(v, axis):
        v = np.moveaxis(v, axis, 0)
        v = v.reshape(2, 2, 4, 64, *v.shape[1:]).swapaxes(1, 2).reshape(v.shape)
        return np.moveaxis(v, 0, axis)

    slabs = np.concatenate([
        w_in_tiles[order], a["a_out_proj"][0].reshape(-1, P, DM),
        slabs_a(a["f_up"][0]).reshape(2, FT, P, DM).swapaxes(0, 1).reshape(-1, P, DM), a["f_down"][0].reshape(-1, P, DM),
        slabs_a(a["w_kv"]), slabs_a(by_kv(a["w_q"][0], 1)), by_kv(a["w_o"][0], 0).reshape(-1, P, DM),
        slabs_a(a["f_up"][1]).reshape(2, FT, P, DM).swapaxes(0, 1).reshape(-1, P, DM), a["f_down"][1].reshape(-1, P, DM),
    ])
    params = {
        "a_pre": a["a_norm_pre"], "a_conv": a["a_conv_w"], "a_convb": a["a_conv_b"], "a_gate": a["a_gate_norm"],
        "a_post": a["a_norm_post"], "kvn": a["kv_norm"], "b_kv": a["b_kv"], "b_pre": a["b_norm_pre"],
        "b_q": by_kv(a["b_q"][0], 0), "b_o": a["b_o"], "b_post": a["b_norm_post"], "f_pre": a["f_norm_pre"],
        "f_conv": a["f_conv_w"], "f_convb": a["f_conv_b"], "f_post": a["f_norm_post"],
    }
    arrays = {
        "x": a["x"][0].T.reshape(KT, P, SEQ).transpose(1, 0, 2),
        "slabs": slabs.reshape(N_SLABS * P, DM),
        "wdt": w_in[:, NG * GROUP_SLABS * P:].reshape(KT, P, NH).transpose(1, 0, 2).reshape(P, KT * NH),
        "par": np.concatenate([tiles(params[n]) for n in COL], axis=1),
        "hpar": np.stack([a["a_dt_bias"][0], a["a_a_log"][0]], axis=1),
        "dskip": a["a_d_skip"][0].reshape(OUT_K, 2).T,
        "sinks": a["sinks"][0].reshape(8, 2).T,
    }
    arrays = {n: np.ascontiguousarray(v) for n, v in arrays.items()}
    nc = bacc.Bacc("TRN2", target_bir_lowering=False, num_devices=1)
    args = [nc.dram_tensor(f"in_{n}", v.shape, F32, kind="ExternalInput").ap() for n, v in arrays.items()]
    out = nc.dram_tensor("out", (P, KT, SEQ), F32, kind="ExternalOutput").ap()
    trunk(nc, *args, out)
    r = run_bass_kernel_spmd(nc, [{f"in_{n}": v for n, v in arrays.items()}], core_ids=[0])
    got = np.asarray(r.results[0]["out"])
    return got.transpose(1, 0, 2).reshape(DM, SEQ).T[None].copy()
```

```python
from contextlib import ExitStack, contextmanager

import numpy as np
import concourse.bass as bass
from concourse import mybir
from concourse.alu_op_type import AluOpType as ALU

F32, F32R = mybir.dt.float32, mybir.dt.float32r
ACT = mybir.ActivationFunctionType
AX_X = mybir.AxisListType.X
ds = bass.ds

P = 128
DM, SEQ, EPS = 1024, 512, 1e-6
KT = DM // P
DI, DS, NG, NH = 2048, 128, 8, 32
HG = NH // NG
SC = 128
NC = SEQ // SC
GROUP_SLABS = 6
DFF = 2816
FT = DFF // P
CH = 64
NCH = SEQ // CH
RING = 4
LAST_DVE = 6
CONV_BANK = (2, 0, 1, 2)
N_IN = NG * GROUP_SLABS
OUT0 = N_IN
OUT_K = DI // P
UP = [OUT0 + OUT_K, 0]
DOWN = [UP[0] + 2 * FT, 0]
KV0 = DOWN[0] + FT
Q0 = KV0 + 4
O0 = Q0 + KT
UP[1] = O0 + KT
DOWN[1] = UP[1] + 2 * FT
N_SLABS = DOWN[1] + FT
_cols, _n = {}, 0
for _name, _count in (("a_pre", KT), ("a_conv", 4 * 32), ("a_convb", 32), ("a_gate", OUT_K), ("a_post", KT),
                      ("kvn", KT), ("b_kv", 4), ("b_pre", KT), ("b_q", KT), ("b_o", KT), ("b_post", KT),
                      ("f_pre", 2 * KT), ("f_conv", 2 * 3 * 2 * FT), ("f_convb", 2 * 2 * FT), ("f_post", 2 * KT)):
    _cols[_name] = _n
    _n += _count
COL, N_COLS = _cols, _n


def score_bank(a):
    return (2, 4)[a % 2] if a < NCH else (2, 4, 0)[(a - NCH) % 3]


class Core:
    pass


class Steps:

    def __init__(self, eng, sem):
        self.eng, self.sem, self.base, self.n = eng, sem, 0, 0

    def done(self, ins):
        ins.then_inc(self.sem, 1)
        self.n += 1

    def wait(self):
        self.eng.wait_ge(self.sem, self.base + self.n)

    def link(self, ins):
        self.done(ins)
        self.wait()


@contextmanager
def looped(eng, lo, hi, *tallies):
    before = [(s, s.base + s.n, per) for s, per in tallies]
    with eng.Fori(lo, hi) as i:
        for s, b, per in before:
            s.base, s.n = b + (i - lo) * per, 0
        yield i
        for s, b, per in before:
            assert s.n == per, (s.n, per)
    for s, b, per in before:
        s.base, s.n = b + (hi - lo) * per, 0


def bcast(ap, shape):
    return ap.to_broadcast(shape)


def sp_program(k, sp):
    def x_tiles(*tiles):
        for c in tiles:
            sp.dma_start(k.h[:, c, :], k.d_x[:, c, :]).then_inc(k.x_loaded[c], 16)

    def slab(s):
        sp.dma_start(k.raw[s][:, :], k.d_slabs[s * P:(s + 1) * P, :]).then_inc(k.raw_loaded[s], 16)

    slab(0)
    sp.dma_start(k.par[:, :], k.d_par).then_inc(k.par_loaded, 16)
    x_tiles(0, 1)
    slab(1)
    x_tiles(2, 3)
    slab(2)
    x_tiles(4, 5, 6, 7)
    sp.dma_start(k.wdt[:, :], k.d_wdt).then_inc(k.small_loaded, 16)
    sp.dma_start(k.hpar[:, :], k.d_hpar).then_inc(k.small_loaded, 16)
    for half in range(2):
        rows = slice(64 * half, 64 * half + 64)
        sp.dma_start(k.dskip[rows, :], bcast(k.d_dskip[half:half + 1, :], [64, 16])).then_inc(k.small_loaded, 16)
        sp.dma_start(k.nsink[rows, :], bcast(k.d_sinks[half:half + 1, :], [64, 8])).then_inc(k.small_loaded, 16)
    slab(3)
    with sp.Fori(1, N_SLABS // RING) as r:
        for s in range(RING):
            row = sp.snap(r * (RING * P) + s * P)
            sp.wait_ge(k.lo_done, r * RING + (s + 1 - RING))
            sp.dma_start(k.raw[s][:, :], k.d_slabs[ds(row, P), :]).then_inc(k.raw_loaded[s], 16)
    for c in (0, 1, 6, 2, 3, 7, 4, 5):
        if c < LAST_DVE:
            sp.wait_ge(k.h_done, 3 * KT + c + 1)
        else:
            sp.wait_ge(k.h_last_done, c - LAST_DVE + 1)
        sp.dma_start(k.d_out[:, c, :], k.h[:, c, :]).then_inc(k.stored, 16)
    sp.wait_ge(k.stored, 16 * KT)


def pool_program(k, pool):
    pool.memset(k.ones[:, :], 1.0).then_inc(k.ones_set, 1)
    pool.wait_ge(k.ones_set, 1)
    pool.affine_select(out=k.ident[:, :], in_=k.ones[:, :], compare_op=ALU.is_equal, fill=0.0,
                       base=0, pattern=[[1, P]], channel_multiplier=-1).then_inc(k.consts_ready, 1)
    pool.affine_select(out=k.tri[:, :], in_=k.ones[:, :], compare_op=ALU.is_ge, fill=0.0,
                       base=0, pattern=[[1, P]], channel_multiplier=-1).then_inc(k.consts_ready, 1)

    def lows(first, end):
        def low(n, s):
            pool.wait_ge(k.hi_done, n + 1)
            pool.tensor_tensor(k.wlo[s][:, :], k.raw[s][:, :], k.whi[s][:, :], ALU.subtract).then_inc(k.lo_done, 1)

        turns = (end - first) // RING
        with pool.Fori(0, turns) as r:
            for j in range(RING):
                low(r * RING + (first + j), (first + j) % RING)
        for n in range(first + turns * RING, end):
            low(n, n % RING)

    def squares(norm):
        for m in range(KT):
            add_square(k, pool, m, norm)

    lows(0, OUT0 + 3)
    for kk in range(RING):
        low_y(k, pool, kk)
    lows(OUT0 + 3, UP[0] + RING)
    squares(2)
    lows(UP[0] + RING, KV0 + RING)
    squares(4)
    lows(KV0 + RING, UP[1] + RING)
    squares(6)
    lows(UP[1] + RING, N_SLABS)
    pool.wait_ge(k.mix_read, 4 * KT)
    pool.wait_ge(k.rstd_done, 8)
    for c in range(LAST_DVE, KT):
        pool.tensor_tensor(k.mix[:, c, :], k.mix[:, c, :], k.rpost[:, :], ALU.mult).then_inc(k.last_scaled, 1)
        pool.wait_ge(k.last_scaled, c - LAST_DVE + 1)
        pool.tensor_tensor(k.h[:, c, :], k.h[:, c, :], k.mix[:, c, :], ALU.add).then_inc(k.h_last_done, 1)


def added_before(norm):
    return KT * norm - norm // 2


def add_square(k, eng, m, norm):
    sq = k.sq[m % 2]
    eng.wait_ge(k.sq_done, norm * KT + m + 1)
    if m == 0:
        if norm:
            eng.wait_ge(k.sums_ready, norm)
        eng.tensor_copy(k.acc[:, :], sq[:, :]).then_inc(k.sq_added, 1)
    else:
        eng.wait_ge(k.sq_added, added_before(norm) + m)
        eng.tensor_tensor(k.acc[:, :], k.acc[:, :], sq[:, :], ALU.add).then_inc(k.sq_added, 1)


def low_y(k, eng, kk):
    s = (OUT0 + kk) % RING
    eng.wait_ge(k.yn_hi_done, kk + 1)
    eng.wait_ge(k.yn_scaled, kk + 1)
    eng.tensor_tensor(k.yn_lo[s][:, :], k.yg[:, kk, :], k.yn_hi[s][:, :], ALU.subtract).then_inc(k.yn_done, 1)


def pe_program(k, pe):
    ps = k.ps

    def slab_a(n, bank, hi, lo, m0=True):
        s = n % RING if isinstance(n, int) else n[1]
        for c in range(KT):
            wh, wl = k.whi[s][:, c * P:(c + 1) * P], k.wlo[s][:, c * P:(c + 1) * P]
            pe.matmul(ps[:, bank, :], wh, hi[:, c, :], start=(c == 0), stop=False)
            pe.matmul(ps[:, bank, :], wh, lo[:, c, :], start=False, stop=False)
            last = pe.matmul(ps[:, bank, :], wl, hi[:, c, :], start=False, stop=(c == KT - 1))
        last.then_inc(k.slab_used, 1)

    def first_slabs_a(n, banks, hi, lo, parts_ready, base, skew=0, after_first=None):
        for step in range(KT + skew * (len(banks) - 1)):
            for j, bank in enumerate(banks):
                s, c = (n + j) % RING, step - skew * j
                if not 0 <= c < KT:
                    continue
                if j == 0:
                    pe.wait_ge(parts_ready, base + c + 1)
                if c == 0:
                    pe.wait_ge(k.lo_done, n + j + 1)
                wh, wl = k.whi[s][:, c * P:(c + 1) * P], k.wlo[s][:, c * P:(c + 1) * P]
                pe.matmul(ps[:, bank, :], wh, hi[:, c, :], start=(c == 0), stop=False)
                pe.matmul(ps[:, bank, :], wh, lo[:, c, :], start=False, stop=False)
                last = pe.matmul(ps[:, bank, :], wl, hi[:, c, :], start=False, stop=(c == KT - 1))
                if c == KT - 1:
                    last.then_inc(k.slab_used, 1)
                    if j == 0 and after_first:
                        after_first()

    def three(m, s, hi_k, lo_k, start, stop):
        wh, wl = k.whi[s][:, m * P:(m + 1) * P], k.wlo[s][:, m * P:(m + 1) * P]
        pe.matmul(ps[:, m, :], wh, hi_k, start=start, stop=False)
        pe.matmul(ps[:, m, :], wh, lo_k, start=False, stop=False)
        return pe.matmul(ps[:, m, :], wl, hi_k, start=False, stop=stop)

    def slab_b(s, hi_k, lo_k, start=False, order=range(KT), bank_0=None):
        for m in order:
            if m == 0 and bank_0 is not None:
                pe.wait_ge(*bank_0)
            last = three(m, s, hi_k, lo_k, start, False)
        last.then_inc(k.slab_used, 1)

    def tail_b(slots, parts):
        for m in range(KT):
            for j, (s, (hi_k, lo_k)) in enumerate(zip(slots, parts)):
                last = three(m, s, hi_k, lo_k, False, j == 1)
                if m == KT - 1 and j == 0:
                    last.then_inc(k.slab_used, 1)
            last.then_inc(k.mix_ready if m < KT - 1 else k.slab_used, 1)

    def column_sums(norm):
        pe.wait_ge(k.sq_added, added_before(norm + 1))
        if norm % 2 == 0:
            pe.matmul(ps[:, 6, :], k.ones[:, :], k.acc[:, :], start=True, stop=True).then_inc(k.sums_ready, 1)
            return
        pe.matmul(ps[:, 6, :], k.ones[:, :], k.acc[:, :], start=True, stop=False)
        pe.wait_ge(k.sq_done, KT * (norm + 1))
        pe.matmul(ps[:, 6, :], k.ones[:, :], k.sq[(KT - 1) % 2][:, :], start=False, stop=True).then_inc(k.sums_ready, 1)

    def keep_clock(n):
        if n == 0:
            for _ in range(18):
                pe.matmul(ps[:, 7, 0:P], k.ones[:, :], k.ones[:, :], start=True, stop=True)
            return
        w = k.whi[n % RING]
        pe.wait_ge(k.lo_done, n + 1)
        for _ in range(16):
            pe.matmul(ps[:, 7, :], w[:, 0:P], w[:, 0:SEQ], start=True, stop=True)

    def ssd_1(g, p):
        pe.wait_ge(k.xbc_done, g * 4 + 4)
        if not isinstance(g, int) or g > 0:
            pe.wait_ge(k.gate_rstd_done, g)
            pe.wait_ge(k.y_done, g * 2)
        for c in range(NC):
            t = slice(c * SC, (c + 1) * SC)
            last = pe.matmul(ps[:, 3, t], k.bt[p][:, t], k.ct[p][:, t], start=True, stop=True)
        last.then_inc(k.cb_ready, 1)
        for c in range(NC):
            t = slice(c * SC, (c + 1) * SC)
            last = pe.transpose(ps[:, 7, t], k.bt[p][:, t], k.ident[:, :])
        last.then_inc(k.btok_ready, 1)
        for j in range(2):
            for c in range(NC):
                t = slice(c * SC, (c + 1) * SC)
                last = pe.transpose(ps[:, 5 + j, t], k.xt[p][:, j, t], k.ident[:, :])
            last.then_inc(k.xtok_ready, 1)

    def ssd_2(g, p):
        pe.wait_ge(k.btok_done, g + 1)
        pe.wait_ge(k.xtok_done, g * 4 + 4)
        pe.wait_ge(k.cbm_done, g + 1)
        for c in range(NC - 1):
            out = ps[:, 4, c * 256:(c + 1) * 256] if c < 2 else ps[:, 3, 0:256]
            last = pe.matmul(out, k.btok[:, c, :], k.xdd[:, c, :], start=True, stop=True)
        last.then_inc(k.state_ready, 1)

    def ssd_3(g, p):
        for hh in range(HG):
            if hh == 0:
                pe.wait_ge(k.m_done, g * 4 + 4)
            j, half = hh // 2, hh % 2
            for c in range(NC):
                t = slice(c * SC, (c + 1) * SC)
                last = pe.matmul(ps[64 * half:64 * half + 64, 5 + j, t], k.xdt[:, c, hh * 64:hh * 64 + 64],
                                 k.csb[:, hh, t], start=True, stop=True)
        last.then_inc(k.ydiag_ready, 1)

    def ssd_4(g, p):
        pe.wait_ge(k.state_done, g + 1)
        for j, bank in enumerate((7, 4)):
            for c in range(1, NC):
                t = slice(c * SC, (c + 1) * SC)
                last = pe.matmul(ps[:, bank, t], k.hst[:, c - 1, j * P:(j + 1) * P], k.ct[p][:, t],
                                 start=True, stop=True)
        last.then_inc(k.yoff_ready, 1)

    def ssd_5(g):
        pe.wait_ge(k.gate_acc_done, g + 1)
        pe.matmul(ps[:, 3, :], k.ones[:, :], k.gacc[:, :], start=True, stop=True).then_inc(k.gate_sums_ready, 1)

    def in_proj_group(G, p):
        g, q = G - 1, 1 - p
        base = G * GROUP_SLABS - 2
        for j in range(GROUP_SLABS if not (isinstance(G, int) and G == NG) else 2):
            pe.wait_ge(k.lo_done, base + (j + 1))
            if j < 3:
                pe.wait_ge(k.xbc_scaled, G * 4 + (j - 2))
            elif j < 5:
                pe.wait_ge(k.z_scaled, G * 2 + (j - 4))
            else:
                pe.wait_ge(k.xbc_scaled, G * 4 + 1)
            slab_a((0, (p * GROUP_SLABS - 2 + j) % RING), j % 3, k.hs_hi, k.hs_lo)
            if j == 0 and not (isinstance(G, int) and G == 1):
                ssd_5(g - 1)
            if j == 1:
                if isinstance(G, int) and G == 1:
                    token_columns()
                ssd_1(g, q)
            if j == 2:
                ssd_2(g, q)
            if j == 3:
                ssd_3(g, q)
            if j == 4:
                ssd_4(g, q)

    def token_columns():
        pe.wait_ge(k.dtw_done, 1)
        for c in range(NC):
            for i, src in enumerate((k.dt_, k.ncs, k.dtw)):
                last = pe.transpose(ps[:, 4, c * 96 + i * NH:c * 96 + (i + 1) * NH], src[:, c * SC:(c + 1) * SC], k.ident[0:NH, 0:NH])
        last.then_inc(k.tok_ready, 1)

    pe.wait_ge(k.ones_set, 1)
    pe.wait_ge(k.consts_ready, 2)
    keep_clock(0)
    first_slabs_a(0, (2, 0, 1), k.hs_hi, k.hs_lo, k.lo_part_done, 0, skew=2, after_first=lambda: column_sums(0))
    pe.wait_ge(k.wdt_lo_done, 1)
    for c in range(KT):
        w = slice(c * NH, (c + 1) * NH)
        pe.matmul(ps[0:NH, 3, :], k.wdt_hi[:, w], k.hs_hi[:, c, :], start=(c == 0), stop=False)
        pe.matmul(ps[0:NH, 3, :], k.wdt_hi[:, w], k.hs_lo[:, c, :], start=False, stop=False)
        last = pe.matmul(ps[0:NH, 3, :], k.wdt_lo[:, w], k.hs_hi[:, c, :], start=False, stop=(c == KT - 1))
    last.then_inc(k.dt_ready, 1)
    pe.wait_ge(k.lo_done, 4)
    pe.wait_ge(k.xbc_scaled, 1)
    slab_a((0, 3), 2, k.hs_hi, k.hs_lo)
    in_proj_group(1, 1)
    with pe.Fori(1, NG // 2) as i:
        in_proj_group(i * 2, 0)
        in_proj_group(i * 2 + 1, 1)
    in_proj_group(NG, 0)
    def out_part(kk, *ms):
        s = (OUT0 + kk) % RING
        for m in ms:
            last = three(m, s, k.yn_hi[s][:, :], k.yn_lo[s][:, :], kk == 0, False)
        return last

    pe.wait_ge(k.z_scaled, 2 * NG)
    pe.wait_ge(k.xbc_scaled, 4 * NG)
    for kk in range(RING):
        if kk == 2:
            ssd_2(NG - 1, 1)
        if kk == 3:
            ssd_3(NG - 1, 1)
            ssd_4(NG - 1, 1)
        pe.wait_ge(k.lo_done, OUT0 + kk + 1)
        pe.wait_ge(k.yn_done, kk + 1)
        out_part(kk, 0, 1, 2)
    pe.wait_ge(k.y_done, 2 * NG - 1)
    for kk in range(RING):
        out_part(kk, 5, 7)
    ssd_5(NG - 1)
    pe.wait_ge(k.y_done, 2 * NG)
    for kk in range(RING):
        out_part(kk, 4, 6)
        pe.wait_ge(k.gate_rstd_done, NG)
        out_part(kk, 3).then_inc(k.slab_used, 1)

    def out_slab(kk, s):
        pe.wait_ge(k.lo_done, OUT0 + kk + 1)
        pe.wait_ge(k.yn_done, kk + 1)
        slab_b(s, k.yn_hi[s][:, :], k.yn_lo[s][:, :])

    out_slab(4, (OUT0 + 4) % RING)
    out_slab(5, (OUT0 + 5) % RING)
    with pe.Fori(1, 3) as i:
        for j in range(RING):
            out_slab(i * RING + (2 + j), (OUT0 + 2 + j) % RING)
    pe.wait_ge(k.lo_done, OUT0 + OUT_K)
    pe.wait_ge(k.yn_done, OUT_K)
    sl = [(OUT0 + OUT_K - 2 + j) % RING for j in range(2)]
    tail_b(sl, [(k.yn_hi[s][:, :], k.yn_lo[s][:, :]) for s in sl])

    def boundary(t, hi, lo, n):
        pe.wait_ge(k.mix_read, KT * t + 7)
        column_sums(1 + 2 * t)
        pe.wait_ge(k.mix_read, KT * (t + 1))
        if n is None:
            return
        keep_clock(n)
        first_slabs_a(n, [(n + j) % 4 for j in range(3)], hi, lo, k.lo_part_done, k.lo_base[t])
        pe.wait_ge(k.rstd_done, 2 + 2 * t)
        column_sums(2 + 2 * t)

    def ffn(l):
        u0, d0 = UP[l], DOWN[l]
        pe.wait_ge(k.lo_done, u0 + 4)
        slab_a((0, (u0 + 3) % RING), (u0 + 3) % 4, k.hs_hi, k.hs_lo)
        with pe.Fori(1, FT // 2) as r:
            for j in range(4):
                pe.wait_ge(k.lo_done, r * 4 + (u0 + j + 1))
                pe.wait_ge(k.u_done, r * 4 + (l * 2 * FT + j - 3))
                slab_a((0, (u0 + j) % RING), (u0 + j) % 4, k.hs_hi, k.hs_lo)
        pe.wait_ge(k.rstd_done, 3 + 4 * l)

        def down_slab(kk, j, start=False):
            s = (d0 + j) % RING
            pe.wait_ge(k.lo_done, kk + (d0 + 1))
            pe.wait_ge(k.f_lo_done, kk + (l * FT + 1))
            if start:
                slab_b(s, k.f_hi[s][:, :], k.f_lo[s][:, :], start, (4, 5, 6, 7, 0, 1, 2, 3), (k.u_done, (l + 1) * 2 * FT))
            else:
                slab_b(s, k.f_hi[s][:, :], k.f_lo[s][:, :])

        for kk in range(RING):
            down_slab(kk, kk, kk == 0)
        with pe.Fori(1, 5) as r:
            for j in range(RING):
                down_slab(r * RING + j, j)
        pe.wait_ge(k.lo_done, d0 + FT)
        pe.wait_ge(k.f_lo_done, (l + 1) * FT)
        sl = [(d0 + FT - 2 + j) % RING for j in range(2)]
        tail_b(sl, [(k.f_hi[s][:, :], k.f_lo[s][:, :]) for s in sl])

    boundary(0, k.hs_hi, k.hs_lo, UP[0])
    ffn(0)
    boundary(1, k.hk_hi, k.hk_lo, KV0)

    pe.wait_ge(k.lo_done, KV0 + 4)
    slab_a(KV0 + 3, (KV0 + 3) % 4, k.hk_hi, k.hk_lo)

    def scores(a):
        kt, c = a // NCH, a % NCH
        last_use = a - 2 if a < NCH + 2 else a - 3
        if last_use >= 0:
            pe.wait_ge(k.exp_done, last_use + 1)
        for u in range(4):
            r = slice(64 * (u // 2), 64 * (u // 2) + 64)
            last = pe.matmul(ps[:, score_bank(a) + u // 2, (u % 2) * P:(u % 2 + 1) * P],
                             k.qt[r, kt, c, (u % 2) * P:(u % 2 + 1) * P],
                             k.kp[r, kt, c * CH:c * CH + P], start=True, stop=True)
        last.then_inc(k.scores_ready, 1)

    def probs_t(a):
        pe.wait_ge(k.probs_done, a + 1)
        if a >= 1:
            pe.wait_ge(k.pt_done, a)
        for u in range(4):
            last = pe.transpose(ps[:, 6, u * P:(u + 1) * P], k.pr[a % 3][:, u, :], k.ident[:, :])
        last.then_inc(k.pt_ready, 1)

    def mix_values(a):
        kt, c = a // NCH, a % NCH
        pe.wait_ge(k.pt_done, a + 1)
        if a >= 1:
            pe.wait_ge(k.o_done, a)
        for half in range(2):
            last = pe.matmul(ps[64 * half:64 * half + 64, 7, 0:256],
                             k.vtok[:, c, kt, 64 * half:64 * half + 64],
                             k.pts[a % 2][:, 2 * half * P:(2 * half + 2) * P], start=True, stop=True)
        last.then_inc(k.o_ready, 1)

    def q_slab_half(n, bank, c0):
        s = n % RING
        for c in range(c0, c0 + KT // 2):
            wh, wl = k.whi[s][:, c * P:(c + 1) * P], k.wlo[s][:, c * P:(c + 1) * P]
            pe.matmul(ps[:, bank, :], wh, k.hs_hi[:, c, :], start=(c == 0), stop=False)
            pe.matmul(ps[:, bank, :], wh, k.hs_lo[:, c, :], start=False, stop=False)
            last = pe.matmul(ps[:, bank, :], wl, k.hs_hi[:, c, :], start=False, stop=(c == KT - 1))
        if c0:
            last.then_inc(k.slab_used, 1)

    def attend(h):
        if h == 0:
            pe.wait_ge(k.kqv_done, 8)
            pe.wait_ge(k.qkv_read, 8)
        if h == NCH:
            pe.wait_ge(k.kqv_done, 12)
            pe.wait_ge(k.qkv_read, 12)
        if h < 2 * NCH:
            scores(h)
        if 0 <= h - 3 < 2 * NCH:
            probs_t(h - 3)
        if h == 4:
            pe.wait_ge(k.vtok_done, 4)
        if 0 <= h - 4 < 2 * NCH:
            mix_values(h - 4)
        if h >= 2 * NCH:
            first, ms = 2 * (h % 2), (0, 1) if h < 2 * NCH + 2 else (2, 3)
            if h == 2 * NCH:
                pe.wait_ge(k.exp_done, 2 * NCH - 2)
                pe.wait_ge(k.lo_done, O0 + RING)
            if h == 2 * NCH + 2:
                pe.wait_ge(k.exp_done, 2 * NCH)
            o_part(first, *ms)
            o_part(first + 1, *ms)

    def o_part(kk, *ms):
        for m in ms:
            last = three(m, (O0 + kk) % RING, k.o_hi[:, kk, :], k.o_lo[:, kk, :], kk == 0, False)
        return last

    for i in range(KT):
        n = Q0 + i
        pe.wait_ge(k.lo_done, n + 1)
        if i == 0:
            pe.wait_ge(k.lo_part_done, k.lo_q_base + KT)
        pe.wait_ge(k.qkv_read, n - KV0 - (1 if i >= 2 else 3))
        q_slab_half(n, k.q_bank[i], 0)
        if i >= 4:
            attend(2 * (i - 4))
        q_slab_half(n, k.q_bank[i], KT // 2)
        if i >= 4:
            attend(2 * (i - 4) + 1)
        if i < 4:
            b = i
            if b == 0:
                pe.wait_ge(k.kqv_done, 4)
            else:
                pe.wait_ge(k.vtok_done, b)
            for w in range(2):
                c = 2 * b + w
                for kt in range(2):
                    last = pe.transpose(ps[:, 7, (w * 2 + kt) * P:(w * 2 + kt + 1) * P],
                                        k.vp[:, kt, c * CH:c * CH + P], k.ident[:, :])
            last.then_inc(k.vtok_ready, 1)
    for h in range(NCH, 2 * NCH + 4):
        attend(h)
    pe.wait_ge(k.pt_done, 2 * NCH)
    pe.wait_ge(k.o_done, 2 * NCH)
    for kk in range(RING):
        o_part(kk, 4, 5, 6, 7).then_inc(k.slab_used, 1)
    for kk in range(RING, KT - 2):
        pe.wait_ge(k.lo_done, O0 + kk + 1)
        slab_b((O0 + kk) % RING, k.o_hi[:, kk, :], k.o_lo[:, kk, :])
    pe.wait_ge(k.lo_done, O0 + KT)
    tail_b([(O0 + KT - 2 + j) % RING for j in range(2)],
           [(k.o_hi[:, KT - 2 + j, :], k.o_lo[:, KT - 2 + j, :]) for j in range(2)])
    boundary(2, k.hs_hi, k.hs_lo, UP[1])
    ffn(1)
    boundary(3, None, None, None)


def act_program(k, act):
    ps, par = k.ps, k.par

    def col(name, i):
        if isinstance(i, int):
            return par[:, COL[name] + i:COL[name] + i + 1]
        return par[:, ds(i + COL[name], 1)]

    def hi(n, s):
        if n >= N_SLABS:
            return
        if n >= RING:
            act.wait_ge(k.slab_used, n - (RING - 1))
        act.wait_ge(k.raw_loaded[s], 16 * (n // RING + 1))
        act.activation(k.whi[s][:, :], k.raw[s][:, :], ACT.Copy).then_inc(k.hi_done, 1)

    def hi_loop(n, s, lap):
        act.wait_ge(k.slab_used, n - (RING - 1))
        act.wait_ge(k.raw_loaded[s], lap * 16)
        act.activation(k.whi[s][:, :], k.raw[s][:, :], ACT.Copy).then_inc(k.hi_done, 1)

    squares = [0]

    def square(src, bias=None):
        norm, m = squares[0] // KT, squares[0] % KT
        if m >= 2:
            act.wait_ge(k.sq_added, added_before(norm) + m - 1)
        kw = {} if bias is None else {"bias": bias}
        act.activation(k.sq[m % 2][:, :], src, ACT.Square, **kw).then_inc(k.sq_done, 1)
        squares[0] += 1

    lns = Steps(act, k.ln_done)

    def rstd(norm, out):
        act.wait_ge(k.sums_ready, norm + 1)
        if norm:
            act.wait_ge(k.rstd_done, norm)
        lns.link(act.activation(out, ps[:, 6, :], ACT.Ln, bias=k.eps[:, :], scale=1.0 / DM))
        act.activation(out, out, ACT.Exp, scale=-0.5).then_inc(k.rstd_done, 1)

    act.preload_act_table_set("natural_log_exp_and_others")
    act.wait_ge(k.eps_set, 1)
    hi(0, 0)
    act.wait_ge(k.par_loaded, 16)
    for c in range(KT):
        act.wait_ge(k.x_loaded[c], 16)
        act.activation(k.hs_hi[:, c, :], k.h[:, c, :], ACT.Copy, scale=col("a_pre", c)).then_inc(k.hi_part_done, 1)
        square(k.h[:, c, :])
        if c in (1, 3):
            hi((c + 1) // 2, (c + 1) // 2)
    hi(3, 3)
    act.wait_ge(k.small_loaded, 16 * 6)
    act.activation(k.wdt_hi[:, :], k.wdt[:, :], ACT.Copy).then_inc(k.wdt_hi_done, 1)
    rstd(0, k.rpre[:, :])

    own = Steps(act, k.act_own)

    def softplus_steps():
        act.wait_ge(k.dt_scaled, 1)
        own.link(act.activation(k.dtx[:, :], k.dta[:, :], ACT.Identity, bias=k.hpar[:, 0:1]))
        own.link(act.activation(k.dta[:, :], k.dtx[:, :], ACT.Abs))
        act.activation(k.dte[:, :], k.dta[:, :], ACT.Exp, scale=-1.0).then_inc(k.dt_exp, 1)
        act.activation(k.aneg[:, :], k.hpar[:, 1:2], ACT.Exp).then_inc(k.dt_exp, 1)
        act.wait_ge(k.dt_u, 1)
        own.link(act.activation(k.dtl[:, :], k.dtu[:, :], ACT.Ln))
        act.activation(k.dtr[:, :], k.dtl[:, :], ACT.Exp, scale=-1.0).then_inc(k.dt_exp, 1)

    def decay_sums():
        act.wait_ge(k.cs_done, 1)
        act.dma_start(k.d_cs, k.cs[:, :]).then_inc(k.cs_stored, 16)
        for c in range(NC):
            t = slice(c * SC, (c + 1) * SC)
            act.activation(k.dtw[:, t], k.cs[:, t], ACT.Exp, scale=-1.0, bias=k.cs[:, (c + 1) * SC - 1:(c + 1) * SC]).then_inc(k.dt_exp, 1)

    def load_cs(g):
        rows = k.d_cs[ds(g * HG, HG), :] if not isinstance(g, int) else k.d_cs[g * HG:(g + 1) * HG, :]
        act.dma_start(k.csb[:, :, :], bcast(rows.rearrange("(o h) t -> o h t", o=1), [P, HG, SEQ])).then_inc(k.cs_loaded, 16)

    def tap0(G, i):
        tile = (G + 16, G + 24, G * 2, G * 2 + 1)[i]
        if not (isinstance(G, int) and G == 0 and i < 2):
            act.wait_ge(k.xbc_done, G * 4 + (i - 1))
        act.wait_ge(k.xbc_scaled, G * 4 + (i + 1))
        act.activation(k.cacc[i % 2][:, :], k.xbc[i % 2][:, :], ACT.Identity, bias=col("a_convb", tile),
                       scale=col("a_conv", 3 * 32 + tile)).then_inc(k.tap0_done, 1)

    def conv_silu(G, p, i):
        dst = (k.bt[p][:, :], k.ct[p][:, :], k.xt[p][:, 0, :], k.xt[p][:, 1, :])[i]
        act.wait_ge(k.conv_done, G * 4 + (i + 1))
        if i == 0 and (not isinstance(G, int) or G >= 2):
            act.wait_ge(k.y_done, G * 2 - 2)
        act.activation(dst, k.cacc[i % 2][:, :], ACT.Silu).then_inc(k.xbc_done, 1)

    def in_group(G, p, i=None):
        static = isinstance(G, int)
        g = G - 1
        end = static and G == NG

        def step(j):
            s = (p * GROUP_SLABS - 2 + j) % RING
            if static:
                hi(G * GROUP_SLABS - 2 + j + RING, s)
            else:
                hi_loop(G * GROUP_SLABS + (j + RING - 2), s, i * 3 + ((p * GROUP_SLABS - 2 + j + RING) // RING + 1))

        step(0)
        if not (static and g == 0):
            gate_rstd(g - 1)
        conv_silu(g, 1 - p, 2)
        conv_silu(g, 1 - p, 3)
        if end:
            for kk in range(RING):
                yn_hi(kk)
        step(1)
        act.preload_act_table_set("natural_log_exp_and_others")
        if static and g == 0:
            exps(0)
        b_tokens(g)
        decays(g)
        for j in range(2):
            act.wait_ge(k.z_scaled, g * 2 + (j + 1))
            act.activation(k.sz[:, j, :], k.sz[:, j, :], ACT.Silu).then_inc(k.z_done, 1)
        if end:
            return
        step(2)
        tap0(G, 0)
        conv_silu(G, p, 0)
        step(3)
        tap0(G, 1)
        conv_silu(G, p, 1)
        act.wait_ge(k.ydiag_ready, g + 1)
        load_cs(g + 1)
        step(4)
        act.preload_act_table_set("natural_log_exp_and_others")
        y_squares(g)
        tap0(G, 2)
        exps(g + 1)
        step(5)
        tap0(G, 3)

    def exps(g):
        act.wait_ge(k.cs_loaded, g * 16 + 16)
        if not isinstance(g, int) or g >= 1:
            act.wait_ge(k.y_done, g * 2)
        for half in range(2):
            r = slice(64 * half, 64 * half + 64)
            src = k.csb[r, :, :].rearrange("p (j e) t -> p e j t", e=2)[:, half, :, SC:SEQ]
            act.activation(k.e2[r, :, :], src, ACT.Exp).then_inc(k.e_done, 1)
        act.activation(k.dec[:, :, :], k.csb[:, :, :].rearrange("p h (c t) -> p h c t", t=SC)[:, :, :, SC - 1],
                       ACT.Exp).then_inc(k.e_done, 1)

    def decays(g):
        for hh in range(HG):
            act.wait_ge(k.seg_done, g * HG + (hh + 1))
            act.activation(k.csb[:, hh, :], k.csb[:, hh, :], ACT.Exp).then_inc(k.l_done, 1)

    def b_tokens(g):
        act.wait_ge(k.btok_ready, g + 1)
        if not isinstance(g, int) or g >= 1:
            act.wait_ge(k.state_ready, g)
        act.activation(k.btok[:, :, :], ps[:, 7, :].rearrange("p (c n) -> p c n", c=NC), ACT.Copy).then_inc(k.btok_done, 1)

    def gate_rstd(g):
        act.wait_ge(k.gate_sums_ready, g + 1)
        if not isinstance(g, int) or g >= 1:
            act.wait_ge(k.yn_scaled, g * 2)
        act.activation(k.grstd[:, :], ps[:, 3, :], ACT.Ln, bias=k.eps[:, :], scale=1.0 / (DI // NG)).then_inc(k.gln_done, 1)
        act.wait_ge(k.gln_done, g + 1)
        act.activation(k.grstd[:, :], k.grstd[:, :], ACT.Exp, scale=-0.5).then_inc(k.gate_rstd_done, 1)

    def y_squares(g):
        for j in range(2):
            act.wait_ge(k.y_done, g * 2 + (j + 1))
            if j == 0 and (not isinstance(g, int) or g >= 1):
                act.wait_ge(k.gate_acc_done, g)
            act.activation(k.gsq[j][:, :], k.yg[:, g * 2 + j, :], ACT.Square).then_inc(k.gsq_done, 1)

    def yn_hi(kk):
        act.wait_ge(k.yn_scaled, kk + 1)
        if kk >= RING:
            act.wait_ge(k.slab_used, kk + (OUT0 - RING + 1))
        act.activation(k.yn_hi[kk % RING][:, :], k.yg[:, kk, :], ACT.Copy).then_inc(k.yn_hi_done, 1)

    tap0(0, 0)
    tap0(0, 1)
    hi(0 + RING, 0)
    conv_silu(0, 0, 0)
    conv_silu(0, 0, 1)
    tap0(0, 2)
    act.preload_act_table_set("natural_log_exp_and_others")
    softplus_steps()
    hi(1 + RING, 1)
    hi(2 + RING, 2)
    tap0(0, 3)
    hi(3 + RING, 3)
    decay_sums()
    act.wait_ge(k.cs_stored, 16)
    load_cs(0)
    in_group(1, 1)
    with act.Fori(1, NG // 2) as i:
        in_group(i * 2, 0, i)
        in_group(i * 2 + 1, 1, i)
    in_group(NG, 0)
    act.preload_act_table_set("natural_log_exp_and_others")
    y_squares(NG - 1)
    gate_rstd(NG - 1)
    for kk in range(2):
        hi(OUT0 + kk + RING, (OUT0 + kk) % RING)
        yn_hi(kk + RING)
    with act.Fori(0, 2) as i:
        for j in range(RING):
            s = (OUT0 + 2 + j) % RING
            hi_loop(i * RING + (OUT0 + 2 + j + RING), s, i + ((OUT0 + 2 + j + RING) // RING + 1))
            act.activation(k.yn_hi[s][:, :], k.yg[:, i * RING + (2 + j + RING), :], ACT.Copy).then_inc(k.yn_hi_done, 1)
    for kk in range(10, 14):
        hi(OUT0 + kk + RING, (OUT0 + kk) % RING)
        if kk + RING < OUT_K:
            yn_hi(kk + RING)

    def boundary(t, w_post, off, nxt, bias=False):
        for m in range(KT):
            if m < KT - 1:
                act.wait_ge(k.mix_ready, (KT - 1) * t + m + 1)
            else:
                act.wait_ge(k.slab_used, (UP[0], KV0, UP[1], N_SLABS)[t])
            b = col("b_o", m) if bias else None
            square(ps[:, m, :], b)
            kw = {"bias": k.bo_post[:, m:m + 1]} if bias else {}
            act.activation(k.mix[:, m, :], ps[:, m, :], ACT.Identity if bias else ACT.Copy,
                           scale=col(w_post, off + m), **kw).then_inc(k.mix_read, 1)
        if nxt:
            hi(nxt + 2, (nxt + 2) % RING)
        rstd(1 + 2 * t, k.rpost[:, :])
        if nxt:
            hi(nxt + 3, (nxt + 3) % RING)

    def next_parts(t, name, off, dst, nxt):
        for c in range(KT):
            act.wait_ge(k.h_done, KT * t + c + 1)
            act.activation(dst[:, c, :], k.h[:, c, :], ACT.Copy, scale=col(name, off + c)).then_inc(k.hi_part_done, 1)
            square(k.h[:, c, :])
            if t == 1:
                act.activation(k.hs_hi[:, c, :], k.h[:, c, :], ACT.Copy, scale=col("b_pre", c)).then_inc(k.hi_part_done, 1)
        hi(nxt + RING, nxt % RING)
        rstd(2 + 2 * t, k.rpre[:, :])

    def ffn(l):
        u0, d0, i0 = UP[l], DOWN[l], l * FT
        def pair(p, q, r=None):
            for v in range(2):
                s = (u0 + 2 * q + v) % RING
                if r is not None:
                    hi_loop(p * 2 + (u0 + v + RING), s, r + ((u0 + 2 * q + v + RING) // RING + 1))
                elif p or v:
                    hi(u0 + 2 * p + v + RING, s)
                act.wait_ge(k.u_done, p * 2 + (2 * i0 + v + 1))
                tile = p + (v * FT)
                if v == 0 and not (isinstance(p, int) and i0 + p < 2):
                    act.wait_ge(k.f_prod_done, p + (i0 - 1))
                act.activation(k.cv[q][v][:, :], k.u[q][v][:, :], ACT.Identity,
                               bias=col("f_convb", tile + l * 2 * FT),
                               scale=col("f_conv", tile + (l * 3 + 2) * 2 * FT)).then_inc(k.ftap0_done, 1)
            act.wait_ge(k.fconv_done, p * 2 + (2 * i0 + 1))
            act.activation(k.cv[q][0][:, :], k.cv[q][0][:, :], ACT.Silu).then_inc(k.fsilu_done, 1)

        def f_part(kk):
            act.wait_ge(k.f_prod_done, i0 + kk + 1)
            if kk >= RING:
                act.wait_ge(k.slab_used, d0 + kk - RING + 1)
            act.activation(k.f_hi[(d0 + kk) % RING][:, :], k.f[:, kk, :], ACT.Copy).then_inc(k.f_hi_done, 1)

        pair(0, 0)
        pair(1, 1)
        f_part(0)
        f_part(1)
        with act.Fori(1, FT // 2) as r:
            pair(r * 2, 0, r)
            pair(r * 2 + 1, 1, r)
        act.preload_act_table_set("natural_log_exp_and_others")
        f_part(2)
        f_part(3)
        for kk in range(RING):
            hi(d0 + kk + RING, (d0 + kk) % RING)
            f_part(kk + RING)
        with act.Fori(1, 4) as r:
            for j in range(RING):
                s = (d0 + j) % RING
                hi_loop(r * RING + (d0 + j + RING), s, r + ((d0 + j + RING) // RING + 1))
                act.activation(k.f_hi[s][:, :], k.f[:, r * RING + (j + RING), :], ACT.Copy).then_inc(k.f_hi_done, 1)
        for kk in range(FT - 6, FT - 2):
            hi(d0 + kk + RING, (d0 + kk) % RING)
            if kk + RING < FT:
                f_part(kk + RING)

    boundary(0, "a_post", 0, UP[0])
    next_parts(0, "f_pre", 0, k.hs_hi, UP[0])
    ffn(0)
    boundary(1, "f_post", 0, KV0)
    next_parts(1, "kvn", 0, k.hk_hi, KV0)
    def kqv(i):
        if i:
            hi(KV0 + i + RING, (KV0 + i) % RING)
        act.wait_ge(k.qkv_read, i + 1)
        src = k.qs[i % 2][:, :]
        if i < 4:
            dst = (k.kp if i < 2 else k.vp)[:, i % 2, CH:CH + SEQ]
            b = col("b_kv", i)
        else:
            dst = k.qt[:, (i - 4) // 4, :, ((i - 4) % 4) * CH:((i - 4) % 4 + 1) * CH]
            src = src.rearrange("p (c t) -> p c t", t=CH)
            b = col("b_q", i - 4)
        act.activation(dst, src, ACT.Identity, bias=b).then_inc(k.kqv_done, 1)

    def values_tokens(b):
        act.wait_ge(k.vtok_ready, b + 1)
        act.activation(k.vtok[:, 2 * b:2 * b + 2, :, :],
                       ps[:, 7, :].rearrange("p (w t d) -> p w t d", w=2, t=2), ACT.Copy).then_inc(k.vtok_done, 1)

    def attend(h):
        a = h - 3
        if 0 <= a < 2 * NCH:
            act.wait_ge(k.pt_ready, a + 1)
            if a >= 2:
                act.wait_ge(k.o_ready, a - 1)
            act.activation(k.pts[a % 2][:, :], ps[:, 6, :], ACT.Copy).then_inc(k.pt_done, 1)
        a = h - 4
        if 0 <= a < 2 * NCH:
            kt, c = a // NCH, a % NCH
            act.wait_ge(k.o_ready, a + 1)
            act.activation(k.o_hi[:, kt * 4:kt * 4 + 4, c * CH:(c + 1) * CH],
                           ps[:, 7, 0:256].rearrange("p (t q) -> p t q", t=4), ACT.Copy).then_inc(k.o_hi_done, 1)
        if h < 2 * NCH:
            b, lo_key = h % 3, CH if h % NCH == 0 else 0
            act.wait_ge(k.nmax_done, h + 1)
            if h >= 3:
                act.wait_ge(k.pt_ready, h - 2)
            for u in range(4):
                act.activation(k.pr[b][:, u, lo_key:P],
                               ps[:, score_bank(h) + u // 2, (u % 2) * P + lo_key:(u % 2 + 1) * P], ACT.Exp,
                               bias=k.nmax[b][:, u:u + 1], scale=CH ** -0.5, accum_out=k.psum_[b][:, u:u + 1])
            act.activation(k.esink[b][:, :], k.dsink[b][:, :], ACT.Exp).then_inc(k.exp_done, 1)

    for i in range(8):
        kqv(i)
        if i >= 4:
            values_tokens(i - 4)
    for i in range(8, 12):
        attend(2 * (i - 8))
        kqv(i)
        attend(2 * (i - 8) + 1)
    for h in range(NCH, 2 * NCH + 4):
        attend(h)
    for kk in range(KT - 2):
        hi(O0 + kk + RING, (O0 + kk) % RING)
    act.wait_ge(k.misc, 1)
    boundary(2, "b_post", 0, UP[1], bias=True)
    next_parts(2, "f_pre", KT, k.hs_hi, UP[1])
    ffn(1)
    boundary(3, "f_post", KT, None)


def dve_program(k, dve):
    ps, par = k.ps, k.par
    own = Steps(dve, k.dve_own)

    def col(name, i):
        if isinstance(i, int):
            return par[:, COL[name] + i:COL[name] + i + 1]
        return par[:, ds(i + COL[name], 1)]

    dve.memset(k.eps[:, :], EPS).then_inc(k.eps_set, 1)
    dve.wait_ge(k.par_loaded, 16)
    for c in range(KT):
        dve.wait_ge(k.hi_part_done, c + 1)
        dve.scalar_tensor_tensor(out=k.hs_lo[:, c, :], in0=k.h[:, c, :], scalar=col("a_pre", c), in1=k.hs_hi[:, c, :],
                                 op0=ALU.mult, op1=ALU.subtract).then_inc(k.lo_part_done, 1)
        add_square(k, dve, c, 0)
    dve.wait_ge(k.wdt_hi_done, 1)
    dve.tensor_tensor(k.wdt_lo[:, :], k.wdt[:, :], k.wdt_hi[:, :], ALU.subtract).then_inc(k.wdt_lo_done, 1)
    dve.wait_ge(k.rstd_done, 1)

    def scale_xbc(G, i):
        dve.wait_ge(k.slab_used, G * GROUP_SLABS + (i + 1))
        if not (isinstance(G, int) and G == 0 and i < 2):
            dve.wait_ge(k.conv_done, G * 4 + (i - 1))
        dve.tensor_tensor(k.xbc[i % 2][:, :], ps[:, CONV_BANK[i], :], k.rpre[:, :], ALU.mult).then_inc(k.xbc_scaled, 1)

    def conv(G, i):
        tile = (G + 16, G + 24, G * 2, G * 2 + 1)[i]
        acc = k.cacc[i % 2]
        dve.wait_ge(k.xbc_scaled, G * 4 + (i + 1))
        dve.wait_ge(k.tap0_done, G * 4 + (i + 1))
        for s in (1, 2, 3):
            ins = dve.scalar_tensor_tensor(out=acc[:, s:SEQ], in0=k.xbc[i % 2][:, 0:SEQ - s],
                                           scalar=col("a_conv", (3 - s) * 32 + tile), in1=acc[:, s:SEQ],
                                           op0=ALU.mult, op1=ALU.add)
            if s < 3:
                own.link(ins)
            else:
                ins.then_inc(k.conv_done, 1)

    def scale_z(g, j):
        dve.wait_ge(k.slab_used, g * GROUP_SLABS + (GROUP_SLABS - 1 + j))
        if not isinstance(g, int) or g >= 1:
            dve.wait_ge(k.y_done, g * 2)
        dve.tensor_tensor(k.sz[:, j, :], ps[:, j, :], k.rpre[:, :], ALU.mult).then_inc(k.z_scaled, 1)

    def dt_steps():
        dve.wait_ge(k.dt_ready, 1)
        dve.tensor_tensor(k.dta[:, :], ps[0:NH, 3, :], k.rpre[0:NH, :], ALU.mult).then_inc(k.dt_scaled, 1)
        conv(0, 2)
        dve.wait_ge(k.dt_exp, 1)
        dve.tensor_scalar(k.dtu[:, :], k.dte[:, :], 1.0, None, ALU.add).then_inc(k.dt_u, 1)
        dve.wait_ge(k.dt_u, 1)
        own.link(dve.tensor_scalar(k.dta[:, :], k.dtu[:, :], -1.0, None, ALU.add))
        own.link(dve.tensor_tensor(k.dte[:, :], k.dte[:, :], k.dta[:, :], ALU.subtract))
        scale_xbc(0, 3)
        dve.wait_ge(k.dt_exp, 3)
        own.link(dve.tensor_tensor(k.dte[:, :], k.dte[:, :], k.dtr[:, :], ALU.mult))
        own.link(dve.tensor_tensor(k.dte[:, :], k.dte[:, :], k.dtl[:, :], ALU.add))
        own.link(dve.scalar_tensor_tensor(out=k.dt_[:, :], in0=k.dtx[:, :], scalar=0.0, in1=k.dte[:, :], op0=ALU.max, op1=ALU.add))
        own.link(dve.tensor_scalar(k.dta[:, :], k.dt_[:, :], k.aneg[:, :], -1.0, ALU.mult, ALU.mult))
        for c in range(NC):
            t = slice(c * SC, (c + 1) * SC)
            own.done(dve.tensor_tensor_scan(out=k.cs[:, t], data0=k.ones[0:NH, :], data1=k.dta[:, t], initial=0.0,
                                            op0=ALU.mult, op1=ALU.add))
        own.wait()
        dve.tensor_scalar(k.ncs[:, :], k.cs[:, :], -1.0, None, ALU.mult).then_inc(k.cs_done, 1)
        conv(0, 3)
        dve.wait_ge(k.dt_exp, 7)
        dve.wait_ge(k.cs_done, 1)
        dve.tensor_tensor(k.dtw[:, :], k.dtw[:, :], k.dt_[:, :], ALU.mult).then_inc(k.dtw_done, 1)
        dve.wait_ge(k.tok_ready, 1)
        dve.tensor_copy(k.tok[:, :], ps[:, 4, 0:NC * 96]).then_inc(k.tok_done, 1)
        dve.wait_ge(k.tok_done, 1)
        dve.wait_ge(k.small_loaded, 16 * 6)
        dve.wait_ge(k.cs_stored, 16)

    tokv = k.tok[:, :].rearrange("p (c i h) -> p c i h", c=NC, i=3)

    def group_columns(g):
        if not isinstance(g, int) or g >= 1:
            dve.wait_ge(k.l_done, g * 4)
            dve.wait_ge(k.xtok_done, g * 4)
        src = tokv[:, :, :, ds(g * HG, HG)] if not isinstance(g, int) else tokv[:, :, :, g * HG:(g + 1) * HG]
        dve.tensor_scalar(k.tokg[:, :, :, :], src, 1.0, None, ALU.mult).then_inc(k.tokg_done, 1)
        dve.wait_ge(k.tokg_done, g + 1)

    def segments(g):
        dve.wait_ge(k.cs_loaded, g * 16 + 16)
        dve.wait_ge(k.e_done, g * 3 + 3)
        for hh in range(HG):
            for c in range(NC):
                t = slice(c * SC, (c + 1) * SC)
                last = dve.tensor_scalar(k.csb[:, hh, t], k.csb[:, hh, t], k.tokg[:, c, 1, hh:hh + 1], 0.0, ALU.add, ALU.min)
            last.then_inc(k.seg_done, 1)

    def ssd_1(g):
        dve.wait_ge(k.cb_ready, g + 1)
        if not isinstance(g, int) or g >= 1:
            dve.wait_ge(k.m_done, g * 4)
        dve.tensor_tensor(k.cbm[:, :].rearrange("p (c l) -> p c l", c=NC), ps[:, 3, :].rearrange("p (c l) -> p c l", c=NC),
                          bcast(k.tri[:, :].rearrange("p (o l) -> p o l", o=1), [P, NC, SC]), ALU.mult).then_inc(k.cbm_done, 1)
        if not isinstance(g, int) or g >= 1:
            dve.wait_ge(k.ydiag_ready, g)
        for j in range(2):
            dve.wait_ge(k.xtok_ready, g * 2 + (j + 1))
            for dst, i in ((k.xdt, 0), (k.xdd, 2)):
                w = k.tokg[:, :, i, 2 * j:2 * j + 2].rearrange("p c (h o) -> p c h o", o=1)
                dve.tensor_tensor(dst[:, :, j * P:(j + 1) * P].rearrange("p c (h d) -> p c h d", h=2),
                                  ps[:, 5 + j, :].rearrange("p (c h d) -> p c h d", c=NC, h=2),
                                  bcast(w, [P, NC, 2, 64]), ALU.mult).then_inc(k.xtok_done, 1)

    def ssd_2(g):
        dve.wait_ge(k.cbm_done, g + 1)
        for hh in range(HG):
            dve.wait_ge(k.l_done, g * 4 + (hh + 1))
            dve.tensor_tensor(k.csb[:, hh, :], k.csb[:, hh, :], k.cbm[:, :], ALU.mult).then_inc(k.m_done, 1)

    def ssd_3(g):
        dve.wait_ge(k.state_ready, g + 1)
        dve.wait_ge(k.e_done, g * 3 + 3)
        if not isinstance(g, int) or g >= 1:
            dve.wait_ge(k.yoff_ready, g)
        own.link(dve.tensor_scalar(k.hst[:, 0, :], ps[:, 4, 0:256], 1.0, None, ALU.mult))
        for c in (1, 2):
            w = bcast(k.dec[:, :, c:c + 1], [P, HG, 64])
            own.link(dve.tensor_tensor(k.htmp[:, :].rearrange("p (h d) -> p h d", h=HG),
                                       k.hst[:, c - 1, :].rearrange("p (h d) -> p h d", h=HG), w, ALU.mult))
            src = ps[:, 4, 256:512] if c == 1 else ps[:, 3, 0:256]
            ins = dve.tensor_tensor(k.hst[:, c, :], k.htmp[:, :], src, ALU.add)
            if c == 1:
                own.link(ins)
            else:
                ins.then_inc(k.state_done, 1)

    def ssd_4(g, q):
        dve.wait_ge(k.ydiag_ready, g + 1)
        if not isinstance(g, int) or g >= 1:
            dve.wait_ge(k.y_done, g * 2)
        for j in range(2):
            tile = g * 2 + j
            dcol = k.dskip[:, tile:tile + 1] if isinstance(g, int) else k.dskip[:, ds(tile, 1)]
            own.link(dve.scalar_tensor_tensor(out=k.yt[j][:, :], in0=k.xt[q][:, j, :], scalar=dcol, in1=ps[:, 5 + j, :],
                                              op0=ALU.mult, op1=ALU.add))
            if j == 0:
                dve.wait_ge(k.yoff_ready, g + 1)
            own.link(dve.tensor_tensor(k.yo[:, :], ps[:, (7, 4)[j], SC:SEQ], k.e2[:, j, :], ALU.mult))
            own.link(dve.tensor_tensor(k.yt[j][:, SC:SEQ], k.yt[j][:, SC:SEQ], k.yo[:, :], ALU.add))
            if j == 0:
                dve.wait_ge(k.z_done, g * 2 + 2)
            dve.tensor_tensor(k.yg[:, tile, :], k.yt[j][:, :], k.sz[:, j, :], ALU.mult).then_inc(k.y_done, 1)

    def ssd_5(g):
        dve.wait_ge(k.gsq_done, g * 2 + 2)
        if not isinstance(g, int) or g >= 1:
            dve.wait_ge(k.gate_sums_ready, g)
        dve.tensor_tensor(k.gacc[:, :], k.gsq[0][:, :], k.gsq[1][:, :], ALU.add).then_inc(k.gate_acc_done, 1)

    def norm_y(g):
        dve.wait_ge(k.gate_rstd_done, g + 1)
        for j in range(2):
            tile = g * 2 + j
            dve.scalar_tensor_tensor(out=k.yg[:, tile, :], in0=k.yg[:, tile, :], scalar=col("a_gate", tile),
                                     in1=k.grstd[:, :], op0=ALU.mult, op1=ALU.mult).then_inc(k.yn_scaled, 1)

    def in_group(G, p):
        g, q = G - 1, 1 - p
        end = isinstance(G, int) and G == NG
        scale_z(g, 0)
        if not (isinstance(G, int) and G == 1):
            norm_y(g - 1)
        group_columns(g)
        if end:
            scale_z(g, 1)
            ssd_1(g)
            segments(g)
            ssd_2(g)
            ssd_3(g)
            ssd_4(g, q)
            ssd_5(g)
            return
        if isinstance(G, int):
            scale_z(g, 1)
            ssd_1(g)
            segments(g)
        else:
            segments(g)
            scale_z(g, 1)
            ssd_1(g)
        ssd_2(g)
        scale_xbc(G, 0)
        conv(G, 0)
        ssd_3(g)
        scale_xbc(G, 1)
        conv(G, 1)
        ssd_4(g, q)
        scale_xbc(G, 2)
        ssd_5(g)
        conv(G, 2)
        scale_xbc(G, 3)
        conv(G, 3)

    scale_xbc(0, 0)
    scale_xbc(0, 1)
    conv(0, 0)
    conv(0, 1)
    scale_xbc(0, 2)
    dt_steps()
    in_group(1, 1)
    with looped(dve, 1, NG // 2, (own, 2 * (4 * 2 + 4 + 6))) as i:
        in_group(i * 2, 0)
        in_group(i * 2 + 1, 1)
    in_group(NG, 0)

    norm_y(NG - 1)
    for kk in range(RING, OUT_K):
        low_y(k, dve, kk)

    def post(t):
        for m in range(KT - 1):
            add_square(k, dve, m, 1 + 2 * t)
        dve.wait_ge(k.rstd_done, 2 + 2 * t)

    def update(t, c, between=None):
        if c == 0:
            dve.wait_ge(k.mix_read, KT * (t + 1))
        own.done(dve.tensor_tensor(k.mix[:, c, :], k.mix[:, c, :], k.rpost[:, :], ALU.mult))
        if between:
            between()
        own.wait()
        dve.tensor_tensor(k.h[:, c, :], k.h[:, c, :], k.mix[:, c, :], ALU.add).then_inc(k.h_done, 1)

    def low(t, c, name, off, hi, lo, part):
        dve.wait_ge(k.h_done, KT * t + c + 1)
        dve.wait_ge(k.hi_part_done, part)
        dve.scalar_tensor_tensor(out=lo[:, c, :], in0=k.h[:, c, :], scalar=col(name, off + c), in1=hi[:, c, :],
                                 op0=ALU.mult, op1=ALU.subtract).then_inc(k.lo_part_done, 1)

    def boundary(t, name, off, hi, lo):
        post(t)
        if name is None:
            dve.wait_ge(k.mix_read, KT * (t + 1))
            for c in range(LAST_DVE + 1):
                if c < LAST_DVE:
                    own.done(dve.tensor_tensor(k.mix[:, c, :], k.mix[:, c, :], k.rpost[:, :], ALU.mult))
                if c:
                    own.wait()
                    dve.tensor_tensor(k.h[:, c - 1, :], k.h[:, c - 1, :], k.mix[:, c - 1, :], ALU.add).then_inc(k.h_done, 1)
            return
        update(t, 0)
        for c in range(KT):
            low_c = lambda c=c: low(t, c, name, off, hi, lo, k.lo_base[t] + (2 * c + 1 if t == 1 else c + 1))
            if c == 0:
                update(t, 1, low_c)
                continue
            if c + 1 < KT:
                update(t, c + 1)
            low_c()

    def ffn(l):
        u0, d0, i0 = UP[l], DOWN[l], l * FT
        dve.wait_ge(k.rstd_done, k.pre_count[l])

        def pair(p, q):
            for v in range(2):
                u, cv = k.u[q][v], k.cv[q][v]
                dve.wait_ge(k.slab_used, p * 2 + (u0 + v + 1))
                if not (isinstance(p, int) and i0 + p < 2) and v == 0:
                    dve.wait_ge(k.f_prod_done, p + (i0 - 1))
                dve.tensor_tensor(u[:, :], ps[:, (u0 + 2 * q + v) % 4, :], k.rpre[:, :], ALU.mult).then_inc(k.u_done, 1)
                dve.wait_ge(k.u_done, p * 2 + (2 * i0 + v + 1))
                dve.wait_ge(k.ftap0_done, p * 2 + (2 * i0 + v + 1))
                for s in (1, 2):
                    w = col("f_conv", p + (v * FT + (l * 3 + 2 - s) * 2 * FT))
                    ins = dve.scalar_tensor_tensor(out=cv[:, s:SEQ], in0=u[:, 0:SEQ - s], scalar=w, in1=cv[:, s:SEQ],
                                                   op0=ALU.mult, op1=ALU.add)
                    if s == 1:
                        own.link(ins)
                    else:
                        ins.then_inc(k.fconv_done, 1)
            dve.wait_ge(k.fconv_done, p * 2 + (2 * i0 + 2))
            dve.wait_ge(k.fsilu_done, p + (i0 + 1))
            dve.tensor_tensor(k.f[:, p, :], k.cv[q][0][:, :], k.cv[q][1][:, :], ALU.mult).then_inc(k.f_prod_done, 1)

        def f_part(kk, j):
            s = (d0 + j) % RING
            dve.wait_ge(k.f_hi_done, kk + (i0 + 1))
            dve.tensor_tensor(k.f_lo[s][:, :], k.f[:, kk, :], k.f_hi[s][:, :], ALU.subtract).then_inc(k.f_lo_done, 1)

        pair(0, 0)
        pair(1, 1)
        f_part(0, 0)
        f_part(1, 1)
        with looped(dve, 1, FT // 2, (own, 4)) as r:
            pair(r * 2, 0)
            pair(r * 2 + 1, 1)
        f_part(2, 2)
        f_part(3, 3)
        with dve.Fori(1, 5) as r:
            for j in range(RING):
                f_part(r * RING + j, j)
        for kk in (FT - 2, FT - 1):
            f_part(kk, kk)

    boundary(0, "f_pre", 0, k.hs_hi, k.hs_lo)
    ffn(0)
    dve.tensor_tensor(k.bo_post[:, :], par[:, COL["b_o"]:COL["b_o"] + KT], par[:, COL["b_post"]:COL["b_post"] + KT], ALU.mult).then_inc(k.misc, 1)
    dve.wait_ge(k.small_loaded, 16 * 6)
    dve.tensor_scalar(k.nsink[:, :], k.nsink[:, :], -1.0, None, ALU.mult).then_inc(k.misc, 1)
    boundary(1, "kvn", 0, k.hk_hi, k.hk_lo)
    for c in range(KT):
        low(1, c, "b_pre", 0, k.hs_hi, k.hs_lo, k.lo_base[1] + 2 * c + 2)
    dve.memset(k.kp[:, :, 0:CH], 0.0).then_inc(k.pads_set, 1)
    dve.memset(k.vp[:, :, 0:CH], 0.0).then_inc(k.pads_set, 1)
    dve.memset(k.pr[0][:, :, 0:CH], 0.0).then_inc(k.pads_set, 1)
    dve.wait_ge(k.rstd_done, 5)

    def scaled(i):
        bank = (KV0 + i) % 4 if i < 4 else k.q_bank[i - 4]
        dve.wait_ge(k.slab_used, KV0 + i + 1)
        if i >= 2:
            dve.wait_ge(k.kqv_done, i - 1)
        dve.tensor_tensor(k.qs[i % 2][:, :], ps[:, bank, :], k.rpre[:, :], ALU.mult).then_inc(k.qkv_read, 1)

    def row_max(a):
        kt, c = a // NCH, a % NCH
        lo_key = CH if c == 0 else 0
        b = a % 3
        dve.wait_ge(k.scores_ready, a + 1)
        if a >= 3:
            dve.wait_ge(k.exp_done, a - 2)
        src = ps[:, score_bank(a):score_bank(a) + 2, 0:2 * P].rearrange("p g (u t) -> p g u t", u=2)[:, :, :, lo_key:P]
        own.link(dve.tensor_reduce(out=k.rmax[b][:, :].rearrange("p (g u) -> p g u", g=2), in_=src,
                                   axis=AX_X, op=ALU.max))
        sink = k.nsink[:, kt * 4:kt * 4 + 4]
        own.link(dve.scalar_tensor_tensor(out=k.nmax[b][:, :], in0=k.rmax[b][:, :], scalar=-(CH ** -0.5), in1=sink,
                                          op0=ALU.mult, op1=ALU.min))
        dve.tensor_tensor(k.dsink[b][:, :], k.nmax[b][:, :], sink, ALU.subtract).then_inc(k.nmax_done, 1)

    def low_o(a):
        kt, c = a // NCH, a % NCH
        dve.wait_ge(k.o_hi_done, a + 1)
        dst = slice(c * CH, (c + 1) * CH)
        dve.tensor_tensor(k.o_lo[:, kt * 4:kt * 4 + 4, dst], ps[:, 7, 0:256].rearrange("p (t q) -> p t q", t=4),
                          k.o_hi[:, kt * 4:kt * 4 + 4, dst], ALU.subtract).then_inc(k.o_done, 1)

    def normalise(a):
        b = a % 3
        dve.wait_ge(k.exp_done, a + 1)
        own.link(dve.tensor_tensor(k.den[:, :], k.psum_[b][:, :], k.esink[b][:, :], ALU.add))
        if a:
            dve.wait_ge(k.probs_done, a)
        own.link(dve.reciprocal(k.rden[:, :], k.den[:, :]))
        w = bcast(k.rden[:, :].rearrange("p (u o) -> p u o", o=1), [P, 4, P])
        if a % NCH == 0:
            if a:
                dve.wait_ge(k.pt_ready, a - 2)
                dve.memset(k.pr[b][:, :, 0:CH], 0.0).then_inc(k.pads_set, 1)
            dve.wait_ge(k.pads_set, 3 + a // NCH)
        dve.tensor_tensor(k.pr[b][:, :, :], k.pr[b][:, :, :], w, ALU.mult).then_inc(k.probs_done, 1)

    def attend(h):
        if h < 2 * NCH:
            row_max(h)
        if 0 <= h - 1 < 2 * NCH:
            normalise(h - 1)
        if 0 <= h - 4 < 2 * NCH:
            low_o(h - 4)

    for i in range(8):
        scaled(i)
    dve.wait_ge(k.misc, 2)
    for i in range(8, 12):
        attend(2 * (i - 8))
        scaled(i)
        attend(2 * (i - 8) + 1)
    for h in range(NCH, 2 * NCH + 4):
        attend(h)
    boundary(2, "f_pre", KT, k.hs_hi, k.hs_lo)
    ffn(1)
    boundary(3, None, 0, None, None)


def trunk(nc, d_x, d_slabs, d_wdt, d_par, d_hpar, d_dskip, d_sinks, d_out):
    k = Core()
    k.d_x, k.d_slabs, k.d_wdt, k.d_par, k.d_hpar, k.d_dskip, k.d_sinks, k.d_out = (
        d_x, d_slabs, d_wdt, d_par, d_hpar, d_dskip, d_sinks, d_out)
    k.d_cs = nc.dram_tensor("cs_scratch", (NH, SEQ), F32, kind="Internal").ap()
    with ExitStack() as ctx:
        def sb(stack, name, shape, dt=F32):
            return stack.enter_context(nc.sbuf_tensor(name, shape, dt))

        keep = ctx
        k.h = sb(keep, "h", [P, KT, SEQ])
        k.hs_hi, k.hs_lo = (sb(keep, f"hs_{x}", [P, KT, SEQ], F32R) for x in ("hi", "lo"))
        k.raw = [sb(keep, f"raw{s}", [P, DM]) for s in range(RING)]
        k.whi = [sb(keep, f"whi{s}", [P, DM], F32R) for s in range(RING)]
        k.wlo = [sb(keep, f"wlo{s}", [P, DM], F32R) for s in range(RING)]
        k.par = sb(keep, "par", [P, N_COLS])
        k.hpar = sb(keep, "hpar", [NH, 2])
        k.dskip = sb(keep, "dskip", [P, OUT_K])
        k.nsink = sb(keep, "nsink", [P, 8])
        k.ones, k.ident, k.tri = (sb(keep, x, [P, P]) for x in ("ones", "ident", "tri"))
        k.eps = sb(keep, "eps", [P, 1])
        k.bo_post = sb(keep, "bo_post", [P, KT])
        k.rpre, k.rpost, k.acc = (sb(keep, x, [P, SEQ]) for x in ("rpre", "rpost", "acc"))
        k.sq = [sb(keep, f"sq{i}", [P, SEQ]) for i in range(2)]

        with ExitStack() as st:
            k.yg = sb(st, "yg", [P, OUT_K, SEQ])
            with ExitStack() as s2:
                def pair_of(name, shape):
                    return [sb(s2, f"{name}{i}", shape) for i in range(2)]

                xt0, bt0, ct0 = sb(s2, "xt0", [P, 2, SEQ]), sb(s2, "bt0", [P, SEQ]), sb(s2, "ct0", [P, SEQ])
                k.cacc, k.xbc = pair_of("cacc", [P, SEQ]), pair_of("xbc", [P, SEQ])
                k.xt, k.bt, k.ct = [xt0, sb(s2, "xt1", [P, 2, SEQ])], [bt0, sb(s2, "bt1", [P, SEQ])], [ct0, sb(s2, "ct1", [P, SEQ])]
                with ExitStack() as s4:
                    k.wdt = sb(s4, "wdt", [P, KT * NH])
                    k.wdt_hi, k.wdt_lo = (sb(s4, x, [P, KT * NH], F32R) for x in ("wdt_hi", "wdt_lo"))
                k.sz = sb(s2, "sz", [P, 2, SEQ])
                k.csb = sb(s2, "csb", [P, HG, SEQ])
                k.btok = sb(s2, "btok", [P, NC, P])
                k.xdt, k.xdd = (sb(s2, x, [P, NC, 256]) for x in ("xdt", "xdd"))
                k.cbm = sb(s2, "cbm", [P, SEQ])
                k.hst = sb(s2, "hst", [P, 3, 256])
                k.htmp = sb(s2, "htmp", [P, 256])
                k.dec = sb(s2, "dec", [P, HG, NC])
                k.e2 = sb(s2, "e2", [P, 2, SEQ - SC])
                k.tok = sb(s2, "tok", [P, NC * 96])
                k.tokg = sb(s2, "tokg", [P, NC, 3, HG])
                k.yt = pair_of("yt", [P, SEQ])
                k.yo = sb(s2, "yo", [P, SEQ - SC])
                k.grstd = sb(s2, "grstd", [P, SEQ])
            k.dtx, k.dta = k.yt[0][0:NH, :], k.yt[1][0:NH, :]
            with ExitStack() as s3:
                k.yn_hi = [sb(s3, f"yn_hi{i}", [P, SEQ], F32R) for i in range(RING)]
                k.yn_lo = [sb(s3, f"yn_lo{i}", [P, SEQ], F32R) for i in range(RING)]
        k.dte, k.dtu = k.rpost[0:NH, :], k.acc[0:NH, :]
        k.dtl, k.dtr = k.grstd[0:NH, :], k.sq[0][0:NH, :]
        k.dt_, k.ncs = k.xdt[0:NH, 0:2, :].rearrange("p c t -> p (c t)"), k.xdt[0:NH, 2:4, :].rearrange("p c t -> p (c t)")
        k.dtw, k.cs = k.xdd[0:NH, 0:2, :].rearrange("p c t -> p (c t)"), k.xdd[0:NH, 2:4, :].rearrange("p c t -> p (c t)")
        k.gsq = k.sq
        k.gacc = k.acc
        k.aneg = k.dec[0:NH, 0, 0:1]

        with ExitStack() as st:
            k.f = sb(st, "f", [P, FT, SEQ])
            k.f_hi = [sb(st, f"f_hi{i}", [P, SEQ], F32R) for i in range(RING)]
            k.f_lo = [sb(st, f"f_lo{i}", [P, SEQ], F32R) for i in range(RING)]
        with ExitStack() as st:
            k.hk_hi, k.hk_lo = (sb(st, f"hk_{x}", [P, KT, SEQ], F32R) for x in ("hi", "lo"))
            k.o_hi, k.o_lo = k.hk_hi, k.hk_lo
            k.qt = sb(st, "qt", [P, 2, NCH, 4 * CH])
            k.kp, k.vp = (sb(st, x, [P, 2, CH + SEQ]) for x in ("kp", "vp"))
            k.vtok = sb(st, "vtok", [P, NCH, 2, P])
            k.pr = [sb(st, f"pr{i}", [P, 4, P]) for i in range(3)]
            k.pts = [sb(st, f"pts{i}", [P, 4 * P]) for i in range(2)]
            k.qs = [sb(st, f"qs{i}", [P, SEQ]) for i in range(2)]
            k.rmax, k.nmax, k.dsink, k.esink, k.psum_ = (
                [sb(st, f"{name}{i}", [P, 4]) for i in range(3)] for name in ("rmax", "nmax", "dsink", "esink", "psum"))
            k.den, k.rden = (sb(st, x, [P, 4]) for x in ("den", "rden"))
            k.mix = sb(st, "mix", [P, KT, SEQ])
            k.u = [[k.mix[:, 4 * b + v, :] for v in range(2)] for b in range(2)]
            k.cv = [[k.mix[:, 4 * b + 2 + v, :] for v in range(2)] for b in range(2)]

        k.ps = ctx.enter_context(nc.psum_tensor("ps", [P, 8, SEQ], F32))

        def sems(*names):
            return [ctx.enter_context(nc.semaphore(name)) for name in names]

        k.par_loaded, k.small_loaded, k.stored, k.ones_set, k.consts_ready, k.eps_set, k.pads_set, k.misc = sems(
            "par_loaded", "small_loaded", "stored", "ones_set", "consts_ready", "eps_set", "pads_set", "misc")
        k.hi_done, k.lo_done, k.slab_used = sems(
            "hi_done", "lo_done", "slab_used")
        k.sq_done, k.sq_added, k.sums_ready, k.ln_done, k.rstd_done, k.hi_part_done, k.lo_part_done = sems(
            "sq_done", "sq_added", "sums_ready", "ln_done", "rstd_done", "hi_part_done", "lo_part_done")
        k.mix_ready, k.mix_read, k.h_done, k.last_scaled, k.h_last_done = sems(
            "mix_ready", "mix_read", "h_done", "last_scaled", "h_last_done")
        k.wdt_hi_done, k.wdt_lo_done, k.dt_scaled, k.xbc_scaled, k.z_scaled = sems(
            "wdt_hi_done", "wdt_lo_done", "dt_scaled", "xbc_scaled", "z_scaled")
        k.dt_ready, k.dt_exp, k.dt_u, k.cs_done, k.dtw_done, k.tok_ready, k.tok_done, k.cs_stored, k.cs_loaded = sems(
            "dt_ready", "dt_exp", "dt_u", "cs_done", "dtw_done", "tok_ready", "tok_done", "cs_stored", "cs_loaded")
        k.tap0_done, k.conv_done, k.xbc_done, k.z_done, k.tokg_done, k.e_done, k.seg_done, k.l_done, k.cb_ready, k.cbm_done = sems(
            "tap0_done", "conv_done", "xbc_done", "z_done", "tokg_done", "e_done", "seg_done", "l_done", "cb_ready", "cbm_done")
        k.btok_ready, k.btok_done, k.xtok_ready, k.xtok_done, k.m_done, k.state_ready, k.state_done, k.ydiag_ready = sems(
            "btok_ready", "btok_done", "xtok_ready", "xtok_done", "m_done", "state_ready", "state_done", "ydiag_ready")
        k.yoff_ready, k.y_done, k.gsq_done, k.gate_acc_done, k.gate_sums_ready, k.gln_done, k.gate_rstd_done = sems(
            "yoff_ready", "y_done", "gsq_done", "gate_acc_done", "gate_sums_ready", "gln_done", "gate_rstd_done")
        k.yn_scaled, k.yn_hi_done, k.yn_done = sems(
            "yn_scaled", "yn_hi_done", "yn_done")
        k.u_done, k.ftap0_done, k.fconv_done, k.fsilu_done, k.f_prod_done, k.f_hi_done, k.f_lo_done = sems(
            "u_done", "ftap0_done", "fconv_done", "fsilu_done", "f_prod_done", "f_hi_done", "f_lo_done")
        k.qkv_read, k.kqv_done, k.vtok_ready, k.vtok_done, k.scores_ready, k.nmax_done, k.exp_done, k.probs_done = sems(
            "qkv_read", "kqv_done", "vtok_ready", "vtok_done", "scores_ready", "nmax_done", "exp_done", "probs_done")
        k.pt_ready, k.pt_done, k.o_ready, k.o_hi_done, k.o_done = sems(
            "pt_ready", "pt_done", "o_ready", "o_hi_done", "o_done")
        k.act_own, k.dve_own = sems(
            "act_own", "dve_own")
        k.raw_loaded = [ctx.enter_context(nc.semaphore(f"raw_loaded{s}")) for s in range(RING)]
        k.x_loaded = [ctx.enter_context(nc.semaphore(f"x_loaded{c}")) for c in range(KT)]
        k.lo_base = {0: KT, 1: 2 * KT, 2: 4 * KT}
        k.lo_q_base = 3 * KT
        k.pre_count = [3, 7]
        k.q_bank = [2, 3, 0, 1, 0, 1, 0, 1]

        block = ctx.enter_context(nc.Block())

        @block.sync
        def _(sp):
            sp_program(k, sp)

        @block.gpsimd
        def _(pool):
            pool_program(k, pool)

        @block.tensor
        def _(pe):
            pe_program(k, pe)

        @block.scalar
        def _(act):
            act_program(k, act)

        @block.vector
        def _(dve):
            dve_program(k, dve)


def kernel(**inputs):
    import concourse.bacc as bacc
    from concourse.bass_utils import run_bass_kernel_spmd

    a = {n: np.asarray(v) for n, v in inputs.items()}

    def tiles(v):
        return v.reshape(-1, P).T

    def slabs_a(w):
        return w.reshape(KT, P, -1, P).transpose(2, 1, 0, 3).reshape(-1, P, DM)

    w_in = a["a_in_proj"][0]
    w_in_tiles = slabs_a(w_in[:, :NG * GROUP_SLABS * P])
    xbc = DI // P
    tiles_of = [(xbc + 16 + g, xbc + 24 + g, xbc + 2 * g, xbc + 2 * g + 1, 2 * g, 2 * g + 1) for g in range(NG)]
    order = [t for group in tiles_of for t in group]
    def by_kv(v, axis):
        v = np.moveaxis(v, axis, 0)
        v = v.reshape(2, 2, 4, 64, *v.shape[1:]).swapaxes(1, 2).reshape(v.shape)
        return np.moveaxis(v, 0, axis)

    slabs = np.concatenate([
        w_in_tiles[order], a["a_out_proj"][0].reshape(-1, P, DM),
        slabs_a(a["f_up"][0]).reshape(2, FT, P, DM).swapaxes(0, 1).reshape(-1, P, DM), a["f_down"][0].reshape(-1, P, DM),
        slabs_a(a["w_kv"]), slabs_a(by_kv(a["w_q"][0], 1)), by_kv(a["w_o"][0], 0).reshape(-1, P, DM),
        slabs_a(a["f_up"][1]).reshape(2, FT, P, DM).swapaxes(0, 1).reshape(-1, P, DM), a["f_down"][1].reshape(-1, P, DM),
    ])
    params = {
        "a_pre": a["a_norm_pre"], "a_conv": a["a_conv_w"], "a_convb": a["a_conv_b"], "a_gate": a["a_gate_norm"],
        "a_post": a["a_norm_post"], "kvn": a["kv_norm"], "b_kv": a["b_kv"], "b_pre": a["b_norm_pre"],
        "b_q": by_kv(a["b_q"][0], 0), "b_o": a["b_o"], "b_post": a["b_norm_post"], "f_pre": a["f_norm_pre"],
        "f_conv": a["f_conv_w"], "f_convb": a["f_conv_b"], "f_post": a["f_norm_post"],
    }
    arrays = {
        "x": a["x"][0].T.reshape(KT, P, SEQ).transpose(1, 0, 2),
        "slabs": slabs.reshape(N_SLABS * P, DM),
        "wdt": w_in[:, NG * GROUP_SLABS * P:].reshape(KT, P, NH).transpose(1, 0, 2).reshape(P, KT * NH),
        "par": np.concatenate([tiles(params[n]) for n in COL], axis=1),
        "hpar": np.stack([a["a_dt_bias"][0], a["a_a_log"][0]], axis=1),
        "dskip": a["a_d_skip"][0].reshape(OUT_K, 2).T,
        "sinks": a["sinks"][0].reshape(8, 2).T,
    }
    arrays = {n: np.ascontiguousarray(v) for n, v in arrays.items()}
    nc = bacc.Bacc("TRN2", target_bir_lowering=False, num_devices=1)
    args = [nc.dram_tensor(f"in_{n}", v.shape, F32, kind="ExternalInput").ap() for n, v in arrays.items()]
    out = nc.dram_tensor("out", (P, KT, SEQ), F32, kind="ExternalOutput").ap()
    trunk(nc, *args, out)
    r = run_bass_kernel_spmd(nc, [{f"in_{n}": v for n, v in arrays.items()}], core_ids=[0])
    got = np.asarray(r.results[0]["out"])
    return got.transpose(1, 0, 2).reshape(DM, SEQ).T[None].copy()
```
